# Optimizing a Trainium2 kernel written in Bass

```python
import math, functools
import jax, jax.numpy as jnp
from jax import lax
import numpy as np

D_MODEL = 1024
BATCH = 1
SEQ = 512
DEPTH = 2
DEC_BATCH = 8
DEC_SEQ = 8
PAST_LEN = 4096
PAGE_SIZE = 128

N_MIXERS = 2
N_A_LAYERS = (DEPTH + 1) // 2
N_B_LAYERS = DEPTH // 2
HEAD_SIZE = 64
RWKV_HEADS = D_MODEL // HEAD_SIZE
DECAY_LORA = 64
AAA_LORA = 64
GATE_LORA = 128
GN_EPS = 6.4e-4
CONV_WIDTH = 31
LN_EPS = 1e-5
N_KEYS = 128
N_EXPERTS = N_KEYS * N_KEYS
PEER_HEADS = 8
PEER_TOPK = 16
PEER_DQ = 256
PEER_DK_HALF = PEER_DQ // 2
PEER_BLOCK = 128
RMS_EPS = 1e-6

kernel_name = "rwkv7_conformerconv_peer_hybrid_step"

def rmsnorm(x, g):
    xf = x.astype(jnp.float32)
    y = xf * lax.rsqrt(jnp.mean(xf * xf, axis=-1, keepdims=True) + RMS_EPS)
    return (y * g).astype(x.dtype)

def rwkv_mix(x, shift_prev, s0, mu, w_rkv, w0, w1, w2, a0, a1, a2, g1, g2, k_k, k_a, r_k, ln_w, ln_b, w_o):
    f32 = jnp.float32
    B, T, D = x.shape
    H, N = RWKV_HEADS, HEAD_SIZE
    xprev = jnp.concatenate([shift_prev[:, None, :].astype(x.dtype), x[:, :-1]], axis=1)
    xx = xprev - x
    xm = x[None] + xx[None] * mu[:, None, None, :]
    r, k, v = jnp.einsum('ibtd,ide->ibte', xm[:3], w_rkv)
    xw, xa, xg = xm[3], xm[4], xm[5]
    w = -jax.nn.softplus(-(w0 + jnp.tanh(xw @ w1) @ w2).astype(f32)) - 0.5
    decay = jnp.exp(-jnp.exp(w))
    a = jax.nn.sigmoid((a0 + (xa @ a1) @ a2).astype(f32))
    g = jax.nn.sigmoid(xg @ g1) @ g2
    heads = lambda t: t.reshape(B, T, H, N)
    kk = heads((k * k_k).astype(f32))
    kk = kk / jnp.maximum(jnp.sqrt(jnp.sum(kk * kk, axis=-1, keepdims=True)), 1e-12)
    kf = heads(k.astype(f32) * (1.0 + (a - 1.0) * k_a.astype(f32)))
    rf, vf = heads(r.astype(f32)), heads(v.astype(f32))
    af, wf = heads(a), heads(decay)
    xs = tuple(jnp.moveaxis(t, 1, 0) for t in (rf, wf, kf, vf, kk, af))

    def step(S, inp):
        r_t, w_t, k_t, v_t, kk_t, a_t = inp
        sa = jnp.einsum('bhij,bhj->bhi', S, -kk_t)
        S = (S * w_t[:, :, None, :] + sa[..., None] * (kk_t * a_t)[:, :, None, :]
             + v_t[..., None] * k_t[:, :, None, :])
        return S, jnp.einsum('bhij,bhj->bhi', S, r_t)

    s_fin, y = lax.scan(step, s0.astype(f32), xs)
    y = jnp.moveaxis(y, 0, 1)
    mean = jnp.mean(y, axis=-1, keepdims=True)
    var = jnp.mean(jnp.square(y - mean), axis=-1, keepdims=True)
    yn = ((y - mean) * lax.rsqrt(var + GN_EPS)).reshape(B, T, D) * ln_w + ln_b
    bonus = jnp.sum(rf * kf * r_k.astype(f32), axis=-1, keepdims=True) * vf
    y = yn + bonus.reshape(B, T, D)
    out = (y.astype(x.dtype) * g) @ w_o
    return out, x[:, -1], s_fin

def conv_mix(x, buf, w_pw1, b_pw1, w_dw, b_dw, ln_g, ln_b, w_pw2, b_pw2):
    D = x.shape[-1]
    h = x @ w_pw1 + b_pw1
    u = h[..., :D] * jax.nn.sigmoid(h[..., D:])
    full = jnp.concatenate([buf.astype(u.dtype), u], axis=1)
    c = lax.conv_general_dilated(full, w_dw[:, None, :].astype(full.dtype), window_strides=(1,),
                                 padding='VALID', dimension_numbers=('NWC', 'WIO', 'NWC'),
                                 feature_group_count=D) + b_dw
    cf = c.astype(jnp.float32)
    mean = jnp.mean(cf, axis=-1, keepdims=True)
    var = jnp.mean(jnp.square(cf - mean), axis=-1, keepdims=True)
    cn = ((cf - mean) * lax.rsqrt(var + LN_EPS) * ln_g + ln_b).astype(x.dtype)
    out = jax.nn.silu(cn) @ w_pw2 + b_pw2
    return out, full[:, -(CONV_WIDTH - 1):]

def peer(x, w_q, sub_keys, u_tab, v_tab):
    B, T, D = x.shape
    n = B * T
    nb = -(-n // PEER_BLOCK)
    pad = nb * PEER_BLOCK - n
    xb_all = jnp.pad(x.reshape(n, D), ((0, pad), (0, 0))).reshape(nb, PEER_BLOCK, D)
    K = PEER_TOPK

    def block(xb):
        q = (xb @ w_q).reshape(PEER_BLOCK, PEER_HEADS, 2, PEER_DK_HALF)
        s = jnp.einsum('bhpc,hpnc->bhpn', q, sub_keys).astype(jnp.float32)
        ts, ti = lax.top_k(s, K)
        cand_s = (ts[:, :, 0, :, None] + ts[:, :, 1, None, :]).reshape(PEER_BLOCK, PEER_HEADS, K * K)
        cand_i = (ti[:, :, 0, :, None] * N_KEYS + ti[:, :, 1, None, :]).reshape(PEER_BLOCK, PEER_HEADS, K * K)
        best_s, pos = lax.top_k(cand_s, K)
        idx = jnp.take_along_axis(cand_i, pos, axis=-1)
        gate = jax.nn.softmax(best_s, axis=-1)
        act = jax.nn.gelu(jnp.einsum('bhkd,bd->bhk', u_tab[idx], xb).astype(jnp.float32), approximate=False)
        return jnp.einsum('bhk,bhkd->bd', (gate * act).astype(xb.dtype), v_tab[idx])

    out = lax.map(block, xb_all).reshape(nb * PEER_BLOCK, D)[:n]
    return out.reshape(B, T, D)

def trunk(x, wkv0, shift0, conv0, rw, cv, norm_mix, norm_ffn, peer_w_q, peer_sub_keys, peer_u, peer_v, norm_final):
    new_wkv, new_shift, new_conv = [], [], []
    for i in range(DEPTH):
        j = i // N_MIXERS
        h = rmsnorm(x, norm_mix[i])
        if i % N_MIXERS == 0:
            out, sh, s_fin = rwkv_mix(h, shift0[j], wkv0[j], *(p[j] for p in rw))
            new_wkv.append(s_fin)
            new_shift.append(sh)
        else:
            out, buf = conv_mix(h, conv0[j], *(p[j] for p in cv))
            new_conv.append(buf)
        x = x + out
        x = x + peer(rmsnorm(x, norm_ffn[i]), peer_w_q[i], peer_sub_keys[i], peer_u[i], peer_v[i])
    return rmsnorm(x, norm_final), jnp.stack(new_wkv), jnp.stack(new_shift), jnp.stack(new_conv)

def setup_inputs(seed: int = 0) -> dict:
    key = jax.random.key(seed)
    ks = iter(jax.random.split(key, 64))
    f32 = jnp.float32
    nrm = lambda shape, scale: jax.random.normal(next(ks), shape, f32) * scale
    D, A, Bn = D_MODEL, N_A_LAYERS, N_B_LAYERS
    H, N = RWKV_HEADS, HEAD_SIZE
    return {
        "x_prompt": nrm((BATCH, SEQ, D), 1.0),
        "x_sample": nrm((DEC_BATCH, DEC_SEQ, D), 1.0),
        "state_wkv": nrm((A, DEC_BATCH, H, N, N), 0.5),
        "state_shift": nrm((A, DEC_BATCH, D), 1.0),
        "state_conv": nrm((Bn, DEC_BATCH, CONV_WIDTH - 1, D), 0.5),
        "rwkv_mu": jax.random.uniform(next(ks), (A, 6, D), f32),
        "rwkv_w_rkv": nrm((A, 3, D, D), D ** -0.5),
        "rwkv_w0": nrm((A, D), 0.5) - 1.0,
        "rwkv_w1": nrm((A, D, DECAY_LORA), D ** -0.5),
        "rwkv_w2": nrm((A, DECAY_LORA, D), 0.5 * DECAY_LORA ** -0.5),
        "rwkv_a0": nrm((A, D), 0.1),
        "rwkv_a1": nrm((A, D, AAA_LORA), D ** -0.5),
        "rwkv_a2": nrm((A, AAA_LORA, D), 0.5 * AAA_LORA ** -0.5),
        "rwkv_g1": nrm((A, D, GATE_LORA), D ** -0.5),
        "rwkv_g2": nrm((A, GATE_LORA, D), GATE_LORA ** -0.5),
        "rwkv_k_k": 0.85 + nrm((A, D), 0.05),
        "rwkv_k_a": 1.0 + nrm((A, D), 0.05),
        "rwkv_r_k": nrm((A, H, N), 0.1),
        "rwkv_ln_w": 1.0 + nrm((A, D), 0.05),
        "rwkv_ln_b": nrm((A, D), 0.01),
        "rwkv_w_o": nrm((A, D, D), D ** -0.5),
        "conv_w_pw1": nrm((Bn, D, 2 * D), D ** -0.5),
        "conv_b_pw1": nrm((Bn, 2 * D), 0.01),
        "conv_w_dw": nrm((Bn, CONV_WIDTH, D), CONV_WIDTH ** -0.5),
        "conv_b_dw": nrm((Bn, D), 0.01),
        "conv_ln_g": 1.0 + nrm((Bn, D), 0.05),
        "conv_ln_b": nrm((Bn, D), 0.01),
        "conv_w_pw2": nrm((Bn, D, D), D ** -0.5),
        "conv_b_pw2": nrm((Bn, D), 0.01),
        "norm_mix": 1.0 + nrm((DEPTH, D), 0.05),
        "norm_ffn": 1.0 + nrm((DEPTH, D), 0.05),
        "peer_w_q": nrm((DEPTH, D, PEER_HEADS * PEER_DQ), D ** -0.5),
        "peer_sub_keys": nrm((DEPTH, PEER_HEADS, 2, N_KEYS, PEER_DK_HALF), PEER_DK_HALF ** -0.5),
        "peer_u": nrm((DEPTH, N_EXPERTS, D), D ** -0.5),
        "peer_v": nrm((DEPTH, N_EXPERTS, D), PEER_HEADS ** -0.5),
        "norm_final": 1.0 + nrm((D,), 0.05),
    }

def reference(x_prompt, x_sample, state_wkv, state_shift, state_conv,
              rwkv_mu, rwkv_w_rkv, rwkv_w0, rwkv_w1, rwkv_w2, rwkv_a0, rwkv_a1, rwkv_a2,
              rwkv_g1, rwkv_g2, rwkv_k_k, rwkv_k_a, rwkv_r_k, rwkv_ln_w, rwkv_ln_b, rwkv_w_o,
              conv_w_pw1, conv_b_pw1, conv_w_dw, conv_b_dw, conv_ln_g, conv_ln_b, conv_w_pw2, conv_b_pw2,
              norm_mix, norm_ffn, peer_w_q, peer_sub_keys, peer_u, peer_v, norm_final):
    rw = (rwkv_mu, rwkv_w_rkv, rwkv_w0, rwkv_w1, rwkv_w2, rwkv_a0, rwkv_a1, rwkv_a2,
          rwkv_g1, rwkv_g2, rwkv_k_k, rwkv_k_a, rwkv_r_k, rwkv_ln_w, rwkv_ln_b, rwkv_w_o)
    cv = (conv_w_pw1, conv_b_pw1, conv_w_dw, conv_b_dw, conv_ln_g, conv_ln_b, conv_w_pw2, conv_b_pw2)
    shared = (norm_mix, norm_ffn, peer_w_q, peer_sub_keys, peer_u, peer_v, norm_final)
    bp = x_prompt.shape[0]
    wkv_p0 = jnp.zeros((N_A_LAYERS, bp, RWKV_HEADS, HEAD_SIZE, HEAD_SIZE), jnp.float32)
    shift_p0 = jnp.zeros((N_A_LAYERS, bp, D_MODEL), x_prompt.dtype)
    conv_p0 = jnp.zeros((N_B_LAYERS, bp, CONV_WIDTH - 1, D_MODEL), x_prompt.dtype)
    y_prompt, wkv_p, shift_p, conv_p = trunk(x_prompt, wkv_p0, shift_p0, conv_p0, rw, cv, *shared)
    y_sample, wkv_s, shift_s, conv_s = trunk(x_sample, state_wkv, state_shift, state_conv, rw, cv, *shared)
    return (y_prompt, y_sample, wkv_p, shift_p, conv_p, wkv_s, shift_s, conv_s)


_drawn_inputs = setup_inputs


def setup_inputs(seed=0):
    import zlib

    import numpy as np

    out = dict(_drawn_inputs(seed))
    spreads = {}
    factors = {'rwkv_ln_b': 2.774,
     'conv_b_pw1': 4.516,
     'conv_b_dw': 3.308,
     'conv_ln_b': 4.989,
     'conv_b_pw2': 3.636}
    for name, (base, spread) in spreads.items():
        noise = np.random.default_rng([zlib.crc32(name.encode()), seed]).standard_normal(out[name].shape)
        drawn = base * np.exp(spread * noise) if base else spread * noise
        out[name] = __import__('jax').numpy.asarray(drawn.astype(out[name].dtype))
    for name, factor in factors.items():
        out[name] = (out[name] * factor).astype(out[name].dtype)
    return out
```

```python
import concourse.bass as bass
from concourse import mybir
from contextlib import ExitStack
import numpy as np

F32 = mybir.dt.float32
U32 = mybir.dt.uint32
ALU = mybir.AluOpType
ACT = mybir.ActivationFunctionType
AX = mybir.AxisListType

P = 128
D = 1024
C = D // P
T = 512
SB, ST = 8, 8
NS = SB * ST
N = T + NS
HALF = N // 2
NB = T // P
HD = 64
TAPS = 31
PAST = TAPS - 1
HEADS, TOPK, NKEYS = 8, 16, 128
KAPPA = float(np.exp(-0.5))
RMS_EPS, GN_EPS, LN_EPS = 1e-6, 6.4e-4, 1e-5
LEVELS = 7
SLEVELS = 3
LOWEST = -3.0e38

(MU0, W0, A0, K_K, K_A, R_K, LN_W, LN_B, B_PA, B_PG, B_DW, CLN_G, CLN_B, B_P2,
 NMIX0, NMIX1, NFFN0, NFFN1, NFIN, TAP0) = (0, 6, 7, 8, 9, 10, 11, 12, 13, 14, 15, 16, 17, 18,
                                            19, 20, 21, 22, 23, 24)
NPAR = TAP0 + TAPS


class Steps:

    def __init__(self, sem, names, start=0):
        self.sem, self.names, self.start, self.next = sem, list(names), start, 0

    def value(self, name, i=0):
        return i * len(self.names) + (self.start + self.names.index(name) + 1)

    def all_before(self, i):
        return i * len(self.names) + self.start

    def begin(self, engine):
        assert self.start == 1 and self.next == 0
        engine.sem_inc(self.sem, 1)

    def at(self, name):
        assert self.names[self.next] == name, (name, self.names[self.next])
        self.next = (self.next + 1) % len(self.names)
        return self.sem


class Region:

    def __init__(self, tensor, at=0):
        self.tensor, self.at = tensor, at

    def cut(self, *shape, parts=P, dtype=F32):
        n = int(np.prod(shape))
        view = self.tensor[0:parts, self.at:self.at + n]
        self.at += n
        assert self.at <= self.tensor.shape[1], (self.at, self.tensor.shape)
        if dtype != F32:
            view = view.bitcast(dtype)
        if len(shape) == 2:
            view = view.rearrange("p (a b) -> p a b", b=shape[1])
        if len(shape) == 3:
            view = view.rearrange("p (a b c) -> p a b c", b=shape[1], c=shape[2])
        return view


def halves(view):
    return view.rearrange("p (a b) -> p a b", b=HALF)


def of_banks(psum, bank, parts=slice(0, P)):
    return psum[parts, bank:bank + 2, 0:HALF]


def unsq(view, axis, n):
    return view.unsqueeze(axis).to_broadcast(list(view.shape[:axis]) + [n] + list(view.shape[axis:]))


def rmsnorm(nc, K, gain, out, store=None):
    n = K.name()
    act_s = Steps(K.sem(f"{n}_act"), [f"square{c}" for c in range(C)] + ["root"])
    pe_s = Steps(K.sem(f"{n}_pe"), [f"summed{c}" for c in range(C)])
    dve_s = Steps(K.sem(f"{n}_dve"), [f"scaled{c}" for c in range(C)])
    stored = K.sem(f"{n}_stored")
    sq = [K.small[:, 0:N], K.small[:, N:2 * N]]
    root, inv = K.small[:, 2 * N:3 * N], K.small[:, 3 * N:4 * N]
    with nc.Block() as block:
        @block.scalar
        def _(act):
            for c in range(C):
                if c >= 2:
                    act.wait_ge(pe_s.sem, pe_s.value(f"summed{c - 2}"))
                act.activation(sq[c % 2], K.x[:, c, :], ACT.Square).then_inc(act_s.at(f"square{c}"), 1)
            act.wait_ge(pe_s.sem, pe_s.value(f"summed{C - 1}"))
            act.activation(halves(root), of_banks(K.ps, 0), ACT.Sqrt,
                                      bias=K.eps[:, 0:1], scale=1.0 / D).then_inc(act_s.at("root"), 1)

        @block.tensor
        def _(pe):
            for c in range(C):
                pe.wait_ge(act_s.sem, act_s.value(f"square{c}"))
                for h in range(2):
                    last = pe.matmul(K.ps[:, h, 0:HALF], K.ones, sq[c % 2][:, h * HALF:(h + 1) * HALF],
                                     start=c == 0, stop=c == C - 1)
                last.then_inc(pe_s.at(f"summed{c}"), 1)

        @block.vector
        def _(dve):
            dve.wait_ge(act_s.sem, act_s.value("root"))
            dve.reciprocal(inv, root)
            dve.drain()
            for c in range(C):
                dve.scalar_tensor_tensor(out=out[:, c, :], in0=K.x[:, c, :],
                                                    scalar=K.par[:, gain, c:c + 1], in1=inv,
                                                    op0=ALU.mult, op1=ALU.mult).then_inc(dve_s.at(f"scaled{c}"), 1)

        @block.sync
        def _(sp):
            if store is not None:
                for c in range(C):
                    sp.wait_ge(dve_s.sem, dve_s.value(f"scaled{c}"))
                    sp.dma_start(store[:, c, :], out[:, c, :]).then_inc(stored, 16)
                sp.wait_ge(stored, 16 * C)


def linear_into_x(nc, K, weights, src, bias=None):
    n = K.name()
    loaded = [K.sem(f"{n}_w{j}") for j in range(2)]
    pe_s = Steps(K.sem(f"{n}_pe"), ["product0", "product1"])
    dve_s = Steps(K.sem(f"{n}_dve"), ["added0", "added1"], start=1)
    with nc.Block() as block:
        @block.sync
        def _(sp):
            for j in range(2):
                sp.dma_start(K.w[j], weights[j]).then_inc(loaded[j], 16)
            with sp.Fori(1, C // 2) as i:
                for j in range(2):
                    sp.wait_ge(pe_s.sem, i * 2 + (j - 1))
                    sp.dma_start(K.w[j], weights[bass.ds(i * 2 + j, 1)].squeeze(0)).then_inc(loaded[j], 16)

        @block.tensor
        def _(pe):
            with pe.Fori(0, C // 2) as i:
                for j in range(2):
                    pe.wait_ge(dve_s.sem, dve_s.all_before(i))
                    pe.wait_ge(loaded[j], i * 16 + 16)
                    for h in range(2):
                        for k in range(C):
                            last = pe.matmul(K.ps[:, 2 * j + h, 0:HALF], K.w[j][:, k, :],
                                             src[:, k, h * HALF:(h + 1) * HALF],
                                             start=k == 0, stop=k == C - 1)
                    last.then_inc(pe_s.at(f"product{j}"), 1)

        @block.vector
        def _(dve):
            dve_s.begin(dve)
            with dve.Fori(0, C // 2) as i:
                for j in range(2):
                    dve.wait_ge(pe_s.sem, pe_s.value(f"product{j}", i))
                    dst = K.x[:, bass.ds(i * 2 + j, 1), :].squeeze(1).rearrange("p (a b) -> p a b", b=HALF)
                    add = K.bias_cols[:, j:j + 1] if bias is not None else 0.0
                    if bias is not None:
                        dve.tensor_copy(add, K.par[:, bias, bass.ds(i * 2 + j, 1)])
                        dve.drain()
                    dve.scalar_tensor_tensor(out=dst, in0=of_banks(K.ps, 2 * j), scalar=add,
                                                        in1=dst, op0=ALU.add, op1=ALU.add).then_inc(dve_s.at(f"added{j}"), 1)


def load_constants(nc, K, I):
    loaded = K.sem("constants_loaded")
    with nc.Block() as block:
        @block.sync
        def _(sp):
            pairs = [(K.x, I["x"]), (K.par, I["par"]), (K.cst, I["cst"]), (K.level, I["level"])]
            for dst, src in pairs:
                sp.dma_start(dst, src).then_inc(loaded, 16)
            sp.wait_ge(loaded, 16 * len(pairs))

        @block.gpsimd
        def _(pool):
            for j, eps in enumerate((RMS_EPS, GN_EPS, LN_EPS)):
                pool.memset(K.eps[:, j:j + 1], eps)


def time_mix_inputs(nc, K, I, h, xx, xm, hid_wa, hid_g):
    n = "mix"
    low, shift = K.low, K.shift
    loaded = K.sem(f"{n}_loaded")
    stored, rows_ready = K.sem(f"{n}_stored"), K.sem(f"{n}_rows_ready")
    new_shift = K.new_shift
    mixes = [f"mixed{m}_{k}" for m in (3, 4, 5) for k in range(C)]
    dve_s = Steps(K.sem(f"{n}_dve"), mixes)
    pe_s = Steps(K.sem(f"{n}_pe"), [f"used{m}_{k}" for m in (3, 4, 5) for k in range(C)])
    tmp = [K.small[:, 0:N], K.small[:, N:2 * N]]
    with nc.Block() as block:
        @block.sync
        def _(sp):
            sp.dma_start(low, I["low1"]).then_inc(loaded, 16)
            sp.dma_start(shift, I["shift"]).then_inc(loaded, 16)
            sp.wait_ge(rows_ready, 1)
            sp.dma_start(I["o_shift"], new_shift).then_inc(stored, 16)
            sp.wait_ge(stored, 16)

        @block.vector
        def _(dve):
            dve.wait_ge(loaded, 32)
            hs, xs = (v[:, :, T:N].rearrange("p c (b t) -> p c b t", t=ST) for v in (h, xx))
            dve.tensor_tensor(xx[:, :, 1:T], h[:, :, 0:T - 1], h[:, :, 1:T], ALU.subtract)
            dve.tensor_scalar(xx[:, :, 0:1], h[:, :, 0:1], -1.0, None, ALU.mult)
            dve.tensor_tensor(xs[:, :, :, 0], shift, hs[:, :, :, 0], ALU.subtract)
            for c in range(C):
                dve.tensor_tensor(xs[:, c, :, 1:ST], hs[:, c, :, 0:ST - 1], hs[:, c, :, 1:ST], ALU.subtract)
            dve.drain()
            q = 0
            for m in (3, 4, 5):
                for k in range(C):
                    if q >= 2:
                        dve.wait_ge(pe_s.sem, q - 1)
                    dve.scalar_tensor_tensor(out=tmp[q % 2], in0=xx[:, k, :],
                                                        scalar=K.par[:, MU0 + m, k:k + 1], in1=h[:, k, :],
                                                        op0=ALU.mult, op1=ALU.add).then_inc(dve_s.at(f"mixed{m}_{k}"), 1)
                    q += 1
            for m in range(3):
                for k in range(C):
                    dve.scalar_tensor_tensor(out=xm[m][:, k, :], in0=xx[:, k, :],
                                             scalar=K.par[:, MU0 + m, k:k + 1], in1=h[:, k, :],
                                             op0=ALU.mult, op1=ALU.add)

        @block.tensor
        def _(pe):
            pe.wait_ge(loaded, 32)
            q = 0
            for m, part, lo, hi in ((3, slice(0, 64), 0, 64), (4, slice(64, P), 64, 128), (5, slice(0, P), 128, 256)):
                for k in range(C):
                    pe.wait_ge(dve_s.sem, dve_s.value(f"mixed{m}_{k}"))
                    for s in range(2):
                        last = pe.matmul(K.ps[part, 2 * (m - 3) + s, 0:HALF], low[:, k, lo:hi],
                                         tmp[q % 2][:, s * HALF:(s + 1) * HALF],
                                         start=k == 0, stop=k == C - 1)
                    last.then_inc(pe_s.at(f"used{m}_{k}"), 1)
                    q += 1

        @block.scalar
        def _(act):
            act.activation(new_shift[:, :, 0:1], h[:, :, T - 1:T], ACT.Copy)
            act.activation(new_shift[:, :, 1:], h[:, :, T:N].rearrange("p c (b t) -> p c b t", t=ST)[:, :, :, ST - 1],
                           ACT.Copy)
            act.drain().then_inc(rows_ready, 1)
            act.wait_ge(pe_s.sem, pe_s.value(f"used3_{C - 1}"))
            act.activation(halves(hid_wa[0:64, :]), of_banks(K.ps, 0, slice(0, 64)), ACT.Tanh)
            act.wait_ge(pe_s.sem, pe_s.value(f"used4_{C - 1}"))
            act.activation(halves(hid_wa[64:P, :]), of_banks(K.ps, 2, slice(64, P)), ACT.Copy)
            act.wait_ge(pe_s.sem, pe_s.value(f"used5_{C - 1}"))
            act.activation(halves(hid_g), of_banks(K.ps, 4), ACT.Sigmoid)


def wkv(nc, K, I, xm, y_out, hid_wa, hid_g, R):
    f = lambda: R.cut(N)
    dead_at = R.at
    r_s, k_s, sg, sq, kk, cum, lprev, kf = f(), f(), f(), f(), f(), f(), f(), f()
    av_at = R.at
    av, v_s, g_s, nrm = f(), f(), f(), f()
    e_pos, e_neg = f(), f()
    prev_at = R.at
    e_prev, at, bt, kt, rt, bon = f(), f(), f(), f(), f(), f()
    ba, rk = lprev, sq
    y_s, yc, ysq, sd = e_pos, e_neg, e_prev, nrm
    low2 = R.cut(2, P)
    prm = R.cut(NPAR)
    sc = R.cut(3 * NB + SB)
    esc = R.cut(3 * NB + SB)
    ptok = R.cut(3, NB, P)
    l_at = R.at
    L, LT, X, XT = (R.cut(2, NB, P) for _ in range(4))
    g_at = R.at
    G, RB, RK = (R.cut(2, NB, P) for _ in range(3))
    Q0 = Region(K.arena, dead_at)
    co, coT, y1, y2 = ([Q0.cut(NB, P) for _ in range(2)] for _ in range(4))
    assert Q0.at <= av_at
    state = R.cut(P)
    Q0 = Region(K.arena, av_at)
    sc_state, s_tmp = [Q0.cut(P) for _ in range(2)], Q0.cut(P)
    Q0 = Region(K.arena, prev_at)
    r_tok, u_tok = Q0.cut(P), Q0.cut(P)
    Q = Region(K.arena, R.at)
    s_state = Q.cut(SB, P)
    Q2 = Region(K.arena, l_at)
    stok = Q2.cut(3, P, parts=NS)
    sL, sLT, sX, sXT, sG, sRB, sRK, sco, scoT = (Q2.cut(2, NS, parts=NS) for _ in range(9))
    sy1, sy2 = Q2.cut(2, NS, parts=NS), Q2.cut(2, NS, parts=NS)
    rT, rT2 = Q2.cut(NS), Q2.cut(NS)
    sr_tok, su_tok = Q2.cut(P, parts=NS), Q2.cut(P, parts=NS)
    Q3 = Region(K.arena, g_at)
    u_exp, v_exp = Q3.cut(SB, P, parts=NS), Q3.cut(SB, P, parts=NS)
    s_prod = Q3.cut(SB, P)

    both = lambda l: 1 if l < LEVELS - 1 else 2
    wl = [K.sem(f"wkv_w{j}") for j in range(3)]
    small_loaded, state_loaded = K.sem("wkv_small_loaded"), K.sem("wkv_state_loaded")
    stored, zeroed = K.sem("wkv_stored"), K.sem("wkv_zeroed")
    pe_s = Steps(K.sem("wkv_pe"),
                 ["k", "w", "a", "r", "v", "g", "norm", "bonus", "tok_b", "tok_k", "tok_v"]
                 + [f"gram_{x}{e}" for e in range(2) for x in ("L", "LT", "G", "RB", "RK")]
                 + [f"{x}{l}_{e}" for l in range(1, LEVELS) for x in ("y1", "y2", "dXT", "dX")[::both(l)] for e in range(2)]
                 + [f"{x}{b}" for b in range(NB) for x in ("R", "U", "Y", "S")]
                 + ["s_tok", "s_gram0", "s_gram1"]
                 + [f"s_{x}{l}" for l in range(1, SLEVELS) for x in ("y", "d")]
                 + ["s_RT", "s_R", "s_U", "s_Y", "s_S", "mean", "var"], start=1)
    act_s = Steps(K.sem("wkv_act"),
                  ["k", "ksq", "w", "a", "r", "v", "g", "norm", "exps", "tok_b", "tok_k", "tok_v"]
                  + [f"gram_{x}{e}" for e in range(2) for x in ("L", "LT")]
                  + [f"{x}{l}_{e}" for l in range(1, LEVELS) for x in ("y1", "y2")[::both(l)] for e in range(2)]
                  + [f"{x}{b}" for b in range(NB) for x in ("R", "U")]
                  + ["Y", "s_tok"]
                  + [f"s_y{l}" for l in range(1, SLEVELS)]
                  + ["s_R", "s_U", "ysq", "sd"], start=1)
    dve_s = Steps(K.sem("wkv_dve"),
                  ["logs", "rk", "factors", "bonus"]
                  + [f"gram{x}{e}" for e in range(2) for x in ("G", "RB", "RK")]
                  + ["level0"]
                  + [f"{x}{l}_{e}" for l in range(1, LEVELS) for x in ("XT", "X")[::both(l)] for e in range(2)]
                  + [f"state{b}" for b in range(NB)]
                  + ["s_gram"]
                  + [f"s_X{l}" for l in range(1, SLEVELS)]
                  + ["s_RT", "s_exp", "s_y", "s_state", "yc", "y"], start=1)
    pool_s = Steps(K.sem("wkv_pool"), [f"{x}{l}_{e}" for l in range(1, LEVELS) for e in range(2) for x in ("co", "coT")[::both(l)]])
    ps = K.ps
    lev = lambda l, t: K.level[:, 2 * l + t, :]

    with nc.Block() as block:
        @block.sync
        def _(sp):
            sp.sem_inc(stored, 16)
            sp.wait_ge(zeroed, 1)
            with sp.Fori(0, C) as i:
                sp.wait_ge(pe_s.sem, pe_s.all_before(i))
                sp.wait_ge(act_s.sem, act_s.all_before(i))
                sp.wait_ge(dve_s.sem, dve_s.all_before(i))
                sp.wait_ge(stored, i * 64 + 16)
                for j, m in enumerate((1, 0, 2)):
                    sp.dma_start(K.w[j], I["w_rkv"][bass.ds(i * 3 + m, 1)].squeeze(0)).then_inc(wl[j], 16)
                    if j == 0:
                        sp.dma_start(low2, I["low2"][bass.ds(i, 1)].squeeze(0)).then_inc(small_loaded, 16)
                        sp.dma_start(prm, I["cpar"][bass.ds(i, 1)].squeeze(0)).then_inc(small_loaded, 16)
                for e in range(2):
                    q = slice(64 * e, 64 * e + 64)
                    sp.dma_start(s_state[q, :, q], I["state"][bass.ds(i, 1), q].squeeze(0)).then_inc(state_loaded, 16)
                sp.wait_ge(dve_s.sem, dve_s.value(f"state{NB - 1}", i))
                for e in range(2):
                    q = slice(64 * e, 64 * e + 64)
                    sp.dma_start(I["o_wkv_p"][bass.ds(i, 1), q].squeeze(0), state[q, q]).then_inc(stored, 16)
                sp.wait_ge(dve_s.sem, dve_s.value("s_state", i))
                for e in range(2):
                    q = slice(64 * e, 64 * e + 64)
                    sp.dma_start(I["o_wkv_s"][bass.ds(i, 1), q].squeeze(0), s_state[q, :, q]).then_inc(stored, 16)
            sp.wait_ge(stored, C * 64 + 16)

        @block.tensor
        def _(pe):
            pe_s.begin(pe)

            def project(src, w, bank, name):
                for h in range(2):
                    for k in range(C):
                        last = pe.matmul(ps[:, bank + h, 0:HALF], w[:, k, :], src[:, k, h * HALF:(h + 1) * HALF],
                                         start=k == 0, stop=k == C - 1)
                last.then_inc(pe_s.at(name), 1)

            def expand(w, src, bank, name):
                for h in range(2):
                    last = pe.matmul(ps[:, bank + h, 0:HALF], w, src[:, h * HALF:(h + 1) * HALF], start=True, stop=True)
                last.then_inc(pe_s.at(name), 1)

            with pe.Fori(0, C) as i:
                pe.wait_ge(act_s.sem, act_s.all_before(i))
                pe.wait_ge(dve_s.sem, dve_s.all_before(i))
                pe.wait_ge(wl[0], i * 16 + 16)
                project(xm[1], K.w[0], 0, "k")
                pe.wait_ge(small_loaded, i * 32 + 32)
                expand(low2[0:64, 0, :], hid_wa[0:64, :], 2, "w")
                expand(low2[64:P, 0, :], hid_wa[64:P, :], 4, "a")
                pe.wait_ge(wl[1], i * 16 + 16)
                project(xm[0], K.w[1], 6, "r")
                pe.wait_ge(act_s.sem, act_s.value("ksq", i))
                pe.wait_ge(wl[2], i * 16 + 16)
                project(xm[2], K.w[2], 0, "v")
                pe.wait_ge(act_s.sem, act_s.value("w", i))
                expand(low2[:, 1, :], hid_g, 2, "g")
                pe.wait_ge(act_s.sem, act_s.value("a", i))
                expand(K.headones, sq, 4, "norm")
                pe.wait_ge(dve_s.sem, dve_s.value("rk", i))
                pe.wait_ge(act_s.sem, act_s.value("r", i))
                expand(K.headones, rk, 6, "bonus")
                pe.wait_ge(act_s.sem, act_s.value("v", i))
                pe.wait_ge(act_s.sem, act_s.value("g", i))
                pe.wait_ge(act_s.sem, act_s.value("norm", i))
                pe.wait_ge(dve_s.sem, dve_s.value("bonus", i))
                for j, (src, name) in enumerate(((bt, "tok_b"), (kt, "tok_k"), (v_s, "tok_v"))):
                    for b in range(NB):
                        last = pe.transpose(ps[:, j, b * P:(b + 1) * P], src[:, b * P:(b + 1) * P], K.ident)
                    last.then_inc(pe_s.at(name), 1)
                bank = {(0, "L"): 4, (0, "LT"): 5, (0, "G"): 6, (0, "RB"): 7, (0, "RK"): 0,
                        (1, "L"): 1, (1, "LT"): 2, (1, "G"): 3, (1, "RB"): 4, (1, "RK"): 5}
                for e in range(2):
                    q = slice(64 * e, 64 * e + 64)
                    for name, left, right, free in (("L", at, bt, (None, "tok_k")), ("LT", bt, at, (None, "tok_v")),
                                                    ("G", kt, at, (None, None)), ("RB", bt, rt, (None, "gram_L0")),
                                                    ("RK", kt, rt, ("tok_b", "gram_LT0"))):
                        if free[e]:
                            pe.wait_ge(act_s.sem, act_s.value(free[e], i))
                        for b in range(NB):
                            t = slice(b * P, (b + 1) * P)
                            last = pe.matmul(ps[:, bank[e, name], t], left[q, t], right[q, t], start=True, stop=True)
                        last.then_inc(pe_s.at(f"gram_{name}{e}"), 1)
                pe.wait_ge(dve_s.sem, dve_s.value("level0", i))
                for l in range(1, LEVELS):
                    for e in range(2):
                        pe.wait_ge(pool_s.sem, pool_s.value(f"co{l}_{e}", i))
                        if l > 1:
                            pe.wait_ge(dve_s.sem, dve_s.value(f"XT{l - 1}_{e}", i))
                        for b in range(NB):
                            last = pe.matmul(ps[:, 4 * e, b * P:(b + 1) * P], co[e][:, b, :], XT[:, e, b, :],
                                             start=True, stop=True)
                        last.then_inc(pe_s.at(f"y1{l}_{e}"), 1)
                    for e in range(2) if both(l) == 1 else ():
                        pe.wait_ge(pool_s.sem, pool_s.value(f"coT{l}_{e}", i))
                        if l > 1:
                            pe.wait_ge(dve_s.sem, dve_s.value(f"X{l - 1}_{e}", i))
                        for b in range(NB):
                            last = pe.matmul(ps[:, 4 * e + 1, b * P:(b + 1) * P], coT[e][:, b, :], X[:, e, b, :],
                                             start=True, stop=True)
                        last.then_inc(pe_s.at(f"y2{l}_{e}"), 1)
                    for e in range(2):
                        pe.wait_ge(act_s.sem, act_s.value(f"y1{l}_{e}", i))
                        if l > 1:
                            pe.wait_ge(dve_s.sem, dve_s.value(f"X{l - 1}_{e}", i))
                        for b in range(NB):
                            last = pe.matmul(ps[:, 4 * e + 2, b * P:(b + 1) * P], X[:, e, b, :], y1[e][:, b, :],
                                             start=True, stop=True)
                        last.then_inc(pe_s.at(f"dXT{l}_{e}"), 1)
                    for e in range(2) if both(l) == 1 else ():
                        pe.wait_ge(act_s.sem, act_s.value(f"y2{l}_{e}", i))
                        for b in range(NB):
                            last = pe.matmul(ps[:, 4 * e + 3, b * P:(b + 1) * P], XT[:, e, b, :], y2[e][:, b, :],
                                             start=True, stop=True)
                        last.then_inc(pe_s.at(f"dX{l}_{e}"), 1)
                pe.wait_ge(dve_s.sem, dve_s.value(f"XT{LEVELS - 1}_1", i))
                for b in range(NB):
                    t = slice(b * P, (b + 1) * P)
                    if b:
                        pe.wait_ge(dve_s.sem, dve_s.value(f"state{b - 1}", i))
                    pe.matmul(ps[:, 0, 0:P], at[:, t], sc_state[b % 2], start=True, stop=False)
                    for e in range(2):
                        q = slice(64 * e, 64 * e + 64)
                        last = pe.matmul(ps[:, 0, q], G[:, e, b, :], ptok[:, 2, b, q], start=False, stop=e == 1)
                    last.then_inc(pe_s.at(f"R{b}"), 1)
                    pe.wait_ge(act_s.sem, act_s.value(f"R{b}", i))
                    for e in range(2):
                        q = slice(64 * e, 64 * e + 64)
                        last = pe.matmul(ps[:, 1, q], XT[:, e, b, :], r_tok[:, q], start=True, stop=True)
                    last.then_inc(pe_s.at(f"U{b}"), 1)
                    pe.matmul(ps[:, 3, t], sc_state[b % 2], rt[:, t], start=True, stop=False)
                    pe.wait_ge(act_s.sem, act_s.value(f"U{b}", i))
                    for e in range(2):
                        q = slice(64 * e, 64 * e + 64)
                        pe.matmul(ps[q, 3, t], u_tok[:, q], RB[:, e, b, :], start=False, stop=False)
                        last = pe.matmul(ps[q, 3, t], ptok[:, 2, b, q], RK[:, e, b, :], start=False, stop=True)
                    last.then_inc(pe_s.at(f"Y{b}"), 1)
                    pe.matmul(ps[:, 2, 0:P], ptok[:, 0, b, :], u_tok, start=True, stop=False)
                    last = pe.matmul(ps[:, 2, 0:P], ptok[:, 1, b, :], ptok[:, 2, b, :], start=False, stop=True)
                    last.then_inc(pe_s.at(f"S{b}"), 1)
                pe.wait_ge(dve_s.sem, dve_s.value(f"state{NB - 1}", i))
                pe.wait_ge(act_s.sem, act_s.value("Y", i))
                pe.nop(nofuse=True)
                for j, src in enumerate((bt, kt, v_s)):
                    last = pe.transpose(ps[0:NS, 4, j * P:(j + 1) * P], src[:, T:N], K.ident)
                last.then_inc(pe_s.at("s_tok"), 1)
                for e in range(2):
                    q = slice(64 * e, 64 * e + 64)
                    for j, (left, right) in enumerate(((at, bt), (bt, at), (kt, at), (bt, rt), (kt, rt))):
                        last = pe.matmul(ps[0:NS, 5 + e, j * NS:(j + 1) * NS], left[q, T:N], right[q, T:N],
                                         start=True, stop=True)
                    last.then_inc(pe_s.at(f"s_gram{e}"), 1)
                for l in range(1, SLEVELS):
                    pe.wait_ge(dve_s.sem, dve_s.value("s_gram" if l == 1 else f"s_X{l - 1}", i))
                    pe.nop(nofuse=True)
                    for e in range(2):
                        pe.matmul(ps[0:NS, 0, e * NS:(e + 1) * NS], sco[:, e, :], sXT[:, e, :], start=True, stop=True)
                    for e in range(2):
                        last = pe.matmul(ps[0:NS, 0, (2 + e) * NS:(3 + e) * NS], scoT[:, e, :], sX[:, e, :],
                                         start=True, stop=True)
                    last.then_inc(pe_s.at(f"s_y{l}"), 1)
                    pe.wait_ge(act_s.sem, act_s.value(f"s_y{l}", i))
                    pe.nop(nofuse=True)
                    for e in range(2):
                        pe.matmul(ps[0:NS, 1, e * NS:(e + 1) * NS], sX[:, e, :], sy1[:, e, :], start=True, stop=True)
                    for e in range(2):
                        last = pe.matmul(ps[0:NS, 1, (2 + e) * NS:(3 + e) * NS], sXT[:, e, :], sy2[:, e, :],
                                         start=True, stop=True)
                    last.then_inc(pe_s.at(f"s_d{l}"), 1)
                pe.wait_ge(state_loaded, i * 32 + 32)
                for b in range(SB):
                    pe.matmul(ps[:, 2, b * ST:(b + 1) * ST], s_state[:, b, :], at[:, T + b * ST:T + (b + 1) * ST],
                              start=True, stop=True)
                for b in range(SB):
                    pe.matmul(ps[:, 3, b * ST:(b + 1) * ST], s_state[:, b, :], rt[:, T + b * ST:T + (b + 1) * ST],
                              start=True, stop=True)
                for e in range(2):
                    q = slice(64 * e, 64 * e + 64)
                    last = pe.matmul(ps[q, 2, NS:2 * NS], stok[:, 2, q], sG[:, e, :], start=True, stop=True)
                last.then_inc(pe_s.at("s_RT"), 1)
                pe.wait_ge(dve_s.sem, dve_s.value("s_RT", i))
                pe.nop(nofuse=True)
                pe.transpose(ps[0:NS, 0, 0:P], rT, K.ident).then_inc(pe_s.at("s_R"), 1)
                pe.wait_ge(act_s.sem, act_s.value("s_R", i))
                pe.nop(nofuse=True)
                for e in range(2):
                    q = slice(64 * e, 64 * e + 64)
                    last = pe.matmul(ps[0:NS, 1, q], sXT[:, e, :], sr_tok[:, q], start=True, stop=True)
                last.then_inc(pe_s.at("s_U"), 1)
                pe.wait_ge(act_s.sem, act_s.value("s_U", i))
                pe.nop(nofuse=True)
                for e in range(2):
                    q = slice(64 * e, 64 * e + 64)
                    pe.matmul(ps[q, 3, NS:2 * NS], su_tok[:, q], sRB[:, e, :], start=True, stop=False)
                    last = pe.matmul(ps[q, 3, NS:2 * NS], stok[:, 2, q], sRK[:, e, :], start=False, stop=True)
                last.then_inc(pe_s.at("s_Y"), 1)
                pe.wait_ge(dve_s.sem, dve_s.value("s_exp", i))
                for h in range(2):
                    hb = slice(4 * h, 4 * h + 4)
                    pe.matmul(ps[:, 6 + h, :], stok[:, 0, :], u_exp[:, hb, :], start=True, stop=False)
                    last = pe.matmul(ps[:, 6 + h, :], stok[:, 1, :], v_exp[:, hb, :], start=False, stop=True)
                last.then_inc(pe_s.at("s_S"), 1)
                pe.wait_ge(dve_s.sem, dve_s.value("s_y", i))
                expand(K.headones, y_s, 0, "mean")
                pe.wait_ge(act_s.sem, act_s.value("ysq", i))
                expand(K.headones, ysq, 4, "var")

        @block.scalar
        def _(act):
            act_s.begin(act)
            with act.Fori(0, C) as i:
                act.wait_ge(dve_s.sem, dve_s.all_before(i))
                act.wait_ge(pe_s.sem, pe_s.all_before(i))
                act.wait_ge(small_loaded, i * 32 + 32)
                act.wait_ge(pe_s.sem, pe_s.value("k", i))
                act.activation(halves(k_s), of_banks(ps, 0), ACT.Copy).then_inc(act_s.at("k"), 1)
                act.activation(halves(sq), of_banks(ps, 0), ACT.Square, scale=prm[:, K_K:K_K + 1]).then_inc(act_s.at("ksq"), 1)
                act.wait_ge(pe_s.sem, pe_s.value("w", i))
                act.activation(halves(sg), of_banks(ps, 2), ACT.Sigmoid, bias=prm[:, W0:W0 + 1]).then_inc(act_s.at("w"), 1)
                act.wait_ge(pe_s.sem, pe_s.value("a", i))
                act.activation(halves(av), of_banks(ps, 4), ACT.Sigmoid, bias=prm[:, A0:A0 + 1]).then_inc(act_s.at("a"), 1)
                act.wait_ge(pe_s.sem, pe_s.value("r", i))
                act.activation(halves(r_s), of_banks(ps, 6), ACT.Copy).then_inc(act_s.at("r"), 1)
                act.wait_ge(pe_s.sem, pe_s.value("v", i))
                act.activation(halves(v_s), of_banks(ps, 0), ACT.Copy).then_inc(act_s.at("v"), 1)
                act.wait_ge(pe_s.sem, pe_s.value("g", i))
                act.activation(halves(g_s), of_banks(ps, 2), ACT.Copy).then_inc(act_s.at("g"), 1)
                act.wait_ge(pe_s.sem, pe_s.value("norm", i))
                act.activation(halves(nrm), of_banks(ps, 4), ACT.Sqrt).then_inc(act_s.at("norm"), 1)
                act.wait_ge(dve_s.sem, dve_s.value("logs", i))
                act.activation(e_pos, cum, ACT.Exp, scale=-KAPPA)
                act.activation(e_neg, cum, ACT.Exp, scale=KAPPA)
                act.activation(e_prev, lprev, ACT.Exp, scale=-KAPPA)
                act.activation(esc, sc, ACT.Exp, scale=-KAPPA).then_inc(act_s.at("exps"), 1)
                for j, name in enumerate(("tok_b", "tok_k", "tok_v")):
                    act.wait_ge(pe_s.sem, pe_s.value(name, i))
                    act.activation(ptok[:, j], ps[:, j, :].rearrange("p (b f) -> p b f", f=P), ACT.Copy).then_inc(act_s.at(name), 1)
                for e, (bL, bLT) in enumerate(((4, 5), (1, 2))):
                    for name, dst, bank in (("L", L, bL), ("LT", LT, bLT)):
                        act.wait_ge(pe_s.sem, pe_s.value(f"gram_{name}{e}", i))
                        act.activation(dst[:, e], ps[:, bank, :].rearrange("p (b f) -> p b f", f=P), ACT.Copy).then_inc(act_s.at(f"gram_{name}{e}"), 1)
                for l in range(1, LEVELS):
                    for j, (name, dst) in enumerate((("y1", y1), ("y2", y2))[::both(l)]):
                        for e in range(2):
                            act.wait_ge(pe_s.sem, pe_s.value(f"{name}{l}_{e}", i))
                            if l > 1:
                                act.wait_ge(pe_s.sem, pe_s.value(f"{('dXT', 'dX')[j]}{l - 1}_{e}", i))
                            act.activation(dst[e], ps[:, 4 * e + j, :].rearrange("p (b f) -> p b f", f=P),
                                                      ACT.Copy).then_inc(act_s.at(f"{name}{l}_{e}"), 1)
                for b in range(NB):
                    act.wait_ge(pe_s.sem, pe_s.value(f"R{b}", i))
                    act.activation(r_tok, ps[:, 0, 0:P], ACT.Copy).then_inc(act_s.at(f"R{b}"), 1)
                    act.wait_ge(pe_s.sem, pe_s.value(f"U{b}", i))
                    act.activation(u_tok, ps[:, 1, 0:P], ACT.Copy).then_inc(act_s.at(f"U{b}"), 1)
                act.wait_ge(pe_s.sem, pe_s.value(f"Y{NB - 1}", i))
                act.activation(y_s[:, 0:T], ps[:, 3, :], ACT.Copy).then_inc(act_s.at("Y"), 1)
                act.wait_ge(dve_s.sem, dve_s.value(f"state{NB - 1}", i))
                act.wait_ge(pe_s.sem, pe_s.value("s_tok", i))
                act.activation(stok, ps[0:NS, 4, 0:3 * P].rearrange("p (j f) -> p j f", f=P), ACT.Copy).then_inc(act_s.at("s_tok"), 1)
                for l in range(1, SLEVELS):
                    act.wait_ge(pe_s.sem, pe_s.value(f"s_y{l}", i))
                    if l > 1:
                        act.wait_ge(pe_s.sem, pe_s.value(f"s_d{l - 1}", i))
                    act.activation(sy1, ps[0:NS, 0, 0:2 * NS].rearrange("p (e f) -> p e f", f=NS), ACT.Copy)
                    act.activation(sy2, ps[0:NS, 0, 2 * NS:4 * NS].rearrange("p (e f) -> p e f", f=NS),
                                              ACT.Copy).then_inc(act_s.at(f"s_y{l}"), 1)
                act.wait_ge(pe_s.sem, pe_s.value("s_R", i))
                act.activation(sr_tok, ps[0:NS, 0, 0:P], ACT.Copy).then_inc(act_s.at("s_R"), 1)
                act.wait_ge(pe_s.sem, pe_s.value("s_U", i))
                act.activation(su_tok, ps[0:NS, 1, 0:P], ACT.Copy).then_inc(act_s.at("s_U"), 1)
                act.wait_ge(dve_s.sem, dve_s.value("yc", i))
                act.activation(ysq, yc, ACT.Square).then_inc(act_s.at("ysq"), 1)
                act.wait_ge(pe_s.sem, pe_s.value("var", i))
                act.activation(halves(sd), of_banks(ps, 4), ACT.Sqrt, bias=K.eps[:, 1:2], scale=1.0 / HD).then_inc(act_s.at("sd"), 1)

        @block.vector
        def _(dve):
            dve_s.begin(dve)
            tt, ts, stt = dve.tensor_tensor, dve.tensor_scalar, dve.scalar_tensor_tensor
            dve.memset(s_state, 0.0).then_inc(zeroed, 1)
            with dve.Fori(0, C) as i:
                dve.wait_ge(act_s.sem, act_s.all_before(i))
                dve.wait_ge(pe_s.sem, pe_s.all_before(i))
                dve.wait_ge(small_loaded, i * 32 + 32)
                dve.wait_ge(stored, i * 64 + 16)
                dve.memset(state, 0.0)
                dve.wait_ge(act_s.sem, act_s.value("w", i))
                dve.tensor_tensor_scan(cum, K.reset, sg, 0.0, ALU.mult, ALU.add)
                dve.drain()
                blocks = cum[:, 0:T].rearrange("p (b t) -> p b t", t=P)
                seqs = cum[:, T:N].rearrange("p (b t) -> p b t", t=ST)
                dve.tensor_copy(sc[:, 0:NB], blocks[:, :, P // 2 - 1])
                dve.tensor_copy(sc[:, NB:2 * NB], blocks[:, :, P - 1])
                dve.tensor_copy(sc[:, 3 * NB:3 * NB + SB], seqs[:, :, ST - 1])
                dve.drain()
                tt(sc[:, 2 * NB:3 * NB], sc[:, NB:2 * NB], sc[:, 0:NB], ALU.subtract)
                tt(blocks, blocks, unsq(sc[:, 0:NB], 2, P), ALU.subtract)
                dve.drain()
                tt(lprev, cum, sg, ALU.subtract).then_inc(dve_s.at("logs"), 1)
                dve.wait_ge(act_s.sem, act_s.value("a", i))
                ts(kf, av, 1.0, prm[:, K_A:K_A + 1], ALU.subtract, ALU.mult)
                dve.drain()
                stt(out=kf, in0=kf, scalar=1.0, in1=k_s, op0=ALU.add, op1=ALU.mult)
                dve.wait_ge(act_s.sem, act_s.value("norm", i))
                ts(nrm, nrm, 1e-12, None, ALU.max)
                dve.drain()
                dve.reciprocal(nrm, nrm)
                dve.drain()
                stt(out=kk, in0=k_s, scalar=prm[:, K_K:K_K + 1], in1=nrm, op0=ALU.mult, op1=ALU.mult)
                stt(out=rk, in0=r_s, scalar=prm[:, R_K:R_K + 1], in1=kf, op0=ALU.mult, op1=ALU.mult).then_inc(dve_s.at("rk"), 1)
                dve.drain()
                dve.wait_ge(act_s.sem, act_s.value("exps", i))
                stt(out=at, in0=kk, scalar=-1.0, in1=e_prev, op0=ALU.mult, op1=ALU.mult)
                tt(ba, kk, av, ALU.mult)
                tt(kt, kf, e_neg, ALU.mult)
                tt(rt, r_s, e_pos, ALU.mult)
                dve.drain()
                tt(bt, ba, e_neg, ALU.mult).then_inc(dve_s.at("factors"), 1)
                dve.memset(sc_state[0], 0.0)
                dve.wait_ge(pe_s.sem, pe_s.value("bonus", i))
                tt(halves(bon), of_banks(ps, 6), halves(v_s), ALU.mult).then_inc(dve_s.at("bonus"), 1)
                banks = {(0, "G"): 6, (0, "RB"): 7, (0, "RK"): 0, (1, "G"): 3, (1, "RB"): 4, (1, "RK"): 5}
                for e in range(2):
                    for name, dst, mask in (("G", G, K.m_before), ("RB", RB, K.m_upto), ("RK", RK, K.m_upto)):
                        dve.wait_ge(pe_s.sem, pe_s.value(f"gram_{name}{e}", i))
                        tt(dst[:, e], ps[:, banks[e, name], :].rearrange("p (b f) -> p b f", f=P),
                                      unsq(mask, 1, NB), ALU.mult).then_inc(dve_s.at(f"gram{name}{e}"), 1)
                dve.wait_ge(act_s.sem, act_s.value("gram_LT1", i))
                for src, dst, m in ((L, X, lev(0, 0)), (LT, XT, lev(0, 1))):
                    for e in range(2):
                        tt(dst[:, e], src[:, e], unsq(m, 1, NB), ALU.mult)
                dve.drain()
                for dst in (X, XT):
                    for e in range(2):
                        last = tt(dst[:, e], dst[:, e], unsq(K.ident, 1, NB), ALU.add)
                last.then_inc(dve_s.at("level0"), 1)
                for l in range(1, LEVELS):
                    for j, (name, dst) in enumerate((("XT", XT), ("X", X))[::both(l)]):
                        for e in range(2):
                            dve.wait_ge(pe_s.sem, pe_s.value(f"{('dX', 'dXT')[both(l) - 1]}{l}_{e}", i))
                            tt(dst[:, e], dst[:, e],
                                          ps[:, 4 * e + 2 + j, :].rearrange("p (b f) -> p b f", f=P), ALU.add).then_inc(dve_s.at(f"{name}{l}_{e}"), 1)
                for b in range(NB):
                    dve.wait_ge(pe_s.sem, pe_s.value(f"S{b}", i))
                    stt(out=s_tmp, in0=ps[:, 2, 0:P], scalar=esc[:, 2 * NB + b:2 * NB + b + 1], in1=K.headones,
                        op0=ALU.mult, op1=ALU.mult)
                    dve.drain()
                    last = stt(out=state, in0=state, scalar=esc[:, NB + b:NB + b + 1], in1=s_tmp,
                               op0=ALU.mult, op1=ALU.add)
                    if b < NB - 1:
                        dve.drain()
                        last = ts(sc_state[(b + 1) % 2], state, esc[:, b + 1:b + 2], None, ALU.mult)
                    last.then_inc(dve_s.at(f"state{b}"), 1)
                dve.wait_ge(act_s.sem, act_s.value("s_tok", i))
                grams = [ps[0:NS, 5 + e, 0:5 * NS].rearrange("p (j f) -> p j f", f=NS) for e in range(2)]
                for e in range(2):
                    dve.wait_ge(pe_s.sem, pe_s.value(f"s_gram{e}", i))
                    for j, (dst, mask) in enumerate(((sX, lev(0, 0)[0:NS, 0:NS]), (sXT, lev(0, 1)[0:NS, 0:NS]),
                                                     (sG, K.ms_before), (sRB, K.ms_upto), (sRK, K.ms_upto))):
                        tt(dst[:, e, :], grams[e][:, j, :], mask, ALU.mult)
                    dve.tensor_copy(sL[:, e, :], grams[e][:, 0, :])
                    dve.tensor_copy(sLT[:, e, :], grams[e][:, 1, :])
                dve.drain()
                for dst in (sX, sXT):
                    tt(dst, dst, unsq(K.ident[0:NS, 0:NS], 1, 2), ALU.add)
                for l in range(1, SLEVELS):
                    if l > 1:
                        dve.wait_ge(pe_s.sem, pe_s.value(f"s_d{l - 1}", i))
                        tt(sXT, sXT, ps[0:NS, 1, 0:2 * NS].rearrange("p (e f) -> p e f", f=NS), ALU.add)
                        tt(sX, sX, ps[0:NS, 1, 2 * NS:4 * NS].rearrange("p (e f) -> p e f", f=NS), ALU.add)
                    tt(sco, sL, unsq(lev(l, 0)[0:NS, 0:NS], 1, 2), ALU.mult)
                    tt(scoT, sLT, unsq(lev(l, 1)[0:NS, 0:NS], 1, 2), ALU.mult).then_inc(dve_s.at("s_gram" if l == 1 else f"s_X{l - 1}"), 1)
                dve.wait_ge(pe_s.sem, pe_s.value(f"s_d{SLEVELS - 1}", i))
                tt(sXT, sXT, ps[0:NS, 1, 0:2 * NS].rearrange("p (e f) -> p e f", f=NS), ALU.add).then_inc(dve_s.at(f"s_X{SLEVELS - 1}"), 1)
                dve.wait_ge(pe_s.sem, pe_s.value("s_RT", i))
                dve.tensor_copy(rT2, ps[:, 2, NS:2 * NS])
                dve.drain()
                tt(rT, ps[:, 2, 0:NS], rT2, ALU.add).then_inc(dve_s.at("s_RT"), 1)
                dve.wait_ge(act_s.sem, act_s.value("s_U", i))
                tt(v_exp, unsq(stok[:, 2, :], 1, SB), unsq(K.seq_of, 2, P), ALU.mult)
                tt(u_exp, unsq(su_tok, 1, SB), unsq(K.seq_of, 2, P), ALU.mult).then_inc(dve_s.at("s_exp"), 1)
                dve.wait_ge(pe_s.sem, pe_s.value("s_Y", i))
                dve.tensor_copy(y_s[:, T:N], ps[:, 3, 0:NS])
                dve.drain()
                tt(y_s[:, T:N], y_s[:, T:N], ps[:, 3, NS:2 * NS], ALU.add).then_inc(dve_s.at("s_y"), 1)
                dve.wait_ge(pe_s.sem, pe_s.value("s_S", i))
                for h in range(2):
                    hb = slice(4 * h, 4 * h + 4)
                    tt(s_prod[:, hb, :], ps[:, 6 + h, :].rearrange("p (b f) -> p b f", f=P), unsq(K.headones, 1, 4), ALU.mult)
                dve.drain()
                tt(s_state, s_state, s_prod, ALU.add)
                dve.drain()
                tt(s_state, s_state, unsq(esc[:, 3 * NB:3 * NB + SB], 2, P), ALU.mult).then_inc(dve_s.at("s_state"), 1)
                dve.wait_ge(pe_s.sem, pe_s.value("mean", i))
                stt(out=halves(yc), in0=of_banks(ps, 0), scalar=-1.0 / HD, in1=halves(y_s),
                               op0=ALU.mult, op1=ALU.add).then_inc(dve_s.at("yc"), 1)
                dve.wait_ge(act_s.sem, act_s.value("sd", i))
                dve.reciprocal(sd, sd)
                dve.drain()
                tt(yc, yc, sd, ALU.mult)
                dve.drain()
                ts(yc, yc, prm[:, LN_W:LN_W + 1], prm[:, LN_B:LN_B + 1], ALU.mult, ALU.add)
                dve.drain()
                tt(yc, yc, bon, ALU.add)
                dve.drain()
                tt(y_out[:, bass.ds(i, 1), :].squeeze(1), yc, g_s, ALU.mult).then_inc(dve_s.at("y"), 1)

        @block.gpsimd
        def _(pool):
            with pool.Fori(0, C) as i:
                pool.wait_ge(act_s.sem, act_s.value("gram_LT1", i))
                for l in range(1, LEVELS):
                    for e in range(2):
                        for name, dst, src, t in (("co", co, L, 0), ("coT", coT, LT, 1))[::both(l)]:
                            if l > 1:
                                pool.wait_ge(pe_s.sem, pe_s.value(f"{('y1', 'y2')[t]}{l - 1}_{e}", i))
                            pool.tensor_tensor(dst[e], src[:, e], unsq(lev(l, t), 1, NB), ALU.mult).then_inc(pool_s.at(f"{name}{l}_{e}"), 1)


def token_major(nc, K, src, dst):
    n = K.name()
    pe_s = Steps(K.sem(f"{n}_pe"), [f"turned{b}" for b in range(NB + 1)])
    act_s = Steps(K.sem(f"{n}_act"), [f"copied{b}" for b in range(NB + 1)])
    with nc.Block() as block:
        @block.tensor
        def _(pe):
            for b in range(NB + 1):
                m = P if b < NB else NS
                if b >= 2:
                    pe.wait_ge(act_s.sem, act_s.value(f"copied{b - 2}"))
                for c in range(C):
                    last = pe.transpose(K.ps[0:m, 2 * (b % 2) + c // 4, (c % 4) * P:(c % 4 + 1) * P],
                                        src[:, c, b * P:b * P + m], K.ident)
                last.then_inc(pe_s.at(f"turned{b}"), 1)

        @block.scalar
        def _(act):
            for b in range(NB + 1):
                m = P if b < NB else NS
                act.wait_ge(pe_s.sem, pe_s.value(f"turned{b}"))
                act.activation(dst[0:m, b, :].rearrange("p (a b) -> p a b", a=2),
                                          K.ps[0:m, 2 * (b % 2):2 * (b % 2) + 2, :], ACT.Copy).then_inc(act_s.at(f"copied{b}"), 1)


def add_token_major(nc, K, acc):
    n = K.name()
    pe_s = Steps(K.sem(f"{n}_pe"), [f"turned{b}" for b in range(NB + 1)])
    dve_s = Steps(K.sem(f"{n}_dve"), [f"added{b}" for b in range(NB + 1)])
    with nc.Block() as block:
        @block.tensor
        def _(pe):
            for b in range(NB + 1):
                m = P if b < NB else NS
                if b >= 2:
                    pe.wait_ge(dve_s.sem, dve_s.value(f"added{b - 2}"))
                for c in range(C):
                    last = pe.transpose(K.ps[:, 2 * (b % 2) + c // 4, (c % 4) * P:(c % 4) * P + m],
                                        acc[0:m, b, c * P:(c + 1) * P], K.ident[0:m, 0:m])
                last.then_inc(pe_s.at(f"turned{b}"), 1)

        @block.vector
        def _(dve):
            for b in range(NB + 1):
                m = P if b < NB else NS
                dve.wait_ge(pe_s.sem, pe_s.value(f"turned{b}"))
                for h in range(2):
                    dst = K.x[:, 4 * h:4 * h + 4, b * P:b * P + m]
                    last = dve.tensor_tensor(dst, dst, K.ps[:, 2 * (b % 2) + h, :].rearrange(
                        "p (c t) -> p c t", t=P)[:, :, 0:m], ALU.add)
                last.then_inc(dve_s.at(f"added{b}"), 1)


def peer(nc, K, I, layer, h, h_tok, acc, R):
    n = f"peer{layer}"
    RING, DIAGS = 8, 4
    NU = NB + 1
    rows = [P] * NB + [NS]
    uring, vring = R.cut(RING, D), R.cut(RING, D)
    diag = R.cut(DIAGS, P)
    q_sb, s_sb = R.cut(2, N), R.cut(NU, 2 * NKEYS)
    swork = R.cut(NKEYS)
    top_v, top_i = R.cut(2, TOPK), R.cut(2, TOPK, dtype=U32)
    top_f = R.cut(2, TOPK)
    cand, cwork = R.cut(TOPK * TOPK), R.cut(TOPK * TOPK)
    best_v, best_p = R.cut(NU, TOPK), R.cut(TOPK, dtype=U32)
    pos_u, pos_f = R.cut(2, TOPK, dtype=U32), R.cut(2, TOPK)
    hit = R.cut(2, TOPK, TOPK)
    part = R.cut(2, TOPK)
    idx_f, idx_next = R.cut(TOPK), R.cut(NU, TOPK, dtype=U32)
    idx = R.cut(NU, TOPK, dtype=U32)
    neg_max, gate, gate_sum = R.cut(NU), R.cut(NU, TOPK), R.cut(NU)
    dots, gelu, coef = R.cut(TOPK), R.cut(TOPK), R.cut(TOPK)
    spare = R.cut(2)

    wl = [K.sem(f"{n}_w{j}") for j in range(2)]
    u_here = [K.sem(f"{n}_u_here{j}") for j in range(RING)]
    v_here = [K.sem(f"{n}_v_here{j}") for j in range(RING)]
    u_free, v_free = K.sem(f"{n}_u_free"), K.sem(f"{n}_v_free")
    index_ready, keys_used, diag_ready = K.sem(f"{n}_index"), K.sem(f"{n}_keys"), K.sem(f"{n}_diag")
    query = ["q0", "q1", "s0", "s1", "s2"]
    pe_names = (query, [f"v{b}" for b in range(NU)])
    act_names = (query + [f"exp{b}" for b in range(NU)], [f"gelu{b}" for b in range(NU)])
    dve_names = ([f"top{b}" for b in range(NU)], [x for b in range(NU) for x in (f"coef{b}", f"acc{b}")])

    def passes(sem, names, order):
        first, both = Steps(sem, names[0]), Steps(sem, order, start=len(names[0]))
        last = Steps(sem, names[1], start=len(names[0]) + (HEADS - 1) * len(order))
        return first, both, last

    pe_p = passes(K.sem(f"{n}_pe"), pe_names, pe_names[0] + pe_names[1])
    act_p = passes(K.sem(f"{n}_act"), act_names, query + [x for b in range(NU) for x in (f"gelu{b}", f"exp{b}")])
    dve_p = passes(K.sem(f"{n}_dve"), dve_names, [x for b in range(NU) for x in (f"coef{b}", f"top{b}", f"acc{b}")])
    s_bank = ((6, 0, 2), (7, 2, 2), (2, 4, 1))
    ps = K.ps

    with nc.Block() as block:
        @block.sync
        def _(sp):
            for j in range(2):
                sp.dma_start(K.w9[j], I["w_q"][layer, j]).then_inc(wl[j], 16)
            with sp.Fori(1, HEADS) as i:
                sp.wait_ge(keys_used, i)
                for j in range(2):
                    sp.dma_start(K.w9[j], I["w_q"][layer, bass.ds(i * 2 + j, 1)].squeeze(0)).then_inc(wl[j], 16)

        @block.gpsimd
        def _(pool):
            pool.memset(spare[:, 0:1], 0.0).then_inc(u_free, RING)
            pool.memset(spare[:, 1:2], 0.0).then_inc(v_free, RING)
            with pool.Fori(0, HEADS) as i:
                for b in range(NU):
                    m = rows[b]
                    pool.wait_ge(index_ready, i * NU + (b + 1))
                    for ring, here, free, table in ((uring, u_here, u_free, I["u"][layer]),
                                                    (vring, v_here, v_free, I["v"][layer])):
                        for j in range(TOPK):
                            pool.wait_ge(free, i * (NU * TOPK) + (b * TOPK + j + 1))
                            pool.nop(nofuse=True)
                            pool.indirect_dma_start(ring[0:m, j % RING, :], None, table,
                                                    bass.IndirectOffsetOnAxis(ap=idx[0:m, b, j:j + 1], axis=0)
                                                    ).then_inc(here[j % RING], 16)

        @block.tensor
        def _(pe):
            def choose(S, A, i, head):
                for j in range(2):
                    pe.wait_ge(wl[j], head * 16 + 16)
                    for s in range(2):
                        for k in range(C):
                            last = pe.matmul(ps[:, 2 + 2 * j + s, 0:HALF], K.w9[j][:, k, :],
                                             h[:, k, s * HALF:(s + 1) * HALF], start=k == 0, stop=k == C - 1)
                    last.then_inc(S.at(f"q{j}"), 1)
                pe.wait_ge(A.sem, A.value("q1", i))
                for g, (bank, b0, nb) in enumerate(s_bank):
                    for b in range(b0, b0 + nb):
                        m = rows[b]
                        for j in range(2):
                            col = ((b - b0) * 2 + j) * NKEYS
                            last = pe.matmul(ps[0:m, bank, col:col + NKEYS], q_sb[:, j, b * P:b * P + m],
                                             K.w9[j][:, C, :], start=True, stop=True)
                    if g == 2:
                        last.then_inc(keys_used, 1)
                        last = pe.drain()
                    last.then_inc(S.at(f"s{g}"), 1)

            def combine(S, i):
                for b in range(NU):
                    m = rows[b]
                    for j in range(TOPK):
                        pe.wait_ge(diag_ready, i * (NU * TOPK) + (b * TOPK + j + 1))
                        pe.wait_ge(v_here[j % RING], i * (2 * NU * 16) + (2 * b + j // RING + 1) * 16)
                        if m < P:
                            pe.nop(nofuse=True)
                        for s in range(2):
                            last = pe.matmul(ps[0:m, s, :], diag[0:m, j % DIAGS, 0:m],
                                             vring[0:m, j % RING, s * 512:(s + 1) * 512],
                                             start=j == 0, stop=j == TOPK - 1)
                        last.then_inc(v_free, 1)
                        if j == TOPK - 1:
                            pe.drain().then_inc(S.at(f"v{b}"), 1)

            choose(pe_p[0], act_p[0], 0, 0)
            with pe.Fori(0, HEADS - 1) as i:
                pe.wait_ge(dve_p[1].sem, dve_p[1].all_before(i))
                pe.wait_ge(act_p[1].sem, act_p[1].all_before(i))
                choose(pe_p[1], act_p[1], i, i + 1)
                combine(pe_p[1], i)
            combine(pe_p[2], HEADS - 1)

        @block.scalar
        def _(act):
            def choose(S, Q, i):
                for j in range(2):
                    act.wait_ge(Q.sem, Q.value(f"q{j}", i))
                    act.activation(halves(q_sb[:, j, :]), of_banks(ps, 2 + 2 * j), ACT.Copy).then_inc(S.at(f"q{j}"), 1)
                for g, (bank, b0, nb) in enumerate(s_bank):
                    m = rows[b0]
                    act.wait_ge(Q.sem, Q.value(f"s{g}", i))
                    act.activation(s_sb[0:m, b0:b0 + nb, :], ps[0:m, bank, 0:nb * 2 * NKEYS].rearrange(
                        "p (b f) -> p b f", b=nb), ACT.Copy).then_inc(S.at(f"s{g}"), 1)

            def softmax(S, V, i, b):
                m = rows[b]
                act.wait_ge(V.sem, V.value(f"top{b}", i))
                act.activation(gate[0:m, b, :], best_v[0:m, b, :], ACT.Exp, bias=neg_max[0:m, b:b + 1],
                                      accum_out=gate_sum[0:m, b:b + 1]).then_inc(S.at(f"exp{b}"), 1)

            def experts(S, V, i, a, b):
                m = rows[b]
                act.wait_ge(V.sem, V.value(f"coef{b}", a))
                for j in range(TOPK):
                    act.wait_ge(v_free, i * (NU * TOPK) + (b * TOPK + j + 1 + RING - DIAGS))
                    act.activation(diag[0:m, j % DIAGS, 0:m], K.ident[0:m, 0:m], ACT.Copy,
                                   scale=coef[0:m, j:j + 1]).then_inc(diag_ready, 1)

            def activate(S, b, i):
                m = rows[b]
                act.wait_ge(u_free, i * (NU * TOPK) + ((b + 1) * TOPK + RING))
                act.activation(gelu[0:m, :], dots[0:m, :], ACT.Gelu).then_inc(S.at(f"gelu{b}"), 1)

            choose(act_p[0], pe_p[0], 0)
            for b in range(NU):
                softmax(act_p[0], dve_p[0], 0, b)
            with act.Fori(0, HEADS - 1) as i:
                act.wait_ge(dve_p[1].sem, dve_p[1].all_before(i))
                choose(act_p[1], pe_p[1], i)
                for b in range(NU):
                    activate(act_p[1], b, i)
                    experts(act_p[1], dve_p[1], i, i, b)
                    softmax(act_p[1], dve_p[1], i, b)
            for b in range(NU):
                activate(act_p[2], b, HEADS - 1)
                experts(act_p[2], dve_p[2], HEADS - 1, 0, b)

        @block.vector
        def _(dve):
            tt, ts, stt = dve.tensor_tensor, dve.tensor_scalar, dve.scalar_tensor_tensor

            def top16(values, work, out_v, out_i):
                dve.max(out_v[:, 0:8], values)
                dve.drain()
                dve.max_index(out_i[:, 0:8], out_v[:, 0:8], values)
                dve.match_replace(out=work, in_to_replace=out_v[:, 0:8], in_values=values, imm_value=LOWEST)
                dve.drain()
                dve.max(out_v[:, 8:16], work)
                dve.drain()
                dve.max_index(out_i[:, 8:16], out_v[:, 8:16], work)

            def choose(S, A, i, b, g):
                m = rows[b]
                dve.wait_ge(A.sem, A.value(f"s{g}", i))
                dve.nop(nofuse=True)
                for j in range(2):
                    top16(s_sb[0:m, b, j * NKEYS:(j + 1) * NKEYS], swork[0:m], top_v[0:m, j, :], top_i[0:m, j, :])
                    dve.drain()
                dve.tensor_copy(top_f[0:m], top_i[0:m])
                tt(cand[0:m].rearrange("p (a b) -> p a b", b=TOPK), unsq(top_v[0:m, 0, :], 2, TOPK),
                   unsq(top_v[0:m, 1, :], 1, TOPK), ALU.add)
                dve.drain()
                top16(cand[0:m], cwork[0:m], best_v[0:m, b, :], best_p[0:m])
                dve.drain()
                ts(neg_max[0:m, b:b + 1], best_v[0:m, b, 0:1], -1.0, None, ALU.mult).then_inc(S.at(f"top{b}"), 1)
                ts(pos_u[0:m, 0, :], best_p[0:m], 4, None, ALU.logical_shift_right)
                ts(pos_u[0:m, 1, :], best_p[0:m], TOPK - 1, None, ALU.bitwise_and)
                dve.drain()
                dve.tensor_copy(pos_f[0:m], pos_u[0:m])
                dve.drain()
                for j in range(2):
                    tt(hit[0:m, j], unsq(pos_f[0:m, j, :], 2, TOPK), unsq(K.iota[0:m], 1, TOPK), ALU.is_equal)
                dve.drain()
                for j in range(2):
                    tt(hit[0:m, j], hit[0:m, j], unsq(top_f[0:m, j, :], 1, TOPK), ALU.mult)
                dve.drain()
                dve.tensor_reduce(out=part[0:m], in_=hit[0:m], op=ALU.add, axis=AX.X)
                dve.drain()
                stt(out=idx_f[0:m], in0=part[0:m, 0, :], scalar=float(NKEYS), in1=part[0:m, 1, :],
                    op0=ALU.mult, op1=ALU.add)
                dve.drain()
                dve.tensor_copy(idx_next[0:m, b, :], idx_f[0:m])
                dve.wait_ge(A.sem, A.value(f"exp{b}", i))
                dve.reciprocal(gate_sum[0:m, b:b + 1], gate_sum[0:m, b:b + 1])
                dve.drain()
                ts(gate[0:m, b, :], gate[0:m, b, :], gate_sum[0:m, b:b + 1], None, ALU.mult)
                dve.drain()

            def publish(b):
                m = rows[b]
                dve.tensor_copy(idx[0:m, b, :], idx_next[0:m, b, :]).then_inc(index_ready, 1)

            def dot(S, A, i, a, b):
                m = rows[b]
                for j in range(TOPK):
                    dve.wait_ge(u_here[j % RING], i * (2 * NU * 16) + (2 * b + j // RING + 1) * 16)
                    row = uring[0:m, j % RING, :]
                    stt(out=row, in0=row, scalar=1.0, in1=h_tok[0:m, b, :], op0=ALU.mult, op1=ALU.mult,
                        accum_out=dots[0:m, j:j + 1]).then_inc(u_free, 1)
                dve.wait_ge(A.sem, A.value(f"gelu{b}", a))
                tt(coef[0:m], gelu[0:m], gate[0:m, b, :], ALU.mult).then_inc(S.at(f"coef{b}"), 1)
                dve.drain()

            def add(S, Q, i, b):
                m = rows[b]
                dve.wait_ge(Q.sem, Q.value(f"v{b}", i))
                dst = acc[0:m, b, :].rearrange("p (a b) -> p a b", a=2)
                return tt(dst, dst, ps[0:m, 0:2, :], ALU.add)

            dve.memset(acc, 0.0)
            group = [g for g, (_, _, nb) in enumerate(s_bank) for _ in range(nb)]
            for b in range(NU):
                choose(dve_p[0], act_p[0], 0, b, group[b])
                publish(b)
            with dve.Fori(0, HEADS - 1) as i:
                for b in range(NU):
                    dot(dve_p[1], act_p[1], i, i, b)
                    choose(dve_p[1], act_p[1], i, b, group[b])
                    add(dve_p[1], pe_p[1], i, b).then_inc(dve_p[1].at(f"acc{b}"), 1)
                    publish(b)
            for b in range(NU):
                dot(dve_p[2], act_p[2], HEADS - 1, 0, b)
                add(dve_p[2], pe_p[2], 0, b).then_inc(dve_p[2].at(f"acc{b}"), 1)


def conv(nc, K, I, h, cv, R):
    PE_TAPS = 16
    up, us = R.cut(PAST + T), R.cut(SB, PAST + ST)
    sg, prm, diags = R.cut(N), R.cut(NPAR), R.cut(PE_TAPS, P)
    wl = [K.sem(f"conv_w{j}") for j in range(2)]
    small, stored, zeroed = K.sem("conv_small"), K.sem("conv_stored"), K.sem("conv_zeroed")
    pe_s = Steps(K.sem("conv_pe"), ["a", "g", "taps"], start=1)
    act_s = Steps(K.sem("conv_act"), ["gate", "diags"], start=1)
    dve_s = Steps(K.sem("conv_dve"), ["u", "sum"], start=1)
    ps = K.ps
    with nc.Block() as block:
        @block.sync
        def _(sp):
            sp.sem_inc(stored, 16)
            sp.wait_ge(zeroed, 1)
            with sp.Fori(0, C) as i:
                sp.wait_ge(pe_s.sem, pe_s.all_before(i))
                for j in range(2):
                    sp.dma_start(K.w[j], I["w_pw1"][bass.ds(i * 2 + j, 1)].squeeze(0)).then_inc(wl[j], 16)
                sp.wait_ge(dve_s.sem, dve_s.all_before(i))
                sp.wait_ge(act_s.sem, act_s.all_before(i))
                sp.wait_ge(stored, i * 32 + 16)
                sp.dma_start(prm, I["cpar"][bass.ds(i, 1)].squeeze(0)).then_inc(small, 16)
                sp.dma_start(us[:, :, 0:PAST], I["state_conv"][bass.ds(i, 1)].squeeze(0)).then_inc(small, 16)
                sp.wait_ge(dve_s.sem, dve_s.value("u", i))
                sp.dma_start(I["o_conv_p"][bass.ds(i, 1)].squeeze(0), up[:, T:T + PAST]).then_inc(stored, 16)
                sp.dma_start(I["o_conv_s"][bass.ds(i, 1)].squeeze(0), us[:, :, ST:ST + PAST]).then_inc(stored, 16)
            sp.wait_ge(stored, C * 32 + 16)

        @block.tensor
        def _(pe):
            pe_s.begin(pe)
            with pe.Fori(0, C) as i:
                pe.wait_ge(dve_s.sem, dve_s.all_before(i))
                for j, name in enumerate(("a", "g")):
                    pe.wait_ge(wl[j], i * 16 + 16)
                    for s in range(2):
                        for k in range(C):
                            last = pe.matmul(ps[:, 2 * j + s, 0:HALF], K.w[j][:, k, :], h[:, k, s * HALF:(s + 1) * HALF],
                                             start=k == 0, stop=k == C - 1)
                    last.then_inc(pe_s.at(name), 1)
                pe.wait_ge(act_s.sem, act_s.value("diags", i))
                pe.wait_ge(dve_s.sem, dve_s.value("u", i))
                for k in range(PE_TAPS):
                    pe.matmul(ps[:, 4, :], diags[:, k, :], up[:, k:k + T], start=k == 0, stop=k == PE_TAPS - 1)
                    last = pe.matmul(ps[:, 5, 0:NS], diags[:, k, :], us[:, :, k:k + ST], start=k == 0, stop=k == PE_TAPS - 1)
                last.then_inc(pe_s.at("taps"), 1)

        @block.scalar
        def _(act):
            act_s.begin(act)
            with act.Fori(0, C) as i:
                act.wait_ge(small, i * 32 + 32)
                act.wait_ge(dve_s.sem, dve_s.all_before(i))
                act.wait_ge(pe_s.sem, pe_s.value("g", i))
                act.activation(halves(sg), of_banks(ps, 2), ACT.Sigmoid, bias=prm[:, B_PG:B_PG + 1]).then_inc(act_s.at("gate"), 1)
                for k in range(PE_TAPS):
                    last = act.activation(diags[:, k, :], K.ident, ACT.Copy, scale=prm[:, TAP0 + k:TAP0 + k + 1])
                last.then_inc(act_s.at("diags"), 1)

        @block.vector
        def _(dve):
            dve_s.begin(dve)
            stt = dve.scalar_tensor_tensor
            dve.memset(up[:, 0:PAST], 0.0).then_inc(zeroed, 1)
            with dve.Fori(0, C) as i:
                dve.wait_ge(small, i * 32 + 32)
                dve.wait_ge(stored, i * 32 + 16)
                dve.wait_ge(pe_s.sem, pe_s.all_before(i))
                dve.wait_ge(act_s.sem, act_s.value("gate", i))
                one = dict(scalar=prm[:, B_PA:B_PA + 1], op0=ALU.add, op1=ALU.mult)
                stt(out=up[:, PAST:PAST + HALF], in0=ps[:, 0, 0:HALF], in1=sg[:, 0:HALF], **one)
                stt(out=up[:, PAST + HALF:], in0=ps[:, 1, 0:T - HALF], in1=sg[:, HALF:T], **one)
                stt(out=us[:, :, PAST:], in0=ps[:, 1, T - HALF:HALF].rearrange("p (b t) -> p b t", t=ST),
                               in1=sg[:, T:N].rearrange("p (b t) -> p b t", t=ST), **one).then_inc(dve_s.at("u"), 1)
                dve.drain()
                outp = cv[:, bass.ds(i, 1), 0:T].squeeze(1)
                outs = cv[:, bass.ds(i, 1), T:N].squeeze(1).rearrange("p (b t) -> p b t", t=ST)
                for k in range(PE_TAPS, TAPS):
                    w = prm[:, TAP0 + k:TAP0 + k + 1]
                    for o, u in ((outp, up[:, k:k + T]), (outs, us[:, :, k:k + ST])):
                        if k == PE_TAPS:
                            dve.tensor_scalar(o, u, w, prm[:, B_DW:B_DW + 1], ALU.mult, ALU.add)
                        else:
                            stt(out=o, in0=u, scalar=w, in1=o, op0=ALU.mult, op1=ALU.add)
                    dve.drain()
                dve.wait_ge(pe_s.sem, pe_s.value("taps", i))
                dve.tensor_tensor(outp, outp, ps[:, 4, :], ALU.add)
                dve.tensor_tensor(outs, outs, ps[:, 5, 0:NS].rearrange("p (b t) -> p b t", t=ST), ALU.add).then_inc(dve_s.at("sum"), 1)


def layernorm_silu(nc, K, v, w):
    act_s = Steps(K.sem("ln_act"), [f"square{c}" for c in range(C)] + ["root"])
    pe_s = Steps(K.sem("ln_pe"), ["sum"] + [f"summed{c}" for c in range(C)])
    dve_s = Steps(K.sem("ln_dve"), [f"centred{c}" for c in range(C)] + [f"scaled{c}" for c in range(C)])
    sq = [K.small[:, 0:N], K.small[:, N:2 * N]]
    mean, root = K.small[:, 2 * N:3 * N], K.small[:, 3 * N:4 * N]
    with nc.Block() as block:
        @block.tensor
        def _(pe):
            for h in range(2):
                for c in range(C):
                    last = pe.matmul(K.ps[:, h, 0:HALF], K.ones, v[:, c, h * HALF:(h + 1) * HALF],
                                     start=c == 0, stop=c == C - 1)
            last.then_inc(pe_s.at("sum"), 1)
            for c in range(C):
                pe.wait_ge(act_s.sem, act_s.value(f"square{c}"))
                for h in range(2):
                    last = pe.matmul(K.ps[:, 2 + h, 0:HALF], K.ones, sq[c % 2][:, h * HALF:(h + 1) * HALF],
                                     start=c == 0, stop=c == C - 1)
                last.then_inc(pe_s.at(f"summed{c}"), 1)

        @block.vector
        def _(dve):
            dve.wait_ge(pe_s.sem, pe_s.value("sum"))
            dve.tensor_scalar(halves(mean), of_banks(K.ps, 0), 1.0 / D, None, ALU.mult)
            dve.drain()
            for c in range(C):
                dve.tensor_tensor(v[:, c, :], v[:, c, :], mean, ALU.subtract).then_inc(dve_s.at(f"centred{c}"), 1)
            dve.wait_ge(act_s.sem, act_s.value("root"))
            dve.reciprocal(root, root)
            dve.drain()
            for c in range(C):
                dve.tensor_tensor(v[:, c, :], v[:, c, :], root, ALU.mult).then_inc(dve_s.at(f"scaled{c}"), 1)

        @block.scalar
        def _(act):
            for c in range(C):
                act.wait_ge(dve_s.sem, dve_s.value(f"centred{c}"))
                if c >= 2:
                    act.wait_ge(pe_s.sem, pe_s.value(f"summed{c - 2}"))
                act.activation(sq[c % 2], v[:, c, :], ACT.Square).then_inc(act_s.at(f"square{c}"), 1)
            act.wait_ge(pe_s.sem, pe_s.value(f"summed{C - 1}"))
            act.activation(halves(root), of_banks(K.ps, 2), ACT.Sqrt, bias=K.eps[:, 2:3], scale=1.0 / D).then_inc(act_s.at("root"), 1)
            for c in range(C):
                act.wait_ge(dve_s.sem, dve_s.value(f"scaled{c}"))
                act.activation(v[:, c, :], v[:, c, :], ACT.Silu, bias=K.par[:, CLN_B, c:c + 1],
                               scale=K.par[:, CLN_G, c:c + 1])


class Kernel:

    def __init__(self, nc, ctx):
        self.nc, self.ctx, self.phases = nc, ctx, 0
        sb = lambda name, shape: ctx.enter_context(nc.sbuf_tensor(name, shape, F32))[tuple(slice(None) for _ in shape)]
        self.x = sb("x", [P, C, N])
        self.par = sb("par", [P, NPAR, C])
        self.cst = sb("cst", [P, CST_COLS])
        self.level = sb("level", [P, 2 * LEVELS, P])
        self.wbuf = sb("wbuf", [P, 3 * (C + 1), P])
        self.eps = sb("eps", [P, 3])
        self.bias_cols = sb("bias_cols", [P, 2])
        self.arena = sb("arena", [P, ARENA])
        self.ps = ctx.enter_context(nc.psum_tensor("psum", [P, 8, 512], F32))[:, :, :]
        cut = Region(self.cst)
        self.ident, self.ones, self.headones = cut.cut(P), cut.cut(P), cut.cut(P)
        self.m_before, self.m_upto = cut.cut(P), cut.cut(P)
        self.ms_before, self.ms_upto = cut.cut(NS, parts=NS), cut.cut(NS, parts=NS)
        self.seq_of, self.iota, self.reset = cut.cut(SB, parts=NS), cut.cut(TOPK), cut.cut(N)
        self.w9 = [self.wbuf[:, j * (C + 1):(j + 1) * (C + 1), :] for j in range(3)]
        self.w = [w[:, 0:C, :] for w in self.w9]

    def sem(self, name):
        return self.ctx.enter_context(self.nc.semaphore(name))

    def name(self):
        self.phases += 1
        return f"phase{self.phases}"


ARENA = 41450
CST_COLS = 5 * P + 2 * NS + SB + TOPK + N


def build(nc, I):
    with ExitStack() as ctx:
        K = Kernel(nc, ctx)
        base = C * N
        h = Region(K.arena, 0).cut(C, N)
        work = base
        K.small = K.arena[:, ARENA - 4 * N:ARENA]
        load_constants(nc, K, I)

        rmsnorm(nc, K, NMIX0, h)
        R = Region(K.arena, work)
        xm = [R.cut(C, N) for _ in range(3)]
        hid_wa, hid_g = R.cut(N), R.cut(N)
        X = Region(K.arena, R.at)
        xx = X.cut(C, N)
        K.low, K.shift, K.new_shift = X.cut(C, 2 * P), X.cut(C, SB), X.cut(C, 1 + SB)
        time_mix_inputs(nc, K, I, h, xx, xm, hid_wa, hid_g)
        wkv(nc, K, I, xm, h, hid_wa, hid_g, R)
        linear_into_x(nc, K, I["w_o"], h)

        for layer, gain in ((0, NFFN0), (1, NFFN1)):
            if layer == 1:
                rmsnorm(nc, K, NMIX1, h)
                R = Region(K.arena, work)
                cv = R.cut(C, N)
                conv(nc, K, I, h, cv, R)
                layernorm_silu(nc, K, cv, None)
                linear_into_x(nc, K, I["w_pw2"], cv, bias=B_P2)
            rmsnorm(nc, K, gain, h)
            R = Region(K.arena, work)
            h_tok, acc = R.cut(NB + 1, D), R.cut(NB + 1, D)
            token_major(nc, K, h, h_tok)
            peer(nc, K, I, layer, h, h_tok, acc, R)
            add_token_major(nc, K, acc)
        rmsnorm(nc, K, NFIN, h, store=I["o_y"])


def constants():
    t, s = np.arange(P)[:, None], np.arange(P)[None, :]
    levels = []
    for l in range(LEVELS):
        m = ((t >> (l + 1)) == (s >> (l + 1))) & ((t >> l) % 2 == 1) & ((s >> l) % 2 == 0)
        levels += [m, m.T]
    tn, sn = np.arange(NS)[:, None], np.arange(NS)[None, :]
    same = (tn // ST) == (sn // ST)
    reset = np.ones(N)
    reset[0:T:P] = 0
    reset[T::ST] = 0
    parts = [np.eye(P), np.ones((P, P)), (t // HD) == (s // HD), t < s, t <= s,
             np.pad(same & (tn < sn), ((0, P - NS), (0, 0))), np.pad(same & (tn <= sn), ((0, P - NS), (0, 0))),
             np.pad((tn // ST) == np.arange(SB)[None, :], ((0, P - NS), (0, 0))),
             np.broadcast_to(np.arange(TOPK), (P, TOPK)), np.broadcast_to(reset, (P, N))]
    cst = np.concatenate([np.asarray(p, np.float32) for p in parts], axis=1)
    return cst, np.stack([np.asarray(m, np.float32) for m in levels], axis=1)


def kernel(**inputs):
    import concourse.bacc as bacc
    from concourse.bass_utils import run_bass_kernel_spmd

    a = {k: np.asarray(v) for k, v in inputs.items()}
    con = np.ascontiguousarray

    def chunks(w):
        return con(w.reshape(C, P, -1, P).transpose(2, 1, 0, 3))

    def feature_major(rows):
        return con(rows.reshape(-1, C, P).transpose(2, 1, 0))

    rows = [*a["rwkv_mu"][0], a["rwkv_w0"][0], a["rwkv_a0"][0], a["rwkv_k_k"][0], a["rwkv_k_a"][0],
            a["rwkv_r_k"][0].reshape(-1), a["rwkv_ln_w"][0], a["rwkv_ln_b"][0],
            a["conv_b_pw1"][0, :D], a["conv_b_pw1"][0, D:], a["conv_b_dw"][0], a["conv_ln_g"][0], a["conv_ln_b"][0],
            a["conv_b_pw2"][0], a["norm_mix"][0], a["norm_mix"][1], a["norm_ffn"][0], a["norm_ffn"][1],
            a["norm_final"], *a["conv_w_dw"][0]]
    par = np.stack(rows).reshape(NPAR, C, P)
    cst, level = constants()
    r, k, v = (chunks(a["rwkv_w_rkv"][0, j]) for j in range(3))
    low1 = np.concatenate([a["rwkv_w1"][0], a["rwkv_a1"][0], a["rwkv_g1"][0]], axis=1)
    low2 = np.concatenate([a["rwkv_w2"][0], a["rwkv_a2"][0], a["rwkv_g2"][0]], axis=0)
    pa, pg = chunks(a["conv_w_pw1"][0][:, :D]), chunks(a["conv_w_pw1"][0][:, D:])
    wq = []
    for j in range(2):
        keys = a["peer_sub_keys"][j].reshape(2 * HEADS, NKEYS, P).transpose(0, 2, 1)
        wq.append(np.concatenate([chunks(a["peer_w_q"][j]), keys[:, :, None, :]], axis=2))
    arrays = {
        "x": feature_major(np.concatenate([a["x_prompt"][0], a["x_sample"].reshape(NS, D)])),
        "par": con(par.transpose(2, 0, 1)),
        "cpar": con(par.transpose(1, 2, 0)),
        "cst": cst, "level": level,
        "shift": con(a["state_shift"][0].reshape(SB, C, P).transpose(2, 1, 0)),
        "low1": con(low1.reshape(C, P, 2 * P).transpose(1, 0, 2)),
        "low2": con(low2.reshape(2, P, C, P).transpose(2, 1, 0, 3)),
        "w_rkv": con(np.stack([r, k, v], axis=1).reshape(3 * C, P, C, P)),
        "w_o": chunks(a["rwkv_w_o"][0]),
        "w_pw1": con(np.stack([pa, pg], axis=1).reshape(2 * C, P, C, P)),
        "w_pw2": chunks(a["conv_w_pw2"][0]),
        "w_q": con(np.stack(wq)),
        "state": con(a["state_wkv"][0].reshape(SB, C, 2, HD, HD).transpose(1, 2, 4, 0, 3).reshape(C, P, SB, HD)),
        "state_conv": con(a["state_conv"][0].reshape(SB, PAST, C, P).transpose(2, 3, 0, 1)),
        "u0": a["peer_u"][0], "u1": a["peer_u"][1], "v0": a["peer_v"][0], "v1": a["peer_v"][1],
    }
    outs = {"o_y": (P, C, N), "o_shift": (P, C, 1 + SB), "o_wkv_p": (C, P, HD), "o_wkv_s": (C, P, SB, HD),
            "o_conv_p": (C, P, PAST), "o_conv_s": (C, P, SB, PAST)}
    nc = bacc.Bacc("TRN2", target_bir_lowering=False, num_devices=1)
    I = {k: nc.dram_tensor(f"in_{k}", v.shape, F32, kind="ExternalInput").ap() for k, v in arrays.items()}
    I |= {k: nc.dram_tensor(f"out_{k}", s, F32, kind="ExternalOutput").ap() for k, s in outs.items()}
    I["u"], I["v"] = (I["u0"], I["u1"]), (I["v0"], I["v1"])
    build(nc, I)
    got = run_bass_kernel_spmd(nc, [{f"in_{k}": con(v) for k, v in arrays.items()}], core_ids=[0]).results[0]
    y, shift, wp, ws, cp, cs = (np.asarray(got[f"out_{k}"]) for k in outs)
    tokens = y.transpose(2, 1, 0).reshape(N, D)
    rows_of = lambda s: s.transpose(2, 1, 0).reshape(-1, D)

    def states(w, b):
        return con(w.reshape(C, 2, HD, b, HD).transpose(3, 0, 1, 4, 2).reshape(1, b, 2 * C, HD, HD))

    return (con(tokens[:T])[None], con(tokens[T:]).reshape(SB, ST, D),
            states(wp, 1), con(rows_of(shift[:, :, 0:1]))[None],
            con(cp.transpose(2, 0, 1).reshape(1, 1, PAST, D)),
            states(ws, SB), con(rows_of(shift[:, :, 1:]))[None],
            con(cs.transpose(2, 3, 0, 1).reshape(1, SB, PAST, D)))
```

```python
import concourse.bass as bass
from concourse import mybir
from contextlib import ExitStack
import numpy as np

F32 = mybir.dt.float32
U32 = mybir.dt.uint32
ALU = mybir.AluOpType
ACT = mybir.ActivationFunctionType
AX = mybir.AxisListType

P = 128
D = 1024
C = D // P
T = 512
SB, ST = 8, 8
NS = SB * ST
N = T + NS
HALF = N // 2
NB = T // P
HD = 64
TAPS = 31
PAST = TAPS - 1
HEADS, TOPK, NKEYS = 8, 16, 128
KAPPA = float(np.exp(-0.5))
RMS_EPS, GN_EPS, LN_EPS = 1e-6, 6.4e-4, 1e-5
LEVELS = 7
SLEVELS = 3
LOWEST = -3.0e38

(MU0, W0, A0, K_K, K_A, R_K, LN_W, LN_B, B_PA, B_PG, B_DW, CLN_G, CLN_B, B_P2,
 NMIX0, NMIX1, NFFN0, NFFN1, NFIN, TAP0) = (0, 6, 7, 8, 9, 10, 11, 12, 13, 14, 15, 16, 17, 18,
                                            19, 20, 21, 22, 23, 24)
NPAR = TAP0 + TAPS


class Steps:

    def __init__(self, sem, names, start=0, a_pass_ahead=False):
        self.sem, self.names, self.next = sem, list(names), 0
        self.start = len(self.names) if a_pass_ahead else start

    def value(self, name, i=0):
        return i * len(self.names) + (self.start + self.names.index(name) + 1)

    def all_before(self, i):
        return i * len(self.names) + self.start

    def before(self, name, i):
        assert self.start == len(self.names)
        return i * len(self.names) + (self.names.index(name) + 1)

    def begin(self, engine):
        assert self.start and self.next == 0
        engine.sem_inc(self.sem, self.start)

    def at(self, name):
        assert self.names[self.next] == name, (name, self.names[self.next])
        self.next = (self.next + 1) % len(self.names)
        return self.sem


class Region:

    def __init__(self, tensor, at=0):
        self.tensor, self.at = tensor, at

    def cut(self, *shape, parts=P, dtype=F32):
        n = int(np.prod(shape))
        view = self.tensor[0:parts, self.at:self.at + n]
        self.at += n
        assert self.at <= self.tensor.shape[1], (self.at, self.tensor.shape)
        if dtype != F32:
            view = view.bitcast(dtype)
        if len(shape) == 2:
            view = view.rearrange("p (a b) -> p a b", b=shape[1])
        if len(shape) == 3:
            view = view.rearrange("p (a b c) -> p a b c", b=shape[1], c=shape[2])
        return view


def halves(view):
    return view.rearrange("p (a b) -> p a b", b=HALF)


def of_banks(psum, bank, parts=slice(0, P)):
    return psum[parts, bank:bank + 2, 0:HALF]


def unsq(view, axis, n):
    return view.unsqueeze(axis).to_broadcast(list(view.shape[:axis]) + [n] + list(view.shape[axis:]))


def rmsnorm(nc, K, gain, out, store=None):
    n = K.name()
    act_s = Steps(K.sem(f"{n}_act"), [f"square{c}" for c in range(C)] + ["root"])
    pe_s = Steps(K.sem(f"{n}_pe"), [f"summed{c}" for c in range(C)])
    dve_s = Steps(K.sem(f"{n}_dve"), [f"scaled{c}" for c in range(C)])
    stored = K.sem(f"{n}_stored")
    sq = [K.small[:, 0:N], K.small[:, N:2 * N]]
    root, inv = K.small[:, 2 * N:3 * N], K.small[:, 3 * N:4 * N]
    with nc.Block() as block:
        @block.scalar
        def _(act):
            for c in range(C):
                if c >= 2:
                    act.wait_ge(pe_s.sem, pe_s.value(f"summed{c - 2}"))
                act.activation(sq[c % 2], K.x[:, c, :], ACT.Square).then_inc(act_s.at(f"square{c}"), 1)
            act.wait_ge(pe_s.sem, pe_s.value(f"summed{C - 1}"))
            act.activation(halves(root), of_banks(K.ps, 0), ACT.Sqrt,
                                      bias=K.eps[:, 0:1], scale=1.0 / D).then_inc(act_s.at("root"), 1)

        @block.tensor
        def _(pe):
            for c in range(C):
                pe.wait_ge(act_s.sem, act_s.value(f"square{c}"))
                for h in range(2):
                    last = pe.matmul(K.ps[:, h, 0:HALF], K.ones, sq[c % 2][:, h * HALF:(h + 1) * HALF],
                                     start=c == 0, stop=c == C - 1)
                last.then_inc(pe_s.at(f"summed{c}"), 1)

        @block.vector
        def _(dve):
            dve.wait_ge(act_s.sem, act_s.value("root"))
            dve.reciprocal(inv, root)
            dve.drain()
            for c in range(C):
                dve.scalar_tensor_tensor(out=out[:, c, :], in0=K.x[:, c, :],
                                                    scalar=K.par[:, gain, c:c + 1], in1=inv,
                                                    op0=ALU.mult, op1=ALU.mult).then_inc(dve_s.at(f"scaled{c}"), 1)

        @block.sync
        def _(sp):
            if store is not None:
                for c in range(C):
                    sp.wait_ge(dve_s.sem, dve_s.value(f"scaled{c}"))
                    sp.dma_start(store[:, c, :], out[:, c, :]).then_inc(stored, 16)
                sp.wait_ge(stored, 16 * C)


def linear_into_x(nc, K, weights, src, bias=None):
    n = K.name()
    loaded = [K.sem(f"{n}_w{j}") for j in range(2)]
    pe_s = Steps(K.sem(f"{n}_pe"), ["product0", "product1"])
    dve_s = Steps(K.sem(f"{n}_dve"), ["added0", "added1"], start=1)
    with nc.Block() as block:
        @block.sync
        def _(sp):
            for j in range(2):
                sp.dma_start(K.w[j], weights[j]).then_inc(loaded[j], 16)
            with sp.Fori(1, C // 2) as i:
                for j in range(2):
                    sp.wait_ge(pe_s.sem, i * 2 + (j - 1))
                    sp.dma_start(K.w[j], weights[bass.ds(i * 2 + j, 1)].squeeze(0)).then_inc(loaded[j], 16)

        @block.tensor
        def _(pe):
            with pe.Fori(0, C // 2) as i:
                for j in range(2):
                    pe.wait_ge(dve_s.sem, dve_s.all_before(i))
                    pe.wait_ge(loaded[j], i * 16 + 16)
                    for h in range(2):
                        for k in range(C):
                            last = pe.matmul(K.ps[:, 2 * j + h, 0:HALF], K.w[j][:, k, :],
                                             src[:, k, h * HALF:(h + 1) * HALF],
                                             start=k == 0, stop=k == C - 1)
                    last.then_inc(pe_s.at(f"product{j}"), 1)

        @block.vector
        def _(dve):
            dve_s.begin(dve)
            with dve.Fori(0, C // 2) as i:
                for j in range(2):
                    dve.wait_ge(pe_s.sem, pe_s.value(f"product{j}", i))
                    dst = K.x[:, bass.ds(i * 2 + j, 1), :].squeeze(1).rearrange("p (a b) -> p a b", b=HALF)
                    add = K.bias_cols[:, j:j + 1] if bias is not None else 0.0
                    if bias is not None:
                        dve.tensor_copy(add, K.par[:, bias, bass.ds(i * 2 + j, 1)])
                        dve.drain()
                    dve.scalar_tensor_tensor(out=dst, in0=of_banks(K.ps, 2 * j), scalar=add,
                                                        in1=dst, op0=ALU.add, op1=ALU.add).then_inc(dve_s.at(f"added{j}"), 1)


def load_constants(nc, K, I):
    loaded = K.sem("constants_loaded")
    with nc.Block() as block:
        @block.sync
        def _(sp):
            pairs = [(K.x, I["x"]), (K.par, I["par"]), (K.cst, I["cst"]), (K.level, I["level"])]
            for dst, src in pairs:
                sp.dma_start(dst, src).then_inc(loaded, 16)
            sp.wait_ge(loaded, 16 * len(pairs))

        @block.gpsimd
        def _(pool):
            for j, eps in enumerate((RMS_EPS, GN_EPS, LN_EPS)):
                pool.memset(K.eps[:, j:j + 1], eps)


def time_mix_inputs(nc, K, I, h, xx, xm, hid_wa, hid_g):
    n = "mix"
    low, shift = K.low, K.shift
    loaded = K.sem(f"{n}_loaded")
    stored, rows_ready = K.sem(f"{n}_stored"), K.sem(f"{n}_rows_ready")
    new_shift = K.new_shift
    mixes = [f"mixed{m}_{k}" for m in (3, 4, 5) for k in range(C)]
    dve_s = Steps(K.sem(f"{n}_dve"), mixes)
    pe_s = Steps(K.sem(f"{n}_pe"), [f"used{m}_{k}" for m in (3, 4, 5) for k in range(C)])
    tmp = [K.small[:, 0:N], K.small[:, N:2 * N]]
    with nc.Block() as block:
        @block.sync
        def _(sp):
            sp.dma_start(low, I["low1"]).then_inc(loaded, 16)
            sp.dma_start(shift, I["shift"]).then_inc(loaded, 16)
            sp.wait_ge(rows_ready, 1)
            sp.dma_start(I["o_shift"], new_shift).then_inc(stored, 16)
            sp.wait_ge(stored, 16)

        @block.vector
        def _(dve):
            dve.wait_ge(loaded, 32)
            hs, xs = (v[:, :, T:N].rearrange("p c (b t) -> p c b t", t=ST) for v in (h, xx))
            dve.tensor_tensor(xx[:, :, 1:T], h[:, :, 0:T - 1], h[:, :, 1:T], ALU.subtract)
            dve.tensor_scalar(xx[:, :, 0:1], h[:, :, 0:1], -1.0, None, ALU.mult)
            dve.tensor_tensor(xs[:, :, :, 0], shift, hs[:, :, :, 0], ALU.subtract)
            for c in range(C):
                dve.tensor_tensor(xs[:, c, :, 1:ST], hs[:, c, :, 0:ST - 1], hs[:, c, :, 1:ST], ALU.subtract)
            dve.drain()
            q = 0
            for m in (3, 4, 5):
                for k in range(C):
                    if q >= 2:
                        dve.wait_ge(pe_s.sem, q - 1)
                    dve.scalar_tensor_tensor(out=tmp[q % 2], in0=xx[:, k, :],
                                                        scalar=K.par[:, MU0 + m, k:k + 1], in1=h[:, k, :],
                                                        op0=ALU.mult, op1=ALU.add).then_inc(dve_s.at(f"mixed{m}_{k}"), 1)
                    q += 1
            for m in range(3):
                for k in range(C):
                    dve.scalar_tensor_tensor(out=xm[m][:, k, :], in0=xx[:, k, :],
                                             scalar=K.par[:, MU0 + m, k:k + 1], in1=h[:, k, :],
                                             op0=ALU.mult, op1=ALU.add)

        @block.tensor
        def _(pe):
            pe.wait_ge(loaded, 32)
            q = 0
            for m, part, lo, hi in ((3, slice(0, 64), 0, 64), (4, slice(64, P), 64, 128), (5, slice(0, P), 128, 256)):
                for k in range(C):
                    pe.wait_ge(dve_s.sem, dve_s.value(f"mixed{m}_{k}"))
                    for s in range(2):
                        last = pe.matmul(K.ps[part, 2 * (m - 3) + s, 0:HALF], low[:, k, lo:hi],
                                         tmp[q % 2][:, s * HALF:(s + 1) * HALF],
                                         start=k == 0, stop=k == C - 1)
                    last.then_inc(pe_s.at(f"used{m}_{k}"), 1)
                    q += 1

        @block.scalar
        def _(act):
            act.activation(new_shift[:, :, 0:1], h[:, :, T - 1:T], ACT.Copy)
            act.activation(new_shift[:, :, 1:], h[:, :, T:N].rearrange("p c (b t) -> p c b t", t=ST)[:, :, :, ST - 1],
                           ACT.Copy)
            act.drain().then_inc(rows_ready, 1)
            act.wait_ge(pe_s.sem, pe_s.value(f"used3_{C - 1}"))
            act.activation(halves(hid_wa[0:64, :]), of_banks(K.ps, 0, slice(0, 64)), ACT.Tanh)
            act.wait_ge(pe_s.sem, pe_s.value(f"used4_{C - 1}"))
            act.activation(halves(hid_wa[64:P, :]), of_banks(K.ps, 2, slice(64, P)), ACT.Copy)
            act.wait_ge(pe_s.sem, pe_s.value(f"used5_{C - 1}"))
            act.activation(halves(hid_g), of_banks(K.ps, 4), ACT.Sigmoid)


def wkv(nc, K, I, xm, y_out, hid_wa, hid_g, R):
    f = lambda: R.cut(N)
    dead_at = R.at
    r_s, k_s, sg, sq, kk, cum, lprev, kf = f(), f(), f(), f(), f(), f(), f(), f()
    av_at = R.at
    av, v_s, g_s, nrm = f(), f(), f(), f()
    e_pos, e_neg = f(), f()
    prev_at = R.at
    e_prev, at, bt, kt, rt, bon = f(), f(), f(), f(), f(), f()
    ba, rk = lprev, sq
    y_s, yc, ysq, sd = e_pos, e_neg, e_prev, nrm
    low2 = R.cut(2, P)
    prm, ln = R.cut(NPAR), R.cut(2)
    sc = R.cut(3 * NB + SB)
    esc = R.cut(3 * NB + SB)
    ptok = R.cut(3, NB, P)
    l_at = R.at
    L, LT, X, XT = (R.cut(2, NB, P) for _ in range(4))
    g_at = R.at
    G, RB, RK = (R.cut(2, NB, P) for _ in range(3))
    Q0 = Region(K.arena, dead_at)
    co, coT, y1, y2 = ([Q0.cut(NB, P) for _ in range(2)] for _ in range(4))
    assert Q0.at <= av_at
    state = R.cut(P)
    Q0 = Region(K.arena, av_at)
    sc_state, s_tmp = [Q0.cut(P) for _ in range(2)], Q0.cut(P)
    Q0 = Region(K.arena, prev_at)
    r_tok, u_tok = Q0.cut(P), Q0.cut(P)
    Q = Region(K.arena, R.at)
    s_state = Q.cut(SB, P)
    Q2 = Region(K.arena, l_at)
    stok = Q2.cut(3, P, parts=NS)
    sL, sLT, sX, sXT, sG, sRB, sRK, sco, scoT = (Q2.cut(2, NS, parts=NS) for _ in range(9))
    sy1, sy2 = Q2.cut(2, NS, parts=NS), Q2.cut(2, NS, parts=NS)
    rT, rT2 = Q2.cut(NS), Q2.cut(NS)
    sr_tok, su_tok = Q2.cut(P, parts=NS), Q2.cut(P, parts=NS)
    Q3 = Region(K.arena, g_at)
    u_exp, v_exp = Q3.cut(SB, P, parts=NS), Q3.cut(SB, P, parts=NS)
    s_prod = Q3.cut(SB, P)

    both = lambda l: 1 if l < LEVELS - 1 else 2
    wl = [K.sem(f"wkv_w{j}") for j in range(3)]
    low_loaded, prm_loaded, state_loaded = (K.sem(f"wkv_{x}_loaded") for x in ("low", "prm", "state"))
    stored, zeroed = K.sem("wkv_stored"), K.sem("wkv_zeroed")
    pe_s = Steps(K.sem("wkv_pe"),
                 ["w", "k", "a", "r", "norm", "v", "g", "bonus", "tok_v", "tok_b", "tok_k"]
                 + [f"gram_{x}{e}" for e in range(2) for x in ("L", "LT", "G", "RB", "RK")]
                 + [f"{x}{l}_{e}" for l in range(1, LEVELS) for x in ("y1", "y2", "dXT", "dX")[::both(l)] for e in range(2)]
                 + [f"{x}{b}" for b in range(NB) for x in ("R", "U", "Y", "S")]
                 + ["s_tok", "s_gram0", "s_gram1"]
                 + [f"s_{x}{l}" for l in range(1, SLEVELS) for x in ("y", "d")]
                 + ["s_RT", "s_R", "s_U", "s_Y", "mean", "s_S", "var"], a_pass_ahead=True)
    act_s = Steps(K.sem("wkv_act"),
                  ["w", "k", "ksq", "a", "r", "norm", "exps", "v", "g", "tok_v", "tok_b", "tok_k"]
                  + [f"gram_{x}{e}" for e in range(2) for x in ("L", "LT")]
                  + [f"{x}{l}_{e}" for l in range(1, LEVELS) for x in ("y1", "y2")[::both(l)] for e in range(2)]
                  + [f"{x}{b}" for b in range(NB) for x in ("R", "U")]
                  + ["Y", "s_tok"]
                  + [f"s_y{l}" for l in range(1, SLEVELS)]
                  + ["s_R", "s_U", "ysq", "sd"], a_pass_ahead=True)
    dve_s = Steps(K.sem("wkv_dve"),
                  ["logs", "rk", "factors", "bonus"]
                  + [f"gram{x}{e}" for e in range(2) for x in ("G", "RB", "RK")]
                  + ["level0"]
                  + [f"{x}{l}_{e}" for l in range(1, LEVELS) for x in ("XT", "X")[::both(l)] for e in range(2)]
                  + [f"state{b}" for b in range(NB)]
                  + ["s_gram"]
                  + [f"s_X{l}" for l in range(1, SLEVELS)]
                  + ["s_RT", "s_y", "s_exp", "yc", "s_state", "y"], a_pass_ahead=True)
    pool_s = Steps(K.sem("wkv_pool"), [f"{x}{l}_{e}" for l in range(1, LEVELS) for e in range(2) for x in ("co", "coT")[::both(l)]])
    ps = K.ps
    lev = lambda l, t: K.level[:, 2 * l + t, :]

    with nc.Block() as block:
        @block.sync
        def _(sp):
            sp.sem_inc(stored, 64)
            weight = (1, 0, 2)

            def load_state(i):
                for e in range(2):
                    q = slice(64 * e, 64 * e + 64)
                    sp.dma_start(s_state[q, :, q], I["state"][bass.ds(i, 1), q].squeeze(0)).then_inc(state_loaded, 16)

            sp.dma_start(low2, I["low2"][0]).then_inc(low_loaded, 16)
            sp.dma_start(prm, I["cpar"][0]).then_inc(prm_loaded, 16)
            for j, m in enumerate(weight):
                sp.dma_start(K.w[j], I["w_rkv"][m]).then_inc(wl[j], 16)
            sp.wait_ge(zeroed, 1)
            load_state(0)
            with sp.Fori(1, C) as i:
                for j, (name, m) in enumerate(zip(("k", "r", "v"), weight)):
                    sp.wait_ge(pe_s.sem, pe_s.before(name, i))
                    sp.dma_start(K.w[j], I["w_rkv"][bass.ds(i * 3 + m, 1)].squeeze(0)).then_inc(wl[j], 16)
                sp.wait_ge(pe_s.sem, pe_s.before("g", i))
                sp.dma_start(low2, I["low2"][bass.ds(i, 1)].squeeze(0)).then_inc(low_loaded, 16)
                sp.wait_ge(act_s.sem, act_s.before("a", i))
                sp.wait_ge(dve_s.sem, dve_s.before("rk", i))
                sp.dma_start(prm, I["cpar"][bass.ds(i, 1)].squeeze(0)).then_inc(prm_loaded, 16)
                sp.wait_ge(dve_s.sem, dve_s.before(f"state{NB - 1}", i))
                for e in range(2):
                    q = slice(64 * e, 64 * e + 64)
                    sp.dma_start(I["o_wkv_p"][bass.ds(i - 1, 1), q].squeeze(0), state[q, q]).then_inc(stored, 16)
                sp.wait_ge(dve_s.sem, dve_s.before("s_state", i))
                for e in range(2):
                    q = slice(64 * e, 64 * e + 64)
                    sp.dma_start(I["o_wkv_s"][bass.ds(i - 1, 1), q].squeeze(0), s_state[q, :, q]).then_inc(stored, 16)
                sp.wait_ge(stored, i * 64 + 64)
                load_state(i)
            sp.wait_ge(dve_s.sem, dve_s.value("s_state", C - 1))
            for e in range(2):
                q = slice(64 * e, 64 * e + 64)
                sp.dma_start(I["o_wkv_p"][C - 1, q], state[q, q]).then_inc(stored, 16)
                sp.dma_start(I["o_wkv_s"][C - 1, q], s_state[q, :, q]).then_inc(stored, 16)
            sp.wait_ge(stored, C * 64 + 64)

        @block.tensor
        def _(pe):
            pe_s.begin(pe)

            def project(src, w, bank, name):
                for h in range(2):
                    for k in range(C):
                        last = pe.matmul(ps[:, bank + h, 0:HALF], w[:, k, :], src[:, k, h * HALF:(h + 1) * HALF],
                                         start=k == 0, stop=k == C - 1)
                last.then_inc(pe_s.at(name), 1)

            def expand(w, src, bank, name):
                for h in range(2):
                    last = pe.matmul(ps[:, bank + h, 0:HALF], w, src[:, h * HALF:(h + 1) * HALF], start=True, stop=True)
                last.then_inc(pe_s.at(name), 1)

            with pe.Fori(0, C) as i:
                pe.wait_ge(low_loaded, i * 16 + 16)
                expand(low2[0:64, 0, :], hid_wa[0:64, :], 4, "w")
                pe.wait_ge(wl[0], i * 16 + 16)
                project(xm[1], K.w[0], 2, "k")
                pe.wait_ge(dve_s.sem, dve_s.before("s_state", i))
                expand(low2[64:P, 0, :], hid_wa[64:P, :], 6, "a")
                pe.wait_ge(act_s.sem, act_s.before("sd", i))
                pe.wait_ge(wl[1], i * 16 + 16)
                project(xm[0], K.w[1], 0, "r")
                pe.wait_ge(act_s.sem, act_s.value("a", i))
                expand(K.headones, sq, 6, "norm")
                pe.wait_ge(wl[2], i * 16 + 16)
                project(xm[2], K.w[2], 2, "v")
                pe.wait_ge(act_s.sem, act_s.value("w", i))
                expand(low2[:, 1, :], hid_g, 4, "g")
                pe.wait_ge(act_s.sem, act_s.value("norm", i))
                pe.wait_ge(dve_s.sem, dve_s.value("rk", i))
                expand(K.headones, rk, 6, "bonus")
                for src, bank, name, other, ready in ((v_s, 2, "tok_v", act_s, "v"), (bt, 0, "tok_b", dve_s, "factors"),
                                                      (kt, 1, "tok_k", act_s, "r")):
                    pe.wait_ge(other.sem, other.value(ready, i))
                    for b in range(NB):
                        last = pe.transpose(ps[:, bank, b * P:(b + 1) * P], src[:, b * P:(b + 1) * P], K.ident)
                    last.then_inc(pe_s.at(name), 1)
                bank = {(0, "L"): 4, (0, "LT"): 5, (0, "G"): 6, (0, "RB"): 7, (0, "RK"): 0,
                        (1, "L"): 1, (1, "LT"): 2, (1, "G"): 3, (1, "RB"): 4, (1, "RK"): 5}
                for e in range(2):
                    q = slice(64 * e, 64 * e + 64)
                    for name, left, right, free in (("L", at, bt, ("g", "tok_k")), ("LT", bt, at, (None, "tok_v")),
                                                    ("G", kt, at, (None, None)), ("RB", bt, rt, (None, "gram_L0")),
                                                    ("RK", kt, rt, ("tok_b", "gram_LT0"))):
                        if free[e]:
                            pe.wait_ge(act_s.sem, act_s.value(free[e], i))
                        if (e, name) == (0, "G"):
                            pe.wait_ge(dve_s.sem, dve_s.value("bonus", i))
                        for b in range(NB):
                            t = slice(b * P, (b + 1) * P)
                            last = pe.matmul(ps[:, bank[e, name], t], left[q, t], right[q, t], start=True, stop=True)
                        last.then_inc(pe_s.at(f"gram_{name}{e}"), 1)
                pe.wait_ge(dve_s.sem, dve_s.value("level0", i))
                for l in range(1, LEVELS):
                    for e in range(2):
                        pe.wait_ge(pool_s.sem, pool_s.value(f"co{l}_{e}", i))
                        if l > 1:
                            pe.wait_ge(dve_s.sem, dve_s.value(f"XT{l - 1}_{e}", i))
                        for b in range(NB):
                            last = pe.matmul(ps[:, 4 * e, b * P:(b + 1) * P], co[e][:, b, :], XT[:, e, b, :],
                                             start=True, stop=True)
                        last.then_inc(pe_s.at(f"y1{l}_{e}"), 1)
                    for e in range(2) if both(l) == 1 else ():
                        pe.wait_ge(pool_s.sem, pool_s.value(f"coT{l}_{e}", i))
                        if l > 1:
                            pe.wait_ge(dve_s.sem, dve_s.value(f"X{l - 1}_{e}", i))
                        for b in range(NB):
                            last = pe.matmul(ps[:, 4 * e + 1, b * P:(b + 1) * P], coT[e][:, b, :], X[:, e, b, :],
                                             start=True, stop=True)
                        last.then_inc(pe_s.at(f"y2{l}_{e}"), 1)
                    for e in range(2):
                        pe.wait_ge(act_s.sem, act_s.value(f"y1{l}_{e}", i))
                        if l > 1:
                            pe.wait_ge(dve_s.sem, dve_s.value(f"X{l - 1}_{e}", i))
                        for b in range(NB):
                            last = pe.matmul(ps[:, 4 * e + 2, b * P:(b + 1) * P], X[:, e, b, :], y1[e][:, b, :],
                                             start=True, stop=True)
                        last.then_inc(pe_s.at(f"dXT{l}_{e}"), 1)
                    for e in range(2) if both(l) == 1 else ():
                        pe.wait_ge(act_s.sem, act_s.value(f"y2{l}_{e}", i))
                        for b in range(NB):
                            last = pe.matmul(ps[:, 4 * e + 3, b * P:(b + 1) * P], XT[:, e, b, :], y2[e][:, b, :],
                                             start=True, stop=True)
                        last.then_inc(pe_s.at(f"dX{l}_{e}"), 1)
                pe.wait_ge(dve_s.sem, dve_s.value(f"XT{LEVELS - 1}_1", i))
                for b in range(NB):
                    t = slice(b * P, (b + 1) * P)
                    if b:
                        pe.wait_ge(dve_s.sem, dve_s.value(f"state{b - 1}", i))
                    pe.matmul(ps[:, 0, 0:P], at[:, t], sc_state[b % 2], start=True, stop=False)
                    for e in range(2):
                        q = slice(64 * e, 64 * e + 64)
                        last = pe.matmul(ps[:, 0, q], G[:, e, b, :], ptok[:, 2, b, q], start=False, stop=e == 1)
                    last.then_inc(pe_s.at(f"R{b}"), 1)
                    pe.wait_ge(act_s.sem, act_s.value(f"R{b}", i))
                    for e in range(2):
                        q = slice(64 * e, 64 * e + 64)
                        last = pe.matmul(ps[:, 1, q], XT[:, e, b, :], r_tok[:, q], start=True, stop=True)
                    last.then_inc(pe_s.at(f"U{b}"), 1)
                    pe.matmul(ps[:, 3, t], sc_state[b % 2], rt[:, t], start=True, stop=False)
                    pe.wait_ge(act_s.sem, act_s.value(f"U{b}", i))
                    for e in range(2):
                        q = slice(64 * e, 64 * e + 64)
                        pe.matmul(ps[q, 3, t], u_tok[:, q], RB[:, e, b, :], start=False, stop=False)
                        last = pe.matmul(ps[q, 3, t], ptok[:, 2, b, q], RK[:, e, b, :], start=False, stop=True)
                    last.then_inc(pe_s.at(f"Y{b}"), 1)
                    pe.matmul(ps[:, 2, 0:P], ptok[:, 0, b, :], u_tok, start=True, stop=False)
                    last = pe.matmul(ps[:, 2, 0:P], ptok[:, 1, b, :], ptok[:, 2, b, :], start=False, stop=True)
                    last.then_inc(pe_s.at(f"S{b}"), 1)
                pe.wait_ge(dve_s.sem, dve_s.value(f"state{NB - 1}", i))
                pe.wait_ge(act_s.sem, act_s.value("Y", i))
                pe.nop(nofuse=True)
                for j, src in enumerate((bt, kt, v_s)):
                    last = pe.transpose(ps[0:NS, 4, j * P:(j + 1) * P], src[:, T:N], K.ident)
                last.then_inc(pe_s.at("s_tok"), 1)
                for e in range(2):
                    q = slice(64 * e, 64 * e + 64)
                    for j, (left, right) in enumerate(((at, bt), (bt, at), (kt, at), (bt, rt), (kt, rt))):
                        last = pe.matmul(ps[0:NS, 5 + e, j * NS:(j + 1) * NS], left[q, T:N], right[q, T:N],
                                         start=True, stop=True)
                    last.then_inc(pe_s.at(f"s_gram{e}"), 1)
                for l in range(1, SLEVELS):
                    pe.wait_ge(dve_s.sem, dve_s.value("s_gram" if l == 1 else f"s_X{l - 1}", i))
                    pe.nop(nofuse=True)
                    for e in range(2):
                        pe.matmul(ps[0:NS, 0, e * NS:(e + 1) * NS], sco[:, e, :], sXT[:, e, :], start=True, stop=True)
                    for e in range(2):
                        last = pe.matmul(ps[0:NS, 0, (2 + e) * NS:(3 + e) * NS], scoT[:, e, :], sX[:, e, :],
                                         start=True, stop=True)
                    last.then_inc(pe_s.at(f"s_y{l}"), 1)
                    pe.wait_ge(act_s.sem, act_s.value(f"s_y{l}", i))
                    pe.nop(nofuse=True)
                    for e in range(2):
                        pe.matmul(ps[0:NS, 1, e * NS:(e + 1) * NS], sX[:, e, :], sy1[:, e, :], start=True, stop=True)
                    for e in range(2):
                        last = pe.matmul(ps[0:NS, 1, (2 + e) * NS:(3 + e) * NS], sXT[:, e, :], sy2[:, e, :],
                                         start=True, stop=True)
                    last.then_inc(pe_s.at(f"s_d{l}"), 1)
                pe.wait_ge(state_loaded, i * 32 + 32)
                for b in range(SB):
                    pe.matmul(ps[:, 2, b * ST:(b + 1) * ST], s_state[:, b, :], at[:, T + b * ST:T + (b + 1) * ST],
                              start=True, stop=True)
                for b in range(SB):
                    pe.matmul(ps[:, 3, b * ST:(b + 1) * ST], s_state[:, b, :], rt[:, T + b * ST:T + (b + 1) * ST],
                              start=True, stop=True)
                for e in range(2):
                    q = slice(64 * e, 64 * e + 64)
                    last = pe.matmul(ps[q, 2, NS:2 * NS], stok[:, 2, q], sG[:, e, :], start=True, stop=True)
                last.then_inc(pe_s.at("s_RT"), 1)
                pe.wait_ge(dve_s.sem, dve_s.value("s_RT", i))
                pe.nop(nofuse=True)
                pe.transpose(ps[0:NS, 0, 0:P], rT, K.ident).then_inc(pe_s.at("s_R"), 1)
                pe.wait_ge(act_s.sem, act_s.value("s_R", i))
                pe.nop(nofuse=True)
                for e in range(2):
                    q = slice(64 * e, 64 * e + 64)
                    last = pe.matmul(ps[0:NS, 1, q], sXT[:, e, :], sr_tok[:, q], start=True, stop=True)
                last.then_inc(pe_s.at("s_U"), 1)
                pe.wait_ge(act_s.sem, act_s.value("s_U", i))
                pe.nop(nofuse=True)
                for e in range(2):
                    q = slice(64 * e, 64 * e + 64)
                    pe.matmul(ps[q, 3, NS:2 * NS], su_tok[:, q], sRB[:, e, :], start=True, stop=False)
                    last = pe.matmul(ps[q, 3, NS:2 * NS], stok[:, 2, q], sRK[:, e, :], start=False, stop=True)
                last.then_inc(pe_s.at("s_Y"), 1)
                pe.wait_ge(dve_s.sem, dve_s.value("s_y", i))
                expand(K.headones, y_s, 0, "mean")
                pe.wait_ge(dve_s.sem, dve_s.value("s_exp", i))
                for h in range(2):
                    hb = slice(4 * h, 4 * h + 4)
                    pe.matmul(ps[:, 6 + h, :], stok[:, 0, :], u_exp[:, hb, :], start=True, stop=False)
                    last = pe.matmul(ps[:, 6 + h, :], stok[:, 1, :], v_exp[:, hb, :], start=False, stop=True)
                last.then_inc(pe_s.at("s_S"), 1)
                pe.wait_ge(act_s.sem, act_s.value("ysq", i))
                expand(K.headones, ysq, 0, "var")

        @block.scalar
        def _(act):
            act_s.begin(act)
            with act.Fori(0, C) as i:
                act.wait_ge(prm_loaded, i * 16 + 16)
                act.wait_ge(pe_s.sem, pe_s.value("w", i))
                act.activation(halves(sg), of_banks(ps, 4), ACT.Sigmoid, bias=prm[:, W0:W0 + 1]).then_inc(act_s.at("w"), 1)
                act.wait_ge(pe_s.sem, pe_s.value("k", i))
                act.activation(halves(k_s), of_banks(ps, 2), ACT.Copy).then_inc(act_s.at("k"), 1)
                act.activation(halves(sq), of_banks(ps, 2), ACT.Square, scale=prm[:, K_K:K_K + 1]).then_inc(act_s.at("ksq"), 1)
                act.wait_ge(pe_s.sem, pe_s.value("a", i))
                act.activation(halves(av), of_banks(ps, 6), ACT.Sigmoid, bias=prm[:, A0:A0 + 1]).then_inc(act_s.at("a"), 1)
                act.wait_ge(pe_s.sem, pe_s.value("r", i))
                act.activation(halves(r_s), of_banks(ps, 0), ACT.Copy).then_inc(act_s.at("r"), 1)
                act.wait_ge(dve_s.sem, dve_s.before("y", i))
                act.wait_ge(pe_s.sem, pe_s.value("norm", i))
                act.activation(halves(nrm), of_banks(ps, 6), ACT.Sqrt).then_inc(act_s.at("norm"), 1)
                act.wait_ge(dve_s.sem, dve_s.value("logs", i))
                act.activation(e_pos, cum, ACT.Exp, scale=-KAPPA)
                act.activation(e_neg, cum, ACT.Exp, scale=KAPPA)
                act.activation(e_prev, lprev, ACT.Exp, scale=-KAPPA)
                act.activation(esc, sc, ACT.Exp, scale=-KAPPA).then_inc(act_s.at("exps"), 1)
                act.wait_ge(pe_s.sem, pe_s.value("v", i))
                act.activation(halves(v_s), of_banks(ps, 2), ACT.Copy).then_inc(act_s.at("v"), 1)
                act.wait_ge(pe_s.sem, pe_s.value("g", i))
                act.activation(halves(g_s), of_banks(ps, 4), ACT.Copy).then_inc(act_s.at("g"), 1)
                for j, bank, name in ((2, 2, "tok_v"), (0, 0, "tok_b"), (1, 1, "tok_k")):
                    act.wait_ge(pe_s.sem, pe_s.value(name, i))
                    act.activation(ptok[:, j], ps[:, bank, :].rearrange("p (b f) -> p b f", f=P), ACT.Copy).then_inc(act_s.at(name), 1)
                for e, (bL, bLT) in enumerate(((4, 5), (1, 2))):
                    for name, dst, bank in (("L", L, bL), ("LT", LT, bLT)):
                        act.wait_ge(pe_s.sem, pe_s.value(f"gram_{name}{e}", i))
                        act.activation(dst[:, e], ps[:, bank, :].rearrange("p (b f) -> p b f", f=P), ACT.Copy).then_inc(act_s.at(f"gram_{name}{e}"), 1)
                for l in range(1, LEVELS):
                    for j, (name, dst) in enumerate((("y1", y1), ("y2", y2))[::both(l)]):
                        for e in range(2):
                            act.wait_ge(pe_s.sem, pe_s.value(f"{name}{l}_{e}", i))
                            if l > 1:
                                act.wait_ge(pe_s.sem, pe_s.value(f"{('dXT', 'dX')[j]}{l - 1}_{e}", i))
                            act.activation(dst[e], ps[:, 4 * e + j, :].rearrange("p (b f) -> p b f", f=P),
                                                      ACT.Copy).then_inc(act_s.at(f"{name}{l}_{e}"), 1)
                for b in range(NB):
                    act.wait_ge(pe_s.sem, pe_s.value(f"R{b}", i))
                    act.activation(r_tok, ps[:, 0, 0:P], ACT.Copy).then_inc(act_s.at(f"R{b}"), 1)
                    act.wait_ge(pe_s.sem, pe_s.value(f"U{b}", i))
                    act.activation(u_tok, ps[:, 1, 0:P], ACT.Copy).then_inc(act_s.at(f"U{b}"), 1)
                act.wait_ge(pe_s.sem, pe_s.value(f"Y{NB - 1}", i))
                act.activation(y_s[:, 0:T], ps[:, 3, :], ACT.Copy).then_inc(act_s.at("Y"), 1)
                act.wait_ge(dve_s.sem, dve_s.value(f"state{NB - 1}", i))
                act.wait_ge(pe_s.sem, pe_s.value("s_tok", i))
                act.activation(stok, ps[0:NS, 4, 0:3 * P].rearrange("p (j f) -> p j f", f=P), ACT.Copy).then_inc(act_s.at("s_tok"), 1)
                for l in range(1, SLEVELS):
                    act.wait_ge(pe_s.sem, pe_s.value(f"s_y{l}", i))
                    if l > 1:
                        act.wait_ge(pe_s.sem, pe_s.value(f"s_d{l - 1}", i))
                    act.activation(sy1, ps[0:NS, 0, 0:2 * NS].rearrange("p (e f) -> p e f", f=NS), ACT.Copy)
                    act.activation(sy2, ps[0:NS, 0, 2 * NS:4 * NS].rearrange("p (e f) -> p e f", f=NS),
                                              ACT.Copy).then_inc(act_s.at(f"s_y{l}"), 1)
                act.wait_ge(pe_s.sem, pe_s.value("s_R", i))
                act.activation(sr_tok, ps[0:NS, 0, 0:P], ACT.Copy).then_inc(act_s.at("s_R"), 1)
                act.wait_ge(pe_s.sem, pe_s.value("s_U", i))
                act.activation(su_tok, ps[0:NS, 1, 0:P], ACT.Copy).then_inc(act_s.at("s_U"), 1)
                act.wait_ge(dve_s.sem, dve_s.value("yc", i))
                act.activation(ysq, yc, ACT.Square).then_inc(act_s.at("ysq"), 1)
                act.wait_ge(pe_s.sem, pe_s.value("var", i))
                act.activation(halves(sd), of_banks(ps, 0), ACT.Sqrt, bias=K.eps[:, 1:2], scale=1.0 / HD).then_inc(act_s.at("sd"), 1)

        @block.vector
        def _(dve):
            dve_s.begin(dve)
            tt, ts, stt = dve.tensor_tensor, dve.tensor_scalar, dve.scalar_tensor_tensor
            dve.memset(s_state, 0.0).then_inc(zeroed, 1)
            with dve.Fori(0, C) as i:
                dve.wait_ge(prm_loaded, i * 16 + 16)
                dve.tensor_copy(ln, prm[:, LN_W:LN_W + 2])
                dve.wait_ge(act_s.sem, act_s.value("w", i))
                dve.tensor_tensor_scan(cum, K.reset, sg, 0.0, ALU.mult, ALU.add)
                dve.drain()
                blocks = cum[:, 0:T].rearrange("p (b t) -> p b t", t=P)
                seqs = cum[:, T:N].rearrange("p (b t) -> p b t", t=ST)
                dve.tensor_copy(sc[:, 0:NB], blocks[:, :, P // 2 - 1])
                dve.tensor_copy(sc[:, NB:2 * NB], blocks[:, :, P - 1])
                dve.tensor_copy(sc[:, 3 * NB:3 * NB + SB], seqs[:, :, ST - 1])
                dve.drain()
                tt(sc[:, 2 * NB:3 * NB], sc[:, NB:2 * NB], sc[:, 0:NB], ALU.subtract)
                tt(blocks, blocks, unsq(sc[:, 0:NB], 2, P), ALU.subtract)
                dve.drain()
                tt(lprev, cum, sg, ALU.subtract).then_inc(dve_s.at("logs"), 1)
                dve.wait_ge(act_s.sem, act_s.value("a", i))
                ts(kf, av, 1.0, prm[:, K_A:K_A + 1], ALU.subtract, ALU.mult)
                dve.drain()
                stt(out=kf, in0=kf, scalar=1.0, in1=k_s, op0=ALU.add, op1=ALU.mult)
                dve.wait_ge(act_s.sem, act_s.value("norm", i))
                ts(nrm, nrm, 1e-12, None, ALU.max)
                dve.drain()
                dve.reciprocal(nrm, nrm)
                dve.drain()
                stt(out=kk, in0=k_s, scalar=prm[:, K_K:K_K + 1], in1=nrm, op0=ALU.mult, op1=ALU.mult)
                stt(out=rk, in0=r_s, scalar=prm[:, R_K:R_K + 1], in1=kf, op0=ALU.mult, op1=ALU.mult).then_inc(dve_s.at("rk"), 1)
                dve.drain()
                dve.wait_ge(act_s.sem, act_s.value("exps", i))
                stt(out=at, in0=kk, scalar=-1.0, in1=e_prev, op0=ALU.mult, op1=ALU.mult)
                tt(ba, kk, av, ALU.mult)
                tt(kt, kf, e_neg, ALU.mult)
                tt(rt, r_s, e_pos, ALU.mult)
                dve.drain()
                tt(bt, ba, e_neg, ALU.mult).then_inc(dve_s.at("factors"), 1)
                dve.memset(sc_state[0], 0.0)
                dve.wait_ge(act_s.sem, act_s.value("v", i))
                dve.wait_ge(pe_s.sem, pe_s.value("bonus", i))
                tt(halves(bon), of_banks(ps, 6), halves(v_s), ALU.mult).then_inc(dve_s.at("bonus"), 1)
                banks = {(0, "G"): 6, (0, "RB"): 7, (0, "RK"): 0, (1, "G"): 3, (1, "RB"): 4, (1, "RK"): 5}
                for e in range(2):
                    for name, dst, mask in (("G", G, K.m_before), ("RB", RB, K.m_upto), ("RK", RK, K.m_upto)):
                        dve.wait_ge(pe_s.sem, pe_s.value(f"gram_{name}{e}", i))
                        tt(dst[:, e], ps[:, banks[e, name], :].rearrange("p (b f) -> p b f", f=P),
                                      unsq(mask, 1, NB), ALU.mult).then_inc(dve_s.at(f"gram{name}{e}"), 1)
                dve.wait_ge(act_s.sem, act_s.value("gram_LT1", i))
                for src, dst, m in ((L, X, lev(0, 0)), (LT, XT, lev(0, 1))):
                    for e in range(2):
                        tt(dst[:, e], src[:, e], unsq(m, 1, NB), ALU.mult)
                dve.drain()
                for dst in (X, XT):
                    for e in range(2):
                        last = tt(dst[:, e], dst[:, e], unsq(K.ident, 1, NB), ALU.add)
                last.then_inc(dve_s.at("level0"), 1)
                dve.wait_ge(stored, i * 64 + 64)
                dve.memset(state, 0.0)
                for l in range(1, LEVELS):
                    for j, (name, dst) in enumerate((("XT", XT), ("X", X))[::both(l)]):
                        for e in range(2):
                            dve.wait_ge(pe_s.sem, pe_s.value(f"{('dX', 'dXT')[both(l) - 1]}{l}_{e}", i))
                            tt(dst[:, e], dst[:, e],
                                          ps[:, 4 * e + 2 + j, :].rearrange("p (b f) -> p b f", f=P), ALU.add).then_inc(dve_s.at(f"{name}{l}_{e}"), 1)
                for b in range(NB):
                    dve.wait_ge(pe_s.sem, pe_s.value(f"S{b}", i))
                    stt(out=s_tmp, in0=ps[:, 2, 0:P], scalar=esc[:, 2 * NB + b:2 * NB + b + 1], in1=K.headones,
                        op0=ALU.mult, op1=ALU.mult)
                    dve.drain()
                    last = stt(out=state, in0=state, scalar=esc[:, NB + b:NB + b + 1], in1=s_tmp,
                               op0=ALU.mult, op1=ALU.add)
                    if b < NB - 1:
                        dve.drain()
                        last = ts(sc_state[(b + 1) % 2], state, esc[:, b + 1:b + 2], None, ALU.mult)
                    last.then_inc(dve_s.at(f"state{b}"), 1)
                dve.wait_ge(act_s.sem, act_s.value("s_tok", i))
                grams = [ps[0:NS, 5 + e, 0:5 * NS].rearrange("p (j f) -> p j f", f=NS) for e in range(2)]
                for e in range(2):
                    dve.wait_ge(pe_s.sem, pe_s.value(f"s_gram{e}", i))
                    for j, (dst, mask) in enumerate(((sX, lev(0, 0)[0:NS, 0:NS]), (sXT, lev(0, 1)[0:NS, 0:NS]),
                                                     (sG, K.ms_before), (sRB, K.ms_upto), (sRK, K.ms_upto))):
                        tt(dst[:, e, :], grams[e][:, j, :], mask, ALU.mult)
                    dve.tensor_copy(sL[:, e, :], grams[e][:, 0, :])
                    dve.tensor_copy(sLT[:, e, :], grams[e][:, 1, :])
                dve.drain()
                for dst in (sX, sXT):
                    tt(dst, dst, unsq(K.ident[0:NS, 0:NS], 1, 2), ALU.add)
                for l in range(1, SLEVELS):
                    if l > 1:
                        dve.wait_ge(pe_s.sem, pe_s.value(f"s_d{l - 1}", i))
                        tt(sXT, sXT, ps[0:NS, 1, 0:2 * NS].rearrange("p (e f) -> p e f", f=NS), ALU.add)
                        tt(sX, sX, ps[0:NS, 1, 2 * NS:4 * NS].rearrange("p (e f) -> p e f", f=NS), ALU.add)
                    tt(sco, sL, unsq(lev(l, 0)[0:NS, 0:NS], 1, 2), ALU.mult)
                    tt(scoT, sLT, unsq(lev(l, 1)[0:NS, 0:NS], 1, 2), ALU.mult).then_inc(dve_s.at("s_gram" if l == 1 else f"s_X{l - 1}"), 1)
                dve.wait_ge(pe_s.sem, pe_s.value(f"s_d{SLEVELS - 1}", i))
                tt(sXT, sXT, ps[0:NS, 1, 0:2 * NS].rearrange("p (e f) -> p e f", f=NS), ALU.add).then_inc(dve_s.at(f"s_X{SLEVELS - 1}"), 1)
                dve.wait_ge(pe_s.sem, pe_s.value("s_RT", i))
                dve.tensor_copy(rT2, ps[:, 2, NS:2 * NS])
                dve.drain()
                tt(rT, ps[:, 2, 0:NS], rT2, ALU.add).then_inc(dve_s.at("s_RT"), 1)
                tt(v_exp, unsq(stok[:, 2, :], 1, SB), unsq(K.seq_of, 2, P), ALU.mult)
                dve.wait_ge(pe_s.sem, pe_s.value("s_Y", i))
                dve.tensor_copy(y_s[:, T:N], ps[:, 3, 0:NS])
                dve.drain()
                tt(y_s[:, T:N], y_s[:, T:N], ps[:, 3, NS:2 * NS], ALU.add).then_inc(dve_s.at("s_y"), 1)
                tt(u_exp, unsq(su_tok, 1, SB), unsq(K.seq_of, 2, P), ALU.mult).then_inc(dve_s.at("s_exp"), 1)
                dve.wait_ge(pe_s.sem, pe_s.value("mean", i))
                stt(out=halves(yc), in0=of_banks(ps, 0), scalar=-1.0 / HD, in1=halves(y_s),
                               op0=ALU.mult, op1=ALU.add).then_inc(dve_s.at("yc"), 1)
                dve.wait_ge(pe_s.sem, pe_s.value("s_S", i))
                for h in range(2):
                    hb = slice(4 * h, 4 * h + 4)
                    tt(s_prod[:, hb, :], ps[:, 6 + h, :].rearrange("p (b f) -> p b f", f=P), unsq(K.headones, 1, 4), ALU.mult)
                dve.drain()
                tt(s_state, s_state, s_prod, ALU.add)
                dve.drain()
                tt(s_state, s_state, unsq(esc[:, 3 * NB:3 * NB + SB], 2, P), ALU.mult).then_inc(dve_s.at("s_state"), 1)
                dve.wait_ge(act_s.sem, act_s.value("sd", i))
                dve.reciprocal(sd, sd)
                dve.drain()
                tt(yc, yc, sd, ALU.mult)
                dve.drain()
                ts(yc, yc, ln[:, 0:1], ln[:, 1:2], ALU.mult, ALU.add)
                dve.drain()
                tt(yc, yc, bon, ALU.add)
                dve.drain()
                tt(y_out[:, bass.ds(i, 1), :].squeeze(1), yc, g_s, ALU.mult).then_inc(dve_s.at("y"), 1)

        @block.gpsimd
        def _(pool):
            with pool.Fori(0, C) as i:
                pool.wait_ge(act_s.sem, act_s.value("gram_LT1", i))
                for l in range(1, LEVELS):
                    for e in range(2):
                        for name, dst, src, t in (("co", co, L, 0), ("coT", coT, LT, 1))[::both(l)]:
                            if l > 1:
                                pool.wait_ge(pe_s.sem, pe_s.value(f"{('y1', 'y2')[t]}{l - 1}_{e}", i))
                            pool.tensor_tensor(dst[e], src[:, e], unsq(lev(l, t), 1, NB), ALU.mult).then_inc(pool_s.at(f"{name}{l}_{e}"), 1)


def token_major(nc, K, src, dst):
    n = K.name()
    pe_s = Steps(K.sem(f"{n}_pe"), [f"turned{b}" for b in range(NB + 1)])
    act_s = Steps(K.sem(f"{n}_act"), [f"copied{b}" for b in range(NB + 1)])
    with nc.Block() as block:
        @block.tensor
        def _(pe):
            for b in range(NB + 1):
                m = P if b < NB else NS
                if b >= 2:
                    pe.wait_ge(act_s.sem, act_s.value(f"copied{b - 2}"))
                for c in range(C):
                    last = pe.transpose(K.ps[0:m, 2 * (b % 2) + c // 4, (c % 4) * P:(c % 4 + 1) * P],
                                        src[:, c, b * P:b * P + m], K.ident)
                last.then_inc(pe_s.at(f"turned{b}"), 1)

        @block.scalar
        def _(act):
            for b in range(NB + 1):
                m = P if b < NB else NS
                act.wait_ge(pe_s.sem, pe_s.value(f"turned{b}"))
                act.activation(dst[0:m, b, :].rearrange("p (a b) -> p a b", a=2),
                                          K.ps[0:m, 2 * (b % 2):2 * (b % 2) + 2, :], ACT.Copy).then_inc(act_s.at(f"copied{b}"), 1)


def add_token_major(nc, K, acc):
    n = K.name()
    pe_s = Steps(K.sem(f"{n}_pe"), [f"turned{b}" for b in range(NB + 1)])
    dve_s = Steps(K.sem(f"{n}_dve"), [f"added{b}" for b in range(NB + 1)])
    with nc.Block() as block:
        @block.tensor
        def _(pe):
            for b in range(NB + 1):
                m = P if b < NB else NS
                if b >= 2:
                    pe.wait_ge(dve_s.sem, dve_s.value(f"added{b - 2}"))
                for c in range(C):
                    last = pe.transpose(K.ps[:, 2 * (b % 2) + c // 4, (c % 4) * P:(c % 4) * P + m],
                                        acc[0:m, b, c * P:(c + 1) * P], K.ident[0:m, 0:m])
                last.then_inc(pe_s.at(f"turned{b}"), 1)

        @block.vector
        def _(dve):
            for b in range(NB + 1):
                m = P if b < NB else NS
                dve.wait_ge(pe_s.sem, pe_s.value(f"turned{b}"))
                for h in range(2):
                    dst = K.x[:, 4 * h:4 * h + 4, b * P:b * P + m]
                    last = dve.tensor_tensor(dst, dst, K.ps[:, 2 * (b % 2) + h, :].rearrange(
                        "p (c t) -> p c t", t=P)[:, :, 0:m], ALU.add)
                last.then_inc(dve_s.at(f"added{b}"), 1)


def peer(nc, K, I, layer, h, h_tok, acc, R):
    n = f"peer{layer}"
    RING = 8
    NU = NB + 1
    rows = [P] * NB + [NS]
    uring, vring = R.cut(RING, D), R.cut(RING, D)
    diag = R.cut(TOPK, P)
    q_sb, s_sb = R.cut(2, N), R.cut(NU, 2 * NKEYS)
    swork = R.cut(NKEYS)
    top_v, top_i = R.cut(2, TOPK), R.cut(2, TOPK, dtype=U32)
    top_f = R.cut(2, TOPK)
    cand, cwork = R.cut(TOPK * TOPK), R.cut(TOPK * TOPK)
    best_v, best_p = R.cut(NU, TOPK), R.cut(TOPK, dtype=U32)
    pos_u, pos_f = R.cut(2, TOPK, dtype=U32), R.cut(2, TOPK)
    hit = R.cut(2, TOPK, TOPK)
    part = R.cut(2, TOPK)
    idx_f, idx = R.cut(TOPK), R.cut(NU, TOPK, dtype=U32)
    neg_max, gate, gate_sum, gate_inv = R.cut(NU), R.cut(NU, TOPK), R.cut(NU), R.cut(1)
    dots, gelu, coef = R.cut(TOPK), R.cut(TOPK), R.cut(TOPK)
    spare = R.cut(2)

    wl = [K.sem(f"{n}_w{j}") for j in range(2)]
    u_here = [K.sem(f"{n}_u_here{j}") for j in range(RING)]
    v_here = [K.sem(f"{n}_v_here{j}") for j in range(RING)]
    u_free, v_free = K.sem(f"{n}_u_free"), K.sem(f"{n}_v_free")
    index_ready, keys_used, diag_ready = K.sem(f"{n}_index"), K.sem(f"{n}_keys"), K.sem(f"{n}_diag")
    LEAD = 3
    nxt = lambda b: (b + 1) % NU
    pick = lambda b: (b + LEAD) % NU

    def passes(sem, before, body, after):
        return (Steps(sem, before), Steps(sem, body, start=len(before)),
                Steps(sem, after, start=len(before) + (HEADS - 1) * len(body)))

    pe_p = passes(K.sem(f"{n}_pe"), ["q0", "q1", "s"], ["v0", "q0", "v1", "q1", "s", "v2", "v3", "v4"],
                  [f"v{b}" for b in range(NU)])
    act_p = passes(K.sem(f"{n}_act"), ["q0", "q1", "s", "exp0", "exp1", "gelu0", "exp2"],
                   ["gelu1", "exp3", "q0", "gelu2", "exp4", "q1", "s"]
                   + [x for b in range(2, NU) for x in (f"gelu{nxt(b)}", f"exp{pick(b)}")],
                   ["gelu1", "exp3", "gelu2", "exp4", "gelu3", "gelu4"])
    dve_p = passes(K.sem(f"{n}_dve"), ["top0", "top1", "coef0", "top2"],
                   [x for b in range(NU) for x in (f"acc{b}", f"coef{nxt(b)}", f"top{pick(b)}")],
                   ["acc0", "coef1", "top3", "acc1", "coef2", "top4", "acc2", "coef3", "acc3", "coef4", "acc4"])
    s_bank = ((6, 0, 2), (7, 2, 2), (2, 4, 1))
    ps = K.ps

    with nc.Block() as block:
        @block.sync
        def _(sp):
            for j in range(2):
                sp.dma_start(K.w9[j], I["w_q"][layer, j]).then_inc(wl[j], 16)
            with sp.Fori(1, HEADS) as i:
                sp.wait_ge(keys_used, i)
                for j in range(2):
                    sp.dma_start(K.w9[j], I["w_q"][layer, bass.ds(i * 2 + j, 1)].squeeze(0)).then_inc(wl[j], 16)

        @block.gpsimd
        def _(pool):
            pool.memset(spare[:, 0:1], 0.0).then_inc(u_free, RING)
            pool.memset(spare[:, 1:2], 0.0).then_inc(v_free, RING)

            def gather(i, b, j, ring, here, free, table):
                m = rows[b % NU]
                pool.wait_ge(free, i * (NU * TOPK) + (b * TOPK + j + 1))
                pool.nop(nofuse=True)
                pool.indirect_dma_start(ring[0:m, j % RING, :], None, table,
                                        bass.IndirectOffsetOnAxis(ap=idx[0:m, b % NU, j:j + 1], axis=0)
                                        ).then_inc(here[j % RING], 16)

            of_u, of_v = (uring, u_here, u_free, I["u"][layer]), (vring, v_here, v_free, I["v"][layer])
            pool.wait_ge(index_ready, 1)
            for j in range(TOPK):
                gather(0, 0, j, *of_u)
            with pool.Fori(0, HEADS - 1) as i:
                for b in range(NU):
                    pool.wait_ge(index_ready, i * NU + (b + 2))
                    for j in range(TOPK):
                        gather(i, b, j, *of_v)
                        gather(i, b + 1, j, *of_u)
            for b in range(NU):
                if b < NU - 1:
                    pool.wait_ge(index_ready, (HEADS - 1) * NU + (b + 2))
                for j in range(TOPK):
                    gather(HEADS - 1, b, j, *of_v)
                    if b < NU - 1:
                        gather(HEADS - 1, b + 1, j, *of_u)

        @block.tensor
        def _(pe):
            def query(S, j, head):
                pe.wait_ge(wl[j], head * 16 + 16)
                for s in range(2):
                    for k in range(C):
                        last = pe.matmul(ps[:, 2 + 2 * j + s, 0:HALF], K.w9[j][:, k, :],
                                         h[:, k, s * HALF:(s + 1) * HALF], start=k == 0, stop=k == C - 1)
                last.then_inc(S.at(f"q{j}"), 1)

            def scores(S, A, i):
                pe.wait_ge(A.sem, A.value("q1", i))
                for bank, b0, nb in s_bank:
                    for b in range(b0, b0 + nb):
                        m = rows[b]
                        for j in range(2):
                            col = ((b - b0) * 2 + j) * NKEYS
                            last = pe.matmul(ps[0:m, bank, col:col + NKEYS], q_sb[:, j, b * P:b * P + m],
                                             K.w9[j][:, C, :], start=True, stop=True)
                last.then_inc(keys_used, 1)
                pe.drain().then_inc(S.at("s"), 1)

            def combine(S, i, b):
                m = rows[b]
                for j in range(TOPK):
                    pe.wait_ge(diag_ready, i * (NU * TOPK) + (b * TOPK + j + 1))
                    pe.wait_ge(v_here[j % RING], i * (2 * NU * 16) + (2 * b + j // RING + 1) * 16)
                    if m < P:
                        pe.nop(nofuse=True)
                    for s in range(2):
                        last = pe.matmul(ps[0:m, s, :], diag[0:m, j, 0:m],
                                         vring[0:m, j % RING, s * 512:(s + 1) * 512],
                                         start=j == 0, stop=j == TOPK - 1)
                    last.then_inc(v_free, 1)
                pe.drain().then_inc(S.at(f"v{b}"), 1)

            query(pe_p[0], 0, 0)
            query(pe_p[0], 1, 0)
            scores(pe_p[0], act_p[0], 0)
            with pe.Fori(0, HEADS - 1) as i:
                combine(pe_p[1], i, 0)
                query(pe_p[1], 0, i + 1)
                combine(pe_p[1], i, 1)
                query(pe_p[1], 1, i + 1)
                scores(pe_p[1], act_p[1], i)
                for b in range(2, NU):
                    combine(pe_p[1], i, b)
            for b in range(NU):
                combine(pe_p[2], HEADS - 1, b)

        @block.scalar
        def _(act):
            def query(S, Q, i, j):
                act.wait_ge(Q.sem, Q.value(f"q{j}", i))
                act.activation(halves(q_sb[:, j, :]), of_banks(ps, 2 + 2 * j), ACT.Copy).then_inc(S.at(f"q{j}"), 1)

            def scores(S, Q, i):
                act.wait_ge(Q.sem, Q.value("s", i))
                for bank, b0, nb in s_bank:
                    m = rows[b0]
                    last = act.activation(s_sb[0:m, b0:b0 + nb, :], ps[0:m, bank, 0:nb * 2 * NKEYS].rearrange(
                        "p (b f) -> p b f", b=nb), ACT.Copy)
                last.then_inc(S.at("s"), 1)

            def softmax(S, V, i, b):
                m = rows[b]
                act.wait_ge(V.sem, V.value(f"top{b}", i))
                act.activation(gate[0:m, b, :], best_v[0:m, b, :], ACT.Exp, bias=neg_max[0:m, b:b + 1],
                                      accum_out=gate_sum[0:m, b:b + 1]).then_inc(S.at(f"exp{b}"), 1)

            def diagonals(V, a, b):
                m = rows[b]
                act.wait_ge(V.sem, V.value(f"coef{b}", a))
                for j in range(TOPK):
                    act.activation(diag[0:m, j, 0:m], K.ident[0:m, 0:m], ACT.Copy,
                                   scale=coef[0:m, j:j + 1]).then_inc(diag_ready, 1)

            def activate(S, i, b):
                m = rows[b % NU]
                act.wait_ge(u_free, i * (NU * TOPK) + ((b + 1) * TOPK + RING))
                act.activation(gelu[0:m, :], dots[0:m, :], ACT.Gelu).then_inc(S.at(f"gelu{b % NU}"), 1)

            query(act_p[0], pe_p[0], 0, 0)
            query(act_p[0], pe_p[0], 0, 1)
            scores(act_p[0], pe_p[0], 0)
            softmax(act_p[0], dve_p[0], 0, 0)
            softmax(act_p[0], dve_p[0], 0, 1)
            activate(act_p[0], 0, 0)
            diagonals(dve_p[0], 0, 0)
            softmax(act_p[0], dve_p[0], 0, 2)
            with act.Fori(0, HEADS - 1) as i:
                for b in range(NU):
                    activate(act_p[1], i, b + 1)
                    diagonals(dve_p[1], i, nxt(b))
                    softmax(act_p[1], dve_p[1], i, pick(b))
                    if b < 2:
                        query(act_p[1], pe_p[1], i, b)
                    if b == 1:
                        scores(act_p[1], pe_p[1], i)
            for b in range(1, NU):
                activate(act_p[2], HEADS - 1, b)
                diagonals(dve_p[2], 0, b)
                if b - 1 < NU - LEAD:
                    softmax(act_p[2], dve_p[2], 0, pick(b - 1))

        @block.vector
        def _(dve):
            tt, ts, stt = dve.tensor_tensor, dve.tensor_scalar, dve.scalar_tensor_tensor

            def top16(values, work, out_v, out_i):
                dve.max(out_v[:, 0:8], values)
                dve.drain()
                dve.max_index(out_i[:, 0:8], out_v[:, 0:8], values)
                dve.match_replace(out=work, in_to_replace=out_v[:, 0:8], in_values=values, imm_value=LOWEST)
                dve.drain()
                dve.max(out_v[:, 8:16], work)
                dve.drain()
                dve.max_index(out_i[:, 8:16], out_v[:, 8:16], work)

            def choose(S, b):
                m = rows[b]
                for j in range(2):
                    top16(s_sb[0:m, b, j * NKEYS:(j + 1) * NKEYS], swork[0:m], top_v[0:m, j, :], top_i[0:m, j, :])
                    dve.drain()
                dve.tensor_copy(top_f[0:m], top_i[0:m])
                tt(cand[0:m].rearrange("p (a b) -> p a b", b=TOPK), unsq(top_v[0:m, 0, :], 2, TOPK),
                   unsq(top_v[0:m, 1, :], 1, TOPK), ALU.add)
                dve.drain()
                top16(cand[0:m], cwork[0:m], best_v[0:m, b, :], best_p[0:m])
                dve.drain()
                ts(neg_max[0:m, b:b + 1], best_v[0:m, b, 0:1], -1.0, None, ALU.mult).then_inc(S.at(f"top{b}"), 1)
                ts(pos_u[0:m, 0, :], best_p[0:m], 4, None, ALU.logical_shift_right)
                ts(pos_u[0:m, 1, :], best_p[0:m], TOPK - 1, None, ALU.bitwise_and)
                dve.drain()
                dve.tensor_copy(pos_f[0:m], pos_u[0:m])
                dve.drain()
                for j in range(2):
                    tt(hit[0:m, j], unsq(pos_f[0:m, j, :], 2, TOPK), unsq(K.iota[0:m], 1, TOPK), ALU.is_equal)
                dve.drain()
                for j in range(2):
                    tt(hit[0:m, j], hit[0:m, j], unsq(top_f[0:m, j, :], 1, TOPK), ALU.mult)
                dve.drain()
                dve.tensor_reduce(out=part[0:m], in_=hit[0:m], op=ALU.add, axis=AX.X)
                dve.drain()
                stt(out=idx_f[0:m], in0=part[0:m, 0, :], scalar=float(NKEYS), in1=part[0:m, 1, :],
                    op0=ALU.mult, op1=ALU.add)
                dve.drain()
                dve.tensor_copy(idx[0:m, b, :], idx_f[0:m]).then_inc(index_ready, 1)

            def dot(i, b):
                m = rows[b % NU]
                for j in range(TOPK):
                    dve.wait_ge(u_here[j % RING], i * (2 * NU * 16) + (2 * b + j // RING + 1) * 16)
                    row = uring[0:m, j % RING, :]
                    stt(out=row, in0=row, scalar=1.0, in1=h_tok[0:m, b % NU, :], op0=ALU.mult, op1=ALU.mult,
                        accum_out=dots[0:m, j:j + 1]).then_inc(u_free, 1)

            def weigh(S, A, a, b):
                m = rows[b]
                dve.reciprocal(gate_inv[0:m], gate_sum[0:m, b:b + 1])
                dve.drain()
                dve.wait_ge(A.sem, A.value(f"gelu{b}", a))
                stt(out=coef[0:m], in0=gate[0:m, b, :], scalar=gate_inv[0:m], in1=gelu[0:m],
                    op0=ALU.mult, op1=ALU.mult).then_inc(S.at(f"coef{b}"), 1)

            def add(S, Q, a, b):
                m = rows[b]
                dve.wait_ge(Q.sem, Q.value(f"v{b}", a))
                dst = acc[0:m, b, :].rearrange("p (a b) -> p a b", a=2)
                tt(dst, dst, ps[0:m, 0:2, :], ALU.add).then_inc(S.at(f"acc{b}"), 1)

            dve.memset(acc, 0.0)
            dve.wait_ge(act_p[0].sem, act_p[0].value("s"))
            dve.drain()
            choose(dve_p[0], 0)
            choose(dve_p[0], 1)
            dot(0, 0)
            dve.wait_ge(act_p[0].sem, act_p[0].value("exp0"))
            weigh(dve_p[0], act_p[0], 0, 0)
            choose(dve_p[0], 2)
            with dve.Fori(0, HEADS - 1) as i:
                for b in range(NU):
                    dot(i, b + 1)
                    add(dve_p[1], pe_p[1], i, b)
                    weigh(dve_p[1], act_p[1], i, nxt(b))
                    if pick(b) == 0:
                        dve.wait_ge(act_p[1].sem, act_p[1].value("s", i))
                        dve.nop(nofuse=True)
                    choose(dve_p[1], pick(b))
            for b in range(NU):
                if b < NU - 1:
                    dot(HEADS - 1, b + 1)
                add(dve_p[2], pe_p[2], 0, b)
                if b < NU - 1:
                    weigh(dve_p[2], act_p[2], 0, b + 1)
                if b < NU - LEAD:
                    choose(dve_p[2], pick(b))


def conv(nc, K, I, h, cv, R):
    PE_TAPS = 16
    up, us = R.cut(PAST + T), R.cut(SB, PAST + ST)
    sg, prm, diags = R.cut(N), R.cut(NPAR), R.cut(PE_TAPS, P)
    wl = [K.sem(f"conv_w{j}") for j in range(2)]
    small, stored, zeroed = K.sem("conv_small"), K.sem("conv_stored"), K.sem("conv_zeroed")
    pe_s = Steps(K.sem("conv_pe"), ["a", "g", "taps"], start=1)
    act_s = Steps(K.sem("conv_act"), ["gate", "diags"], start=1)
    dve_s = Steps(K.sem("conv_dve"), ["u", "sum"], start=1)
    ps = K.ps
    with nc.Block() as block:
        @block.sync
        def _(sp):
            sp.sem_inc(stored, 16)
            sp.wait_ge(zeroed, 1)
            with sp.Fori(0, C) as i:
                sp.wait_ge(pe_s.sem, pe_s.all_before(i))
                for j in range(2):
                    sp.dma_start(K.w[j], I["w_pw1"][bass.ds(i * 2 + j, 1)].squeeze(0)).then_inc(wl[j], 16)
                sp.wait_ge(dve_s.sem, dve_s.all_before(i))
                sp.wait_ge(act_s.sem, act_s.all_before(i))
                sp.wait_ge(stored, i * 32 + 16)
                sp.dma_start(prm, I["cpar"][bass.ds(i, 1)].squeeze(0)).then_inc(small, 16)
                sp.dma_start(us[:, :, 0:PAST], I["state_conv"][bass.ds(i, 1)].squeeze(0)).then_inc(small, 16)
                sp.wait_ge(dve_s.sem, dve_s.value("u", i))
                sp.dma_start(I["o_conv_p"][bass.ds(i, 1)].squeeze(0), up[:, T:T + PAST]).then_inc(stored, 16)
                sp.dma_start(I["o_conv_s"][bass.ds(i, 1)].squeeze(0), us[:, :, ST:ST + PAST]).then_inc(stored, 16)
            sp.wait_ge(stored, C * 32 + 16)

        @block.tensor
        def _(pe):
            pe_s.begin(pe)
            with pe.Fori(0, C) as i:
                pe.wait_ge(dve_s.sem, dve_s.all_before(i))
                for j, name in enumerate(("a", "g")):
                    pe.wait_ge(wl[j], i * 16 + 16)
                    for s in range(2):
                        for k in range(C):
                            last = pe.matmul(ps[:, 2 * j + s, 0:HALF], K.w[j][:, k, :], h[:, k, s * HALF:(s + 1) * HALF],
                                             start=k == 0, stop=k == C - 1)
                    last.then_inc(pe_s.at(name), 1)
                pe.wait_ge(act_s.sem, act_s.value("diags", i))
                pe.wait_ge(dve_s.sem, dve_s.value("u", i))
                for k in range(PE_TAPS):
                    pe.matmul(ps[:, 4, :], diags[:, k, :], up[:, k:k + T], start=k == 0, stop=k == PE_TAPS - 1)
                    last = pe.matmul(ps[:, 5, 0:NS], diags[:, k, :], us[:, :, k:k + ST], start=k == 0, stop=k == PE_TAPS - 1)
                last.then_inc(pe_s.at("taps"), 1)

        @block.scalar
        def _(act):
            act_s.begin(act)
            with act.Fori(0, C) as i:
                act.wait_ge(small, i * 32 + 32)
                act.wait_ge(dve_s.sem, dve_s.all_before(i))
                act.wait_ge(pe_s.sem, pe_s.value("g", i))
                act.activation(halves(sg), of_banks(ps, 2), ACT.Sigmoid, bias=prm[:, B_PG:B_PG + 1]).then_inc(act_s.at("gate"), 1)
                for k in range(PE_TAPS):
                    last = act.activation(diags[:, k, :], K.ident, ACT.Copy, scale=prm[:, TAP0 + k:TAP0 + k + 1])
                last.then_inc(act_s.at("diags"), 1)

        @block.vector
        def _(dve):
            dve_s.begin(dve)
            stt = dve.scalar_tensor_tensor
            dve.memset(up[:, 0:PAST], 0.0).then_inc(zeroed, 1)
            with dve.Fori(0, C) as i:
                dve.wait_ge(small, i * 32 + 32)
                dve.wait_ge(stored, i * 32 + 16)
                dve.wait_ge(pe_s.sem, pe_s.all_before(i))
                dve.wait_ge(act_s.sem, act_s.value("gate", i))
                one = dict(scalar=prm[:, B_PA:B_PA + 1], op0=ALU.add, op1=ALU.mult)
                stt(out=up[:, PAST:PAST + HALF], in0=ps[:, 0, 0:HALF], in1=sg[:, 0:HALF], **one)
                stt(out=up[:, PAST + HALF:], in0=ps[:, 1, 0:T - HALF], in1=sg[:, HALF:T], **one)
                stt(out=us[:, :, PAST:], in0=ps[:, 1, T - HALF:HALF].rearrange("p (b t) -> p b t", t=ST),
                               in1=sg[:, T:N].rearrange("p (b t) -> p b t", t=ST), **one).then_inc(dve_s.at("u"), 1)
                dve.drain()
                outp = cv[:, bass.ds(i, 1), 0:T].squeeze(1)
                outs = cv[:, bass.ds(i, 1), T:N].squeeze(1).rearrange("p (b t) -> p b t", t=ST)
                for k in range(PE_TAPS, TAPS):
                    w = prm[:, TAP0 + k:TAP0 + k + 1]
                    for o, u in ((outp, up[:, k:k + T]), (outs, us[:, :, k:k + ST])):
                        if k == PE_TAPS:
                            dve.tensor_scalar(o, u, w, prm[:, B_DW:B_DW + 1], ALU.mult, ALU.add)
                        else:
                            stt(out=o, in0=u, scalar=w, in1=o, op0=ALU.mult, op1=ALU.add)
                    dve.drain()
                dve.wait_ge(pe_s.sem, pe_s.value("taps", i))
                dve.tensor_tensor(outp, outp, ps[:, 4, :], ALU.add)
                dve.tensor_tensor(outs, outs, ps[:, 5, 0:NS].rearrange("p (b t) -> p b t", t=ST), ALU.add).then_inc(dve_s.at("sum"), 1)


def layernorm_silu(nc, K, v, w):
    act_s = Steps(K.sem("ln_act"), [f"square{c}" for c in range(C)] + ["root"])
    pe_s = Steps(K.sem("ln_pe"), ["sum"] + [f"summed{c}" for c in range(C)])
    dve_s = Steps(K.sem("ln_dve"), [f"centred{c}" for c in range(C)] + [f"scaled{c}" for c in range(C)])
    sq = [K.small[:, 0:N], K.small[:, N:2 * N]]
    mean, root = K.small[:, 2 * N:3 * N], K.small[:, 3 * N:4 * N]
    with nc.Block() as block:
        @block.tensor
        def _(pe):
            for h in range(2):
                for c in range(C):
                    last = pe.matmul(K.ps[:, h, 0:HALF], K.ones, v[:, c, h * HALF:(h + 1) * HALF],
                                     start=c == 0, stop=c == C - 1)
            last.then_inc(pe_s.at("sum"), 1)
            for c in range(C):
                pe.wait_ge(act_s.sem, act_s.value(f"square{c}"))
                for h in range(2):
                    last = pe.matmul(K.ps[:, 2 + h, 0:HALF], K.ones, sq[c % 2][:, h * HALF:(h + 1) * HALF],
                                     start=c == 0, stop=c == C - 1)
                last.then_inc(pe_s.at(f"summed{c}"), 1)

        @block.vector
        def _(dve):
            dve.wait_ge(pe_s.sem, pe_s.value("sum"))
            dve.tensor_scalar(halves(mean), of_banks(K.ps, 0), 1.0 / D, None, ALU.mult)
            dve.drain()
            for c in range(C):
                dve.tensor_tensor(v[:, c, :], v[:, c, :], mean, ALU.subtract).then_inc(dve_s.at(f"centred{c}"), 1)
            dve.wait_ge(act_s.sem, act_s.value("root"))
            dve.reciprocal(root, root)
            dve.drain()
            for c in range(C):
                dve.tensor_tensor(v[:, c, :], v[:, c, :], root, ALU.mult).then_inc(dve_s.at(f"scaled{c}"), 1)

        @block.scalar
        def _(act):
            for c in range(C):
                act.wait_ge(dve_s.sem, dve_s.value(f"centred{c}"))
                if c >= 2:
                    act.wait_ge(pe_s.sem, pe_s.value(f"summed{c - 2}"))
                act.activation(sq[c % 2], v[:, c, :], ACT.Square).then_inc(act_s.at(f"square{c}"), 1)
            act.wait_ge(pe_s.sem, pe_s.value(f"summed{C - 1}"))
            act.activation(halves(root), of_banks(K.ps, 2), ACT.Sqrt, bias=K.eps[:, 2:3], scale=1.0 / D).then_inc(act_s.at("root"), 1)
            for c in range(C):
                act.wait_ge(dve_s.sem, dve_s.value(f"scaled{c}"))
                act.activation(v[:, c, :], v[:, c, :], ACT.Silu, bias=K.par[:, CLN_B, c:c + 1],
                               scale=K.par[:, CLN_G, c:c + 1])


class Kernel:

    def __init__(self, nc, ctx):
        self.nc, self.ctx, self.phases = nc, ctx, 0
        sb = lambda name, shape: ctx.enter_context(nc.sbuf_tensor(name, shape, F32))[tuple(slice(None) for _ in shape)]
        self.x = sb("x", [P, C, N])
        self.par = sb("par", [P, NPAR, C])
        self.cst = sb("cst", [P, CST_COLS])
        self.level = sb("level", [P, 2 * LEVELS, P])
        self.wbuf = sb("wbuf", [P, 3 * (C + 1), P])
        self.eps = sb("eps", [P, 3])
        self.bias_cols = sb("bias_cols", [P, 2])
        self.arena = sb("arena", [P, ARENA])
        self.ps = ctx.enter_context(nc.psum_tensor("psum", [P, 8, 512], F32))[:, :, :]
        cut = Region(self.cst)
        self.ident, self.ones, self.headones = cut.cut(P), cut.cut(P), cut.cut(P)
        self.m_before, self.m_upto = cut.cut(P), cut.cut(P)
        self.ms_before, self.ms_upto = cut.cut(NS, parts=NS), cut.cut(NS, parts=NS)
        self.seq_of, self.iota, self.reset = cut.cut(SB, parts=NS), cut.cut(TOPK), cut.cut(N)
        self.w9 = [self.wbuf[:, j * (C + 1):(j + 1) * (C + 1), :] for j in range(3)]
        self.w = [w[:, 0:C, :] for w in self.w9]

    def sem(self, name):
        return self.ctx.enter_context(self.nc.semaphore(name))

    def name(self):
        self.phases += 1
        return f"phase{self.phases}"


ARENA = 41450
CST_COLS = 5 * P + 2 * NS + SB + TOPK + N


def build(nc, I):
    with ExitStack() as ctx:
        K = Kernel(nc, ctx)
        base = C * N
        h = Region(K.arena, 0).cut(C, N)
        work = base
        K.small = K.arena[:, ARENA - 4 * N:ARENA]
        load_constants(nc, K, I)

        rmsnorm(nc, K, NMIX0, h)
        R = Region(K.arena, work)
        xm = [R.cut(C, N) for _ in range(3)]
        hid_wa, hid_g = R.cut(N), R.cut(N)
        X = Region(K.arena, R.at)
        xx = X.cut(C, N)
        K.low, K.shift, K.new_shift = X.cut(C, 2 * P), X.cut(C, SB), X.cut(C, 1 + SB)
        time_mix_inputs(nc, K, I, h, xx, xm, hid_wa, hid_g)
        wkv(nc, K, I, xm, h, hid_wa, hid_g, R)
        linear_into_x(nc, K, I["w_o"], h)

        for layer, gain in ((0, NFFN0), (1, NFFN1)):
            if layer == 1:
                rmsnorm(nc, K, NMIX1, h)
                R = Region(K.arena, work)
                cv = R.cut(C, N)
                conv(nc, K, I, h, cv, R)
                layernorm_silu(nc, K, cv, None)
                linear_into_x(nc, K, I["w_pw2"], cv, bias=B_P2)
            rmsnorm(nc, K, gain, h)
            R = Region(K.arena, work)
            h_tok, acc = R.cut(NB + 1, D), R.cut(NB + 1, D)
            token_major(nc, K, h, h_tok)
            peer(nc, K, I, layer, h, h_tok, acc, R)
            add_token_major(nc, K, acc)
        rmsnorm(nc, K, NFIN, h, store=I["o_y"])


def constants():
    t, s = np.arange(P)[:, None], np.arange(P)[None, :]
    levels = []
    for l in range(LEVELS):
        m = ((t >> (l + 1)) == (s >> (l + 1))) & ((t >> l) % 2 == 1) & ((s >> l) % 2 == 0)
        levels += [m, m.T]
    tn, sn = np.arange(NS)[:, None], np.arange(NS)[None, :]
    same = (tn // ST) == (sn // ST)
    reset = np.ones(N)
    reset[0:T:P] = 0
    reset[T::ST] = 0
    parts = [np.eye(P), np.ones((P, P)), (t // HD) == (s // HD), t < s, t <= s,
             np.pad(same & (tn < sn), ((0, P - NS), (0, 0))), np.pad(same & (tn <= sn), ((0, P - NS), (0, 0))),
             np.pad((tn // ST) == np.arange(SB)[None, :], ((0, P - NS), (0, 0))),
             np.broadcast_to(np.arange(TOPK), (P, TOPK)), np.broadcast_to(reset, (P, N))]
    cst = np.concatenate([np.asarray(p, np.float32) for p in parts], axis=1)
    return cst, np.stack([np.asarray(m, np.float32) for m in levels], axis=1)


def kernel(**inputs):
    import concourse.bacc as bacc
    from concourse.bass_utils import run_bass_kernel_spmd

    a = {k: np.asarray(v) for k, v in inputs.items()}
    con = np.ascontiguousarray

    def chunks(w):
        return con(w.reshape(C, P, -1, P).transpose(2, 1, 0, 3))

    def feature_major(rows):
        return con(rows.reshape(-1, C, P).transpose(2, 1, 0))

    rows = [*a["rwkv_mu"][0], a["rwkv_w0"][0], a["rwkv_a0"][0], a["rwkv_k_k"][0], a["rwkv_k_a"][0],
            a["rwkv_r_k"][0].reshape(-1), a["rwkv_ln_w"][0], a["rwkv_ln_b"][0],
            a["conv_b_pw1"][0, :D], a["conv_b_pw1"][0, D:], a["conv_b_dw"][0], a["conv_ln_g"][0], a["conv_ln_b"][0],
            a["conv_b_pw2"][0], a["norm_mix"][0], a["norm_mix"][1], a["norm_ffn"][0], a["norm_ffn"][1],
            a["norm_final"], *a["conv_w_dw"][0]]
    par = np.stack(rows).reshape(NPAR, C, P)
    cst, level = constants()
    r, k, v = (chunks(a["rwkv_w_rkv"][0, j]) for j in range(3))
    low1 = np.concatenate([a["rwkv_w1"][0], a["rwkv_a1"][0], a["rwkv_g1"][0]], axis=1)
    low2 = np.concatenate([a["rwkv_w2"][0], a["rwkv_a2"][0], a["rwkv_g2"][0]], axis=0)
    pa, pg = chunks(a["conv_w_pw1"][0][:, :D]), chunks(a["conv_w_pw1"][0][:, D:])
    wq = []
    for j in range(2):
        keys = a["peer_sub_keys"][j].reshape(2 * HEADS, NKEYS, P).transpose(0, 2, 1)
        wq.append(np.concatenate([chunks(a["peer_w_q"][j]), keys[:, :, None, :]], axis=2))
    arrays = {
        "x": feature_major(np.concatenate([a["x_prompt"][0], a["x_sample"].reshape(NS, D)])),
        "par": con(par.transpose(2, 0, 1)),
        "cpar": con(par.transpose(1, 2, 0)),
        "cst": cst, "level": level,
        "shift": con(a["state_shift"][0].reshape(SB, C, P).transpose(2, 1, 0)),
        "low1": con(low1.reshape(C, P, 2 * P).transpose(1, 0, 2)),
        "low2": con(low2.reshape(2, P, C, P).transpose(2, 1, 0, 3)),
        "w_rkv": con(np.stack([r, k, v], axis=1).reshape(3 * C, P, C, P)),
        "w_o": chunks(a["rwkv_w_o"][0]),
        "w_pw1": con(np.stack([pa, pg], axis=1).reshape(2 * C, P, C, P)),
        "w_pw2": chunks(a["conv_w_pw2"][0]),
        "w_q": con(np.stack(wq)),
        "state": con(a["state_wkv"][0].reshape(SB, C, 2, HD, HD).transpose(1, 2, 4, 0, 3).reshape(C, P, SB, HD)),
        "state_conv": con(a["state_conv"][0].reshape(SB, PAST, C, P).transpose(2, 3, 0, 1)),
        "u0": a["peer_u"][0], "u1": a["peer_u"][1], "v0": a["peer_v"][0], "v1": a["peer_v"][1],
    }
    outs = {"o_y": (P, C, N), "o_shift": (P, C, 1 + SB), "o_wkv_p": (C, P, HD), "o_wkv_s": (C, P, SB, HD),
            "o_conv_p": (C, P, PAST), "o_conv_s": (C, P, SB, PAST)}
    nc = bacc.Bacc("TRN2", target_bir_lowering=False, num_devices=1)
    I = {k: nc.dram_tensor(f"in_{k}", v.shape, F32, kind="ExternalInput").ap() for k, v in arrays.items()}
    I |= {k: nc.dram_tensor(f"out_{k}", s, F32, kind="ExternalOutput").ap() for k, s in outs.items()}
    I["u"], I["v"] = (I["u0"], I["u1"]), (I["v0"], I["v1"])
    build(nc, I)
    got = run_bass_kernel_spmd(nc, [{f"in_{k}": con(v) for k, v in arrays.items()}], core_ids=[0]).results[0]
    y, shift, wp, ws, cp, cs = (np.asarray(got[f"out_{k}"]) for k in outs)
    tokens = y.transpose(2, 1, 0).reshape(N, D)
    rows_of = lambda s: s.transpose(2, 1, 0).reshape(-1, D)

    def states(w, b):
        return con(w.reshape(C, 2, HD, b, HD).transpose(3, 0, 1, 4, 2).reshape(1, b, 2 * C, HD, HD))

    return (con(tokens[:T])[None], con(tokens[T:]).reshape(SB, ST, D),
            states(wp, 1), con(rows_of(shift[:, :, 0:1]))[None],
            con(cp.transpose(2, 0, 1).reshape(1, 1, PAST, D)),
            states(ws, SB), con(rows_of(shift[:, :, 1:]))[None],
            con(cs.transpose(2, 3, 0, 1).reshape(1, SB, PAST, D)))
```

```python
import concourse.bass as bass
from concourse import mybir
from contextlib import ExitStack
import numpy as np

F32 = mybir.dt.float32
U32 = mybir.dt.uint32
ALU = mybir.AluOpType
ACT = mybir.ActivationFunctionType
AX = mybir.AxisListType

P = 128
D = 1024
C = D // P
T = 512
SB, ST = 8, 8
NS = SB * ST
N = T + NS
HALF = N // 2
NB = T // P
HD = 64
TAPS = 31
PAST = TAPS - 1
HEADS, TOPK, NKEYS = 8, 16, 128
KAPPA = float(np.exp(-0.5))
RMS_EPS, GN_EPS, LN_EPS = 1e-6, 6.4e-4, 1e-5
LEVELS = 7
SLEVELS = 3
LOWEST = -3.0e38

(MU0, W0, A0, K_K, K_A, R_K, LN_W, LN_B, B_PA, B_PG, B_DW, CLN_G, CLN_B, B_P2,
 NMIX0, NMIX1, NFFN0, NFFN1, NFIN, TAP0) = (0, 6, 7, 8, 9, 10, 11, 12, 13, 14, 15, 16, 17, 18,
                                            19, 20, 21, 22, 23, 24)
NPAR = TAP0 + TAPS


class Steps:

    def __init__(self, sem, names, start=0, a_pass_ahead=False):
        self.sem, self.names, self.next = sem, list(names), 0
        self.start = len(self.names) if a_pass_ahead else start

    def value(self, name, i=0):
        return i * len(self.names) + (self.start + self.names.index(name) + 1)

    def all_before(self, i):
        return i * len(self.names) + self.start

    def before(self, name, i):
        assert self.start == len(self.names)
        return i * len(self.names) + (self.names.index(name) + 1)

    def begin(self, engine):
        assert self.start and self.next == 0
        engine.sem_inc(self.sem, self.start)

    def at(self, name):
        assert self.names[self.next] == name, (name, self.names[self.next])
        self.next = (self.next + 1) % len(self.names)
        return self.sem


class Region:

    def __init__(self, tensor, at=0):
        self.tensor, self.at = tensor, at

    def cut(self, *shape, parts=P, dtype=F32):
        n = int(np.prod(shape))
        view = self.tensor[0:parts, self.at:self.at + n]
        self.at += n
        assert self.at <= self.tensor.shape[1], (self.at, self.tensor.shape)
        if dtype != F32:
            view = view.bitcast(dtype)
        if len(shape) == 2:
            view = view.rearrange("p (a b) -> p a b", b=shape[1])
        if len(shape) == 3:
            view = view.rearrange("p (a b c) -> p a b c", b=shape[1], c=shape[2])
        return view


def halves(view):
    return view.rearrange("p (a b) -> p a b", b=HALF)


def of_banks(psum, bank, parts=slice(0, P)):
    return psum[parts, bank:bank + 2, 0:HALF]


def unsq(view, axis, n):
    return view.unsqueeze(axis).to_broadcast(list(view.shape[:axis]) + [n] + list(view.shape[axis:]))


def rmsnorm(nc, K, gain, out, store=None, ahead=()):
    n = K.name()
    act_s = Steps(K.sem(f"{n}_act"), [f"square{c}" for c in range(C)] + ["root"])
    pe_s = Steps(K.sem(f"{n}_pe"), [f"summed{c}" for c in range(C)])
    dve_s = Steps(K.sem(f"{n}_dve"), [f"scaled{c}" for c in range(C)])
    stored = K.sem(f"{n}_stored")
    sq = [K.small[:, 0:N], K.small[:, N:2 * N]]
    root, inv = K.small[:, 2 * N:3 * N], K.small[:, 3 * N:4 * N]
    with nc.Block() as block:
        @block.scalar
        def _(act):
            for c in range(C):
                if c >= 2:
                    act.wait_ge(pe_s.sem, pe_s.value(f"summed{c - 2}"))
                act.activation(sq[c % 2], K.x[:, c, :], ACT.Square).then_inc(act_s.at(f"square{c}"), 1)
            act.wait_ge(pe_s.sem, pe_s.value(f"summed{C - 1}"))
            act.activation(halves(root), of_banks(K.ps, 0), ACT.Sqrt,
                                      bias=K.eps[:, 0:1], scale=1.0 / D).then_inc(act_s.at("root"), 1)

        @block.tensor
        def _(pe):
            for c in range(C):
                pe.wait_ge(act_s.sem, act_s.value(f"square{c}"))
                for h in range(2):
                    last = pe.matmul(K.ps[:, h, 0:HALF], K.ones, sq[c % 2][:, h * HALF:(h + 1) * HALF],
                                     start=c == 0, stop=c == C - 1)
                last.then_inc(pe_s.at(f"summed{c}"), 1)

        @block.vector
        def _(dve):
            dve.wait_ge(act_s.sem, act_s.value("root"))
            dve.reciprocal(inv, root)
            dve.drain()
            for c in range(C):
                dve.scalar_tensor_tensor(out=out[:, c, :], in0=K.x[:, c, :],
                                                    scalar=K.par[:, gain, c:c + 1], in1=inv,
                                                    op0=ALU.mult, op1=ALU.mult).then_inc(dve_s.at(f"scaled{c}"), 1)

        @block.sync
        def _(sp):
            for buffer, source, loaded in ahead:
                sp.dma_start(buffer, source).then_inc(loaded, 16)
            if store is not None:
                for c in range(C):
                    sp.wait_ge(dve_s.sem, dve_s.value(f"scaled{c}"))
                    sp.dma_start(store[:, c, :], out[:, c, :]).then_inc(stored, 16)
                sp.wait_ge(stored, 16 * C)


def linear_into_x(nc, K, weights, src, loaded, bias=None):
    n = K.name()
    pe_s = Steps(K.sem(f"{n}_pe"), ["product0", "product1"])
    dve_s = Steps(K.sem(f"{n}_dve"), ["added0", "added1"], a_pass_ahead=True)
    with nc.Block() as block:
        @block.sync
        def _(sp):
            with sp.Fori(1, C // 2) as i:
                for j in range(2):
                    sp.wait_ge(pe_s.sem, i * 2 + (j - 1))
                    sp.dma_start(K.w[j], weights[bass.ds(i * 2 + j, 1)].squeeze(0)).then_inc(loaded[j], 16)

        @block.tensor
        def _(pe):
            with pe.Fori(0, C // 2) as i:
                for j in range(2):
                    pe.wait_ge(dve_s.sem, dve_s.before(f"added{j}", i))
                    pe.wait_ge(loaded[j], i * 16 + 16)
                    for h in range(2):
                        for k in range(C):
                            last = pe.matmul(K.ps[:, 2 * j + h, 0:HALF], K.w[j][:, k, :],
                                             src[:, k, h * HALF:(h + 1) * HALF],
                                             start=k == 0, stop=k == C - 1)
                    last.then_inc(pe_s.at(f"product{j}"), 1)

        @block.vector
        def _(dve):
            dve_s.begin(dve)
            with dve.Fori(0, C // 2) as i:
                for j in range(2):
                    dve.wait_ge(pe_s.sem, pe_s.value(f"product{j}", i))
                    dst = K.x[:, bass.ds(i * 2 + j, 1), :].squeeze(1).rearrange("p (a b) -> p a b", b=HALF)
                    add = K.bias_cols[:, j:j + 1] if bias is not None else 0.0
                    if bias is not None:
                        dve.tensor_copy(add, K.par[:, bias, bass.ds(i * 2 + j, 1)])
                        dve.drain()
                    dve.scalar_tensor_tensor(out=dst, in0=of_banks(K.ps, 2 * j), scalar=add,
                                                        in1=dst, op0=ALU.add, op1=ALU.add).then_inc(dve_s.at(f"added{j}"), 1)


def load_constants(nc, K, I):
    loaded = K.sem("constants_loaded")
    with nc.Block() as block:
        @block.sync
        def _(sp):
            pairs = [(K.x, I["x"]), (K.par, I["par"]), (K.cst, I["cst"]), (K.level, I["level"])]
            for dst, src in pairs:
                sp.dma_start(dst, src).then_inc(loaded, 16)
            sp.wait_ge(loaded, 16 * len(pairs))

        @block.gpsimd
        def _(pool):
            for j, eps in enumerate((RMS_EPS, GN_EPS, LN_EPS)):
                pool.memset(K.eps[:, j:j + 1], eps)


def time_mix_inputs(nc, K, I, h, xx, xm, hid_wa, hid_g, loaded):
    n = "mix"
    low, shift = K.low, K.shift
    stored, rows_ready = K.sem(f"{n}_stored"), K.sem(f"{n}_rows_ready")
    new_shift = K.new_shift
    mixes = [f"mixed{m}_{k}" for m in (3, 4, 5) for k in range(C)]
    dve_s = Steps(K.sem(f"{n}_dve"), mixes)
    pe_s = Steps(K.sem(f"{n}_pe"), [f"used{m}_{k}" for m in (3, 4, 5) for k in range(C)])
    tmp = [K.small[:, 0:N], K.small[:, N:2 * N]]
    with nc.Block() as block:
        @block.sync
        def _(sp):
            sp.wait_ge(rows_ready, 1)
            sp.dma_start(I["o_shift"], new_shift).then_inc(stored, 16)
            sp.wait_ge(stored, 16)

        @block.vector
        def _(dve):
            dve.wait_ge(loaded, 32)
            hs, xs = (v[:, :, T:N].rearrange("p c (b t) -> p c b t", t=ST) for v in (h, xx))
            dve.tensor_tensor(xx[:, :, 1:T], h[:, :, 0:T - 1], h[:, :, 1:T], ALU.subtract)
            dve.tensor_scalar(xx[:, :, 0:1], h[:, :, 0:1], -1.0, None, ALU.mult)
            dve.tensor_tensor(xs[:, :, :, 0], shift, hs[:, :, :, 0], ALU.subtract)
            for c in range(C):
                dve.tensor_tensor(xs[:, c, :, 1:ST], hs[:, c, :, 0:ST - 1], hs[:, c, :, 1:ST], ALU.subtract)
            dve.drain()
            q = 0
            for m in (3, 4, 5):
                for k in range(C):
                    if q >= 2:
                        dve.wait_ge(pe_s.sem, q - 1)
                    dve.scalar_tensor_tensor(out=tmp[q % 2], in0=xx[:, k, :],
                                                        scalar=K.par[:, MU0 + m, k:k + 1], in1=h[:, k, :],
                                                        op0=ALU.mult, op1=ALU.add).then_inc(dve_s.at(f"mixed{m}_{k}"), 1)
                    dve.scalar_tensor_tensor(out=xm[m - 3][:, k, :], in0=xx[:, k, :],
                                             scalar=K.par[:, MU0 + m - 3, k:k + 1], in1=h[:, k, :],
                                             op0=ALU.mult, op1=ALU.add)
                    q += 1

        @block.tensor
        def _(pe):
            pe.wait_ge(loaded, 32)
            q = 0
            for m, part, lo, hi in ((3, slice(0, 64), 0, 64), (4, slice(64, P), 64, 128), (5, slice(0, P), 128, 256)):
                for k in range(C):
                    pe.wait_ge(dve_s.sem, dve_s.value(f"mixed{m}_{k}"))
                    for s in range(2):
                        last = pe.matmul(K.ps[part, 2 * (m - 3) + s, 0:HALF], low[:, k, lo:hi],
                                         tmp[q % 2][:, s * HALF:(s + 1) * HALF],
                                         start=k == 0, stop=k == C - 1)
                    last.then_inc(pe_s.at(f"used{m}_{k}"), 1)
                    q += 1

        @block.scalar
        def _(act):
            act.activation(new_shift[:, :, 0:1], h[:, :, T - 1:T], ACT.Copy)
            act.activation(new_shift[:, :, 1:], h[:, :, T:N].rearrange("p c (b t) -> p c b t", t=ST)[:, :, :, ST - 1],
                           ACT.Copy)
            act.drain().then_inc(rows_ready, 1)
            act.wait_ge(pe_s.sem, pe_s.value(f"used3_{C - 1}"))
            act.activation(halves(hid_wa[0:64, :]), of_banks(K.ps, 0, slice(0, 64)), ACT.Tanh)
            act.wait_ge(pe_s.sem, pe_s.value(f"used4_{C - 1}"))
            act.activation(halves(hid_wa[64:P, :]), of_banks(K.ps, 2, slice(64, P)), ACT.Copy)
            act.wait_ge(pe_s.sem, pe_s.value(f"used5_{C - 1}"))
            act.activation(halves(hid_g), of_banks(K.ps, 4), ACT.Sigmoid)


def wkv(nc, K, I, xm, y_out, hid_wa, hid_g, R, wo_loaded):
    f = lambda: R.cut(N)
    dead_at = R.at
    r_s, k_s, sg, sq, kk, cum, lprev, kf = f(), f(), f(), f(), f(), f(), f(), f()
    av_at = R.at
    av, v_s, g_s, nrm = f(), f(), f(), f()
    e_pos, e_neg = f(), f()
    prev_at = R.at
    e_prev, factors, bon = f(), R.cut(4, N), f()
    at, rt, bt, kt = (factors[:, j, :] for j in range(4))
    s_at_rt = R.cut(2, NS)
    ba, rk = lprev, sq
    y_s, yc, ysq, sd = e_pos, e_neg, e_prev, nrm
    low2 = R.cut(2, P)
    prm, ln = R.cut(NPAR), R.cut(2)
    sc = R.cut(3 * NB + SB)
    esc = R.cut(3 * NB + SB)
    ptok = R.cut(3, NB, P)
    l_at = R.at
    L, X = R.cut(2, NB, P), R.cut(2, NB, P)
    R.cut(P)
    x_end = R.at
    XT = R.cut(2, NB, P)
    g_at = R.at
    G, RB, RK = (R.cut(2, NB, P) for _ in range(3))
    Q0 = Region(K.arena, dead_at)
    co = [[Q0.cut(NB, P) for _ in range(2)] for _ in range(2)]
    y1 = [Q0.cut(NB, P // 2) for _ in range(2)]
    s_pick, s_rows = Q0.cut(SB, P), Q0.cut(P)
    assert Q0.at <= av_at
    state = R.cut(P)
    Q0 = Region(K.arena, av_at)
    sc_state, s_tmp = [Q0.cut(P) for _ in range(2)], Q0.cut(P)
    Q0 = Region(K.arena, prev_at)
    r_tok, u_tok = Q0.cut(P), Q0.cut(P)
    Q = Region(K.arena, R.at)
    s_state = Q.cut(SB, P)
    Q2 = Region(K.arena, l_at)
    stok = Q2.cut(3, P, parts=NS)
    sL, sLT, sX, sXT, sG, sRB, sRK, sco, scoT = (Q2.cut(2, NS, parts=NS) for _ in range(9))
    sy1, sy2 = Q2.cut(2, NS, parts=NS), Q2.cut(2, NS, parts=NS)
    sr_tok, su_tok = Q2.cut(P, parts=NS), Q2.cut(P, parts=NS)
    assert Q2.at <= x_end
    Q3 = Region(K.arena, g_at)
    u_exp, v_exp = Q3.cut(SB, P, parts=NS), Q3.cut(SB, P, parts=NS)
    s_prod = Q3.cut(SB, P)

    wl = [K.sem(f"wkv_w{j}") for j in range(3)]
    low_loaded, prm_loaded, state_loaded = (K.sem(f"wkv_{x}_loaded") for x in ("low", "prm", "state"))
    stored, zeroed = K.sem("wkv_stored"), K.sem("wkv_zeroed")
    pe_s = Steps(K.sem("wkv_pe"),
                 ["w", "k", "a", "r", "norm", "v", "g", "bonus", "tok_v", "tok_b", "tok_k"]
                 + [f"gram_{x}{e}" for e in range(2) for x in ("L", "LT", "G", "RB", "RK")]
                 + [f"{x}{l}_{e}" for l in range(1, LEVELS) for x in ("y", "turn", "dXT") for e in range(2)]
                 + ["R0", "s_tok", "s_gram0", "s_gram1", "U0", "Y0", "S0"]
                 + ["s_y1", "R1", "s_d1", "U1", "Y1", "S1"]
                 + ["s_y2", "R2", "s_d2", "U2", "Y2", "S2"]
                 + ["s_RT", "R3", "U3", "s_U", "Y3", "S3"]
                 + ["s_Y", "mean", "s_S", "var"], a_pass_ahead=True)
    act_s = Steps(K.sem("wkv_act"),
                  ["w", "k", "ksq", "a", "r", "norm", "exps", "v", "g", "tok_v", "tok_b", "tok_k", "gram_L0", "gram_L1"]
                  + [f"{x}{l}_{e}" for l in range(1, LEVELS) for x in ("y", "X") for e in range(2)]
                  + ["R0", "s_tok", "U0", "s_y1", "R1", "U1", "s_y2", "R2", "U2", "R3", "U3", "s_U"]
                  + ["Y", "ysq", "sd"], a_pass_ahead=True)
    dve_s = Steps(K.sem("wkv_dve"),
                  ["logs", "rk", "factors", "bonus"]
                  + [f"{x}{e}" for e in range(2) for x in ("maskLT", "level0_", "gramG", "gramRB", "gramRK")]
                  + [f"XT{l}_{e}" for l in range(1, LEVELS) for e in range(2)]
                  + ["s_gram", "state0", "s_X1", "state1", "s_X2", "state2", "s_RT", "state3"]
                  + ["s_y", "s_exp", "yc", "s_state", "y"], a_pass_ahead=True)
    pool_s = Steps(K.sem("wkv_pool"), ["s_at_rt"] + [f"co{l}_{e}" for l in range(1, LEVELS) for e in range(2)])
    assert NB == 4 and SLEVELS == 3
    ps = K.ps
    lev = lambda l, t: K.level[:, 2 * l + t, :]

    def later(view, l):
        return view.rearrange("p (g two r) -> p g two r", two=2, r=2 ** l)[:, :, 1, :]

    def packed(view, l):
        return view.rearrange("p (g r) -> p g r", r=2 ** l)

    with nc.Block() as block:
        @block.sync
        def _(sp):
            sp.sem_inc(stored, 64)
            weight = (1, 0, 2)

            def load_state(i):
                for e in range(2):
                    q = slice(64 * e, 64 * e + 64)
                    sp.dma_start(s_state[q, :, q], I["state"][bass.ds(i, 1), q].squeeze(0)).then_inc(state_loaded, 16)

            sp.dma_start(low2, I["low2"][0]).then_inc(low_loaded, 16)
            sp.dma_start(prm, I["cpar"][0]).then_inc(prm_loaded, 16)
            for j, m in enumerate(weight):
                sp.dma_start(K.w[j], I["w_rkv"][m]).then_inc(wl[j], 16)
            sp.wait_ge(zeroed, 1)
            load_state(0)
            with sp.Fori(1, C) as i:
                for j, (name, m) in enumerate(zip(("k", "r", "v"), weight)):
                    sp.wait_ge(pe_s.sem, pe_s.before(name, i))
                    sp.dma_start(K.w[j], I["w_rkv"][bass.ds(i * 3 + m, 1)].squeeze(0)).then_inc(wl[j], 16)
                sp.wait_ge(pe_s.sem, pe_s.before("g", i))
                sp.dma_start(low2, I["low2"][bass.ds(i, 1)].squeeze(0)).then_inc(low_loaded, 16)
                sp.wait_ge(act_s.sem, act_s.before("a", i))
                sp.wait_ge(dve_s.sem, dve_s.before("rk", i))
                sp.dma_start(prm, I["cpar"][bass.ds(i, 1)].squeeze(0)).then_inc(prm_loaded, 16)
                sp.wait_ge(dve_s.sem, dve_s.before(f"state{NB - 1}", i))
                for e in range(2):
                    q = slice(64 * e, 64 * e + 64)
                    sp.dma_start(I["o_wkv_p"][bass.ds(i - 1, 1), q].squeeze(0), state[q, q]).then_inc(stored, 16)
                sp.wait_ge(dve_s.sem, dve_s.before("s_state", i))
                for e in range(2):
                    q = slice(64 * e, 64 * e + 64)
                    sp.dma_start(I["o_wkv_s"][bass.ds(i - 1, 1), q].squeeze(0), s_state[q, :, q]).then_inc(stored, 16)
                sp.wait_ge(stored, i * 64 + 64)
                load_state(i)
            sp.wait_ge(pe_s.sem, pe_s.value("r", C - 1))
            for j in range(2):
                sp.dma_start(K.w[j], I["w_o"][j]).then_inc(wo_loaded[j], 16)
            sp.wait_ge(dve_s.sem, dve_s.value("s_state", C - 1))
            for e in range(2):
                q = slice(64 * e, 64 * e + 64)
                sp.dma_start(I["o_wkv_p"][C - 1, q], state[q, q]).then_inc(stored, 16)
                sp.dma_start(I["o_wkv_s"][C - 1, q], s_state[q, :, q]).then_inc(stored, 16)
            sp.wait_ge(stored, C * 64 + 64)

        @block.tensor
        def _(pe):
            pe_s.begin(pe)

            def project(src, w, bank, name):
                for h in range(2):
                    for k in range(C):
                        last = pe.matmul(ps[:, bank + h, 0:HALF], w[:, k, :], src[:, k, h * HALF:(h + 1) * HALF],
                                         start=k == 0, stop=k == C - 1)
                last.then_inc(pe_s.at(name), 1)

            def expand(w, src, bank, name):
                for h in range(2):
                    last = pe.matmul(ps[:, bank + h, 0:HALF], w, src[:, h * HALF:(h + 1) * HALF], start=True, stop=True)
                last.then_inc(pe_s.at(name), 1)

            with pe.Fori(0, C) as i:
                pe.wait_ge(low_loaded, i * 16 + 16)
                expand(low2[0:64, 0, :], hid_wa[0:64, :], 4, "w")
                pe.wait_ge(wl[0], i * 16 + 16)
                project(xm[1], K.w[0], 2, "k")
                pe.wait_ge(dve_s.sem, dve_s.before("s_state", i))
                expand(low2[64:P, 0, :], hid_wa[64:P, :], 6, "a")
                pe.wait_ge(act_s.sem, act_s.before("sd", i))
                pe.wait_ge(wl[1], i * 16 + 16)
                project(xm[0], K.w[1], 0, "r")
                pe.wait_ge(act_s.sem, act_s.value("a", i))
                expand(K.headones, sq, 6, "norm")
                pe.wait_ge(wl[2], i * 16 + 16)
                project(xm[2], K.w[2], 2, "v")
                pe.wait_ge(act_s.sem, act_s.value("w", i))
                expand(low2[:, 1, :], hid_g, 4, "g")
                pe.wait_ge(act_s.sem, act_s.value("norm", i))
                pe.wait_ge(dve_s.sem, dve_s.value("rk", i))
                expand(K.headones, rk, 6, "bonus")
                for src, bank, name, other, ready in ((v_s, 2, "tok_v", act_s, "v"), (bt, 0, "tok_b", dve_s, "factors"),
                                                      (kt, 1, "tok_k", act_s, "r")):
                    pe.wait_ge(other.sem, other.value(ready, i))
                    for b in range(NB):
                        last = pe.transpose(ps[:, bank, b * P:(b + 1) * P], src[:, b * P:(b + 1) * P], K.ident)
                    last.then_inc(pe_s.at(name), 1)
                bank = {(0, "L"): 4, (0, "LT"): 5, (0, "G"): 6, (0, "RB"): 7, (0, "RK"): 0,
                        (1, "L"): 1, (1, "LT"): 2, (1, "G"): 3, (1, "RB"): 4, (1, "RK"): 5}
                for e in range(2):
                    q = slice(64 * e, 64 * e + 64)
                    for name, left, right, free in (("L", at, bt, ("g", "tok_k")), ("LT", bt, at, ("g", "tok_v")),
                                                    ("G", kt, at, (None, None)), ("RB", bt, rt, (None, "gram_L0")),
                                                    ("RK", kt, rt, ("tok_b", None))):
                        if free[e]:
                            pe.wait_ge(act_s.sem, act_s.value(free[e], i))
                        if (e, name) == (0, "G"):
                            pe.wait_ge(dve_s.sem, dve_s.value("bonus", i))
                        if (e, name) == (1, "RK"):
                            pe.wait_ge(dve_s.sem, dve_s.value("maskLT0", i))
                        for b in range(NB):
                            t = slice(b * P, (b + 1) * P)
                            last = pe.matmul(ps[:, bank[e, name], t], left[q, t], right[q, t], start=True, stop=True)
                        last.then_inc(pe_s.at(f"gram_{name}{e}"), 1)
                for l in range(1, LEVELS):
                    for e in range(2):
                        pe.wait_ge(pool_s.sem, pool_s.value(f"co{l}_{e}", i))
                        if l == 1:
                            pe.wait_ge(dve_s.sem, dve_s.value(f"gramRK{e}", i))
                        else:
                            pe.wait_ge(dve_s.sem, dve_s.value(f"XT{l - 1}_{e}", i))
                        for b in range(NB):
                            last = pe.matmul(packed(ps[:, 4 * e, b * P // 2:(b + 1) * P // 2], l), co[l % 2][e][:, b, :],
                                             later(XT[:, e, b, :], l), start=True, stop=True)
                        last.then_inc(pe_s.at(f"y{l}_{e}"), 1)
                    for e in range(2):
                        if (l, e) == (1, 0):
                            pe.wait_ge(act_s.sem, act_s.value("gram_L1", i))
                        for b in range(NB):
                            last = pe.transpose(ps[:, 4 * e + 1, b * P:(b + 1) * P], XT[:, e, b, :], K.ident)
                        last.then_inc(pe_s.at(f"turn{l}_{e}"), 1)
                    for e in range(2):
                        pe.wait_ge(act_s.sem, act_s.value(f"X{l}_{e}", i))
                        for b in range(NB):
                            last = pe.matmul(ps[:, 4 * e + 2, b * P // 2:(b + 1) * P // 2], X[:, e, b, :], y1[e][:, b, :],
                                             start=True, stop=True)
                        last.then_inc(pe_s.at(f"dXT{l}_{e}"), 1)

                def rows_R(b):
                    t = slice(b * P, (b + 1) * P)
                    if b:
                        pe.wait_ge(dve_s.sem, dve_s.value(f"state{b - 1}", i))
                    pe.matmul(ps[:, 0, 0:P], at[:, t], sc_state[b % 2], start=True, stop=False)
                    for e in range(2):
                        q = slice(64 * e, 64 * e + 64)
                        last = pe.matmul(ps[:, 0, q], G[:, e, b, :], ptok[:, 2, b, q], start=False, stop=e == 1)
                    last.then_inc(pe_s.at(f"R{b}"), 1)

                def rows_U(b):
                    pe.wait_ge(act_s.sem, act_s.value(f"R{b}", i))
                    for e in range(2):
                        q = slice(64 * e, 64 * e + 64)
                        last = pe.matmul(ps[:, 1, q], XT[:, e, b, :], r_tok[:, q], start=True, stop=True)
                    last.then_inc(pe_s.at(f"U{b}"), 1)

                def rows_Y_S(b):
                    t = slice(b * P, (b + 1) * P)
                    pe.matmul(ps[:, 3, t], sc_state[b % 2], rt[:, t], start=True, stop=False)
                    pe.wait_ge(act_s.sem, act_s.value(f"U{b}", i))
                    for e in range(2):
                        q = slice(64 * e, 64 * e + 64)
                        pe.matmul(ps[q, 3, t], u_tok[:, q], RB[:, e, b, :], start=False, stop=False)
                        last = pe.matmul(ps[q, 3, t], ptok[:, 2, b, q], RK[:, e, b, :], start=False, stop=True)
                    last.then_inc(pe_s.at(f"Y{b}"), 1)
                    pe.matmul(ps[:, 2, 0:P], ptok[:, 0, b, :], u_tok, start=True, stop=False)
                    last = pe.matmul(ps[:, 2, 0:P], ptok[:, 1, b, :], ptok[:, 2, b, :], start=False, stop=True)
                    last.then_inc(pe_s.at(f"S{b}"), 1)

                def sample_y(l):
                    pe.wait_ge(dve_s.sem, dve_s.value("s_gram" if l == 1 else f"s_X{l - 1}", i))
                    pe.nop(nofuse=True)
                    for e in range(2):
                        last = pe.matmul(ps[0:NS, 7, e * NS:(e + 1) * NS], sco[:, e, :], sXT[:, e, :], start=True, stop=True)
                    for e in range(2) if l < SLEVELS - 1 else ():
                        last = pe.matmul(ps[0:NS, 7, (2 + e) * NS:(3 + e) * NS], scoT[:, e, :], sX[:, e, :],
                                         start=True, stop=True)
                    last.then_inc(pe_s.at(f"s_y{l}"), 1)

                def sample_d(l):
                    pe.wait_ge(act_s.sem, act_s.value(f"s_y{l}", i))
                    pe.nop(nofuse=True)
                    for e in range(2):
                        last = pe.matmul(ps[0:NS, 4, e * NS:(e + 1) * NS], sX[:, e, :], sy1[:, e, :], start=True, stop=True)
                    for e in range(2) if l < SLEVELS - 1 else ():
                        last = pe.matmul(ps[0:NS, 4, (2 + e) * NS:(3 + e) * NS], sXT[:, e, :], sy2[:, e, :],
                                         start=True, stop=True)
                    last.then_inc(pe_s.at(f"s_d{l}"), 1)

                pe.wait_ge(dve_s.sem, dve_s.value(f"XT{LEVELS - 1}_1", i))
                rows_R(0)
                for j, src in enumerate((bt, kt, v_s)):
                    last = pe.transpose(ps[0:NS, 4, j * P:(j + 1) * P], src[:, T:N], K.ident)
                last.then_inc(pe_s.at("s_tok"), 1)
                for e in range(2):
                    q = slice(64 * e, 64 * e + 64)
                    for j, (left, right) in enumerate(((at, bt), (bt, at), (kt, at), (bt, rt), (kt, rt))):
                        last = pe.matmul(ps[0:NS, 5 + e, j * NS:(j + 1) * NS], left[q, T:N], right[q, T:N],
                                         start=True, stop=True)
                    last.then_inc(pe_s.at(f"s_gram{e}"), 1)
                rows_U(0)
                rows_Y_S(0)
                for b in (1, 2):
                    sample_y(b)
                    rows_R(b)
                    sample_d(b)
                    rows_U(b)
                    rows_Y_S(b)
                pe.wait_ge(state_loaded, i * 32 + 32)
                pe.wait_ge(dve_s.sem, dve_s.value("s_X2", i))
                for h in range(2):
                    pe.matmul(ps[:, 5 + h, :], s_at_rt.rearrange("p a b -> p (a b)"), s_state[:, 4 * h:4 * h + 4, :], start=True, stop=True)
                for e in range(2):
                    q = slice(64 * e, 64 * e + 64)
                    last = pe.matmul(ps[0:NS, 4, q], sG[:, e, :], stok[:, 2, q], start=True, stop=True)
                last.then_inc(pe_s.at("s_RT"), 1)
                rows_R(3)
                rows_U(3)
                pe.wait_ge(dve_s.sem, dve_s.value("s_RT", i))
                pe.nop(nofuse=True)
                for e in range(2):
                    q = slice(64 * e, 64 * e + 64)
                    last = pe.matmul(ps[0:NS, 7, q], sXT[:, e, :], sr_tok[:, q], start=True, stop=True)
                last.then_inc(pe_s.at("s_U"), 1)
                rows_Y_S(3)
                pe.wait_ge(act_s.sem, act_s.value("s_U", i))
                pe.nop(nofuse=True)
                pe.matmul(ps[:, 4, 0:NS], s_rows[NS:P, :], K.ident[NS:P, NS:P], start=True, stop=False)
                for e in range(2):
                    q = slice(64 * e, 64 * e + 64)
                    pe.matmul(ps[q, 4, 0:NS], su_tok[:, q], sRB[:, e, :], start=False, stop=False)
                    last = pe.matmul(ps[q, 4, 0:NS], stok[:, 2, q], sRK[:, e, :], start=False, stop=True)
                last.then_inc(pe_s.at("s_Y"), 1)
                pe.wait_ge(dve_s.sem, dve_s.value("s_y", i))
                pe.wait_ge(act_s.sem, act_s.value("Y", i))
                expand(K.headones, y_s, 0, "mean")
                pe.wait_ge(dve_s.sem, dve_s.value("s_exp", i))
                for h in range(2):
                    hb = slice(4 * h, 4 * h + 4)
                    pe.matmul(ps[:, 6 + h, :], stok[:, 0, :], u_exp[:, hb, :], start=True, stop=False)
                    last = pe.matmul(ps[:, 6 + h, :], stok[:, 1, :], v_exp[:, hb, :], start=False, stop=True)
                last.then_inc(pe_s.at("s_S"), 1)
                pe.wait_ge(act_s.sem, act_s.value("ysq", i))
                expand(K.headones, ysq, 0, "var")

        @block.scalar
        def _(act):
            act_s.begin(act)
            with act.Fori(0, C) as i:
                act.wait_ge(prm_loaded, i * 16 + 16)
                act.wait_ge(pe_s.sem, pe_s.value("w", i))
                act.activation(halves(sg), of_banks(ps, 4), ACT.Sigmoid, bias=prm[:, W0:W0 + 1]).then_inc(act_s.at("w"), 1)
                act.wait_ge(pe_s.sem, pe_s.value("k", i))
                act.activation(halves(k_s), of_banks(ps, 2), ACT.Copy).then_inc(act_s.at("k"), 1)
                act.activation(halves(sq), of_banks(ps, 2), ACT.Square, scale=prm[:, K_K:K_K + 1]).then_inc(act_s.at("ksq"), 1)
                act.wait_ge(pe_s.sem, pe_s.value("a", i))
                act.activation(halves(av), of_banks(ps, 6), ACT.Sigmoid, bias=prm[:, A0:A0 + 1]).then_inc(act_s.at("a"), 1)
                act.wait_ge(pe_s.sem, pe_s.value("r", i))
                act.activation(halves(r_s), of_banks(ps, 0), ACT.Copy).then_inc(act_s.at("r"), 1)
                act.wait_ge(dve_s.sem, dve_s.before("y", i))
                act.wait_ge(pe_s.sem, pe_s.value("norm", i))
                act.activation(halves(nrm), of_banks(ps, 6), ACT.Sqrt).then_inc(act_s.at("norm"), 1)
                act.wait_ge(dve_s.sem, dve_s.value("logs", i))
                act.activation(e_pos, cum, ACT.Exp, scale=-KAPPA)
                act.activation(e_neg, cum, ACT.Exp, scale=KAPPA)
                act.activation(e_prev, lprev, ACT.Exp, scale=-KAPPA)
                act.activation(esc, sc, ACT.Exp, scale=-KAPPA).then_inc(act_s.at("exps"), 1)
                act.wait_ge(pe_s.sem, pe_s.value("v", i))
                act.activation(halves(v_s), of_banks(ps, 2), ACT.Copy).then_inc(act_s.at("v"), 1)
                act.wait_ge(pe_s.sem, pe_s.value("g", i))
                act.activation(halves(g_s), of_banks(ps, 4), ACT.Copy).then_inc(act_s.at("g"), 1)
                for j, bank, name in ((2, 2, "tok_v"), (0, 0, "tok_b"), (1, 1, "tok_k")):
                    act.wait_ge(pe_s.sem, pe_s.value(name, i))
                    act.activation(ptok[:, j], ps[:, bank, :].rearrange("p (b f) -> p b f", f=P), ACT.Copy).then_inc(act_s.at(name), 1)
                for e, bank in enumerate((4, 1)):
                    act.wait_ge(pe_s.sem, pe_s.value(f"gram_L{e}", i))
                    act.activation(L[:, e], ps[:, bank, :].rearrange("p (b f) -> p b f", f=P), ACT.Copy).then_inc(act_s.at(f"gram_L{e}"), 1)
                for l in range(1, LEVELS):
                    for e in range(2):
                        act.wait_ge(pe_s.sem, pe_s.value(f"y{l}_{e}", i))
                        act.activation(y1[e], ps[:, 4 * e, 0:T // 2].rearrange("p (b f) -> p b f", f=P // 2),
                                       ACT.Copy).then_inc(act_s.at(f"y{l}_{e}"), 1)
                    for e in range(2):
                        act.wait_ge(pe_s.sem, pe_s.value(f"turn{l}_{e}", i))
                        act.activation(X[:, e], ps[:, 4 * e + 1, :].rearrange("p (b f) -> p b f", f=P),
                                       ACT.Copy).then_inc(act_s.at(f"X{l}_{e}"), 1)

                def rows_R(b):
                    act.wait_ge(pe_s.sem, pe_s.value(f"R{b}", i))
                    act.activation(r_tok, ps[:, 0, 0:P], ACT.Copy).then_inc(act_s.at(f"R{b}"), 1)

                def rows_U(b):
                    act.wait_ge(pe_s.sem, pe_s.value(f"U{b}", i))
                    act.activation(u_tok, ps[:, 1, 0:P], ACT.Copy).then_inc(act_s.at(f"U{b}"), 1)

                rows_R(0)
                act.wait_ge(pe_s.sem, pe_s.value("s_tok", i))
                act.activation(stok, ps[0:NS, 4, 0:3 * P].rearrange("p (j f) -> p j f", f=P), ACT.Copy).then_inc(act_s.at("s_tok"), 1)
                rows_U(0)
                for b in (1, 2):
                    act.wait_ge(pe_s.sem, pe_s.value(f"s_y{b}", i))
                    last = act.activation(sy1, ps[0:NS, 7, 0:2 * NS].rearrange("p (e f) -> p e f", f=NS), ACT.Copy)
                    if b < SLEVELS - 1:
                        last = act.activation(sy2, ps[0:NS, 7, 2 * NS:4 * NS].rearrange("p (e f) -> p e f", f=NS), ACT.Copy)
                    last.then_inc(act_s.at(f"s_y{b}"), 1)
                    rows_R(b)
                    rows_U(b)
                rows_R(3)
                rows_U(3)
                act.wait_ge(pe_s.sem, pe_s.value("s_U", i))
                act.activation(su_tok, ps[0:NS, 7, 0:P], ACT.Copy).then_inc(act_s.at("s_U"), 1)
                act.wait_ge(pe_s.sem, pe_s.value(f"Y{NB - 1}", i))
                act.activation(y_s[:, 0:T], ps[:, 3, :], ACT.Copy).then_inc(act_s.at("Y"), 1)
                act.wait_ge(dve_s.sem, dve_s.value("yc", i))
                act.activation(ysq, yc, ACT.Square).then_inc(act_s.at("ysq"), 1)
                act.wait_ge(pe_s.sem, pe_s.value("var", i))
                act.activation(halves(sd), of_banks(ps, 0), ACT.Sqrt, bias=K.eps[:, 1:2], scale=1.0 / HD).then_inc(act_s.at("sd"), 1)

        @block.vector
        def _(dve):
            dve_s.begin(dve)
            tt, ts, stt = dve.tensor_tensor, dve.tensor_scalar, dve.scalar_tensor_tensor
            dve.memset(s_state, 0.0).then_inc(zeroed, 1)
            with dve.Fori(0, C) as i:
                dve.wait_ge(prm_loaded, i * 16 + 16)
                dve.tensor_copy(ln, prm[:, LN_W:LN_W + 2])
                dve.wait_ge(act_s.sem, act_s.value("w", i))
                dve.tensor_tensor_scan(cum, K.reset, sg, 0.0, ALU.mult, ALU.add)
                dve.drain()
                blocks = cum[:, 0:T].rearrange("p (b t) -> p b t", t=P)
                seqs = cum[:, T:N].rearrange("p (b t) -> p b t", t=ST)
                dve.tensor_copy(sc[:, 0:NB], blocks[:, :, P // 2 - 1])
                dve.tensor_copy(sc[:, NB:2 * NB], blocks[:, :, P - 1])
                dve.tensor_copy(sc[:, 3 * NB:3 * NB + SB], seqs[:, :, ST - 1])
                dve.drain()
                tt(sc[:, 2 * NB:3 * NB], sc[:, NB:2 * NB], sc[:, 0:NB], ALU.subtract)
                tt(blocks, blocks, unsq(sc[:, 0:NB], 2, P), ALU.subtract)
                dve.drain()
                tt(lprev, cum, sg, ALU.subtract).then_inc(dve_s.at("logs"), 1)
                dve.wait_ge(act_s.sem, act_s.value("a", i))
                ts(kf, av, 1.0, prm[:, K_A:K_A + 1], ALU.subtract, ALU.mult)
                dve.drain()
                stt(out=kf, in0=kf, scalar=1.0, in1=k_s, op0=ALU.add, op1=ALU.mult)
                dve.wait_ge(act_s.sem, act_s.value("norm", i))
                ts(nrm, nrm, 1e-12, None, ALU.max)
                dve.drain()
                dve.reciprocal(nrm, nrm)
                dve.drain()
                stt(out=kk, in0=k_s, scalar=prm[:, K_K:K_K + 1], in1=nrm, op0=ALU.mult, op1=ALU.mult)
                stt(out=rk, in0=r_s, scalar=prm[:, R_K:R_K + 1], in1=kf, op0=ALU.mult, op1=ALU.mult).then_inc(dve_s.at("rk"), 1)
                dve.drain()
                dve.wait_ge(act_s.sem, act_s.value("exps", i))
                stt(out=at, in0=kk, scalar=-1.0, in1=e_prev, op0=ALU.mult, op1=ALU.mult)
                tt(ba, kk, av, ALU.mult)
                tt(kt, kf, e_neg, ALU.mult)
                tt(rt, r_s, e_pos, ALU.mult)
                dve.drain()
                tt(bt, ba, e_neg, ALU.mult).then_inc(dve_s.at("factors"), 1)
                dve.memset(sc_state[0], 0.0)
                dve.wait_ge(act_s.sem, act_s.value("v", i))
                dve.wait_ge(pe_s.sem, pe_s.value("bonus", i))
                tt(halves(bon), of_banks(ps, 6), halves(v_s), ALU.mult).then_inc(dve_s.at("bonus"), 1)
                banks = {(0, "LT"): 5, (0, "G"): 6, (0, "RB"): 7, (0, "RK"): 0,
                         (1, "LT"): 2, (1, "G"): 3, (1, "RB"): 4, (1, "RK"): 5}
                gram = lambda e, name: ps[:, banks[e, name], :].rearrange("p (b f) -> p b f", f=P)
                for e in range(2):
                    dve.wait_ge(pe_s.sem, pe_s.value(f"gram_LT{e}", i))
                    tt(XT[:, e], gram(e, "LT"), unsq(lev(0, 1), 1, NB), ALU.mult).then_inc(dve_s.at(f"maskLT{e}"), 1)
                    dve.drain()
                    tt(XT[:, e], XT[:, e], unsq(K.ident, 1, NB), ALU.add).then_inc(dve_s.at(f"level0_{e}"), 1)
                    for name, dst, mask in (("G", G, K.m_before), ("RB", RB, K.m_upto), ("RK", RK, K.m_upto)):
                        dve.wait_ge(pe_s.sem, pe_s.value(f"gram_{name}{e}", i))
                        tt(dst[:, e], gram(e, name), unsq(mask, 1, NB), ALU.mult).then_inc(dve_s.at(f"gram{name}{e}"), 1)
                dve.wait_ge(stored, i * 64 + 64)
                dve.memset(state, 0.0)
                for l in range(1, LEVELS):
                    for e in range(2):
                        dve.wait_ge(pe_s.sem, pe_s.value(f"dXT{l}_{e}", i))
                        rows = later(XT[:, e].rearrange("p b f -> p (b f)"), l)
                        tt(rows, rows, packed(ps[:, 4 * e + 2, 0:T // 2], l), ALU.add).then_inc(dve_s.at(f"XT{l}_{e}"), 1)

                def update_state(b):
                    dve.wait_ge(pe_s.sem, pe_s.value(f"S{b}", i))
                    stt(out=s_tmp, in0=ps[:, 2, 0:P], scalar=esc[:, 2 * NB + b:2 * NB + b + 1], in1=K.headones,
                        op0=ALU.mult, op1=ALU.mult)
                    dve.drain()
                    last = stt(out=state, in0=state, scalar=esc[:, NB + b:NB + b + 1], in1=s_tmp,
                               op0=ALU.mult, op1=ALU.add)
                    if b < NB - 1:
                        dve.drain()
                        last = ts(sc_state[(b + 1) % 2], state, esc[:, b + 1:b + 2], None, ALU.mult)
                    last.then_inc(dve_s.at(f"state{b}"), 1)

                grams = [ps[0:NS, 5 + e, 0:5 * NS].rearrange("p (j f) -> p j f", f=NS) for e in range(2)]
                for e in range(2):
                    dve.wait_ge(pe_s.sem, pe_s.value(f"s_gram{e}", i))
                    for j, (dst, mask) in enumerate(((sX, lev(0, 0)[0:NS, 0:NS]), (sXT, lev(0, 1)[0:NS, 0:NS]),
                                                     (sG, K.ms_before), (sRB, K.ms_upto), (sRK, K.ms_upto))):
                        tt(dst[:, e, :], grams[e][:, j, :], mask, ALU.mult)
                    dve.tensor_copy(sL[:, e, :], grams[e][:, 0, :])
                    dve.tensor_copy(sLT[:, e, :], grams[e][:, 1, :])
                dve.drain()
                for dst in (sX, sXT):
                    tt(dst, dst, unsq(K.ident[0:NS, 0:NS], 1, 2), ALU.add)
                tt(sco, sL, unsq(lev(1, 0)[0:NS, 0:NS], 1, 2), ALU.mult)
                tt(scoT, sLT, unsq(lev(1, 1)[0:NS, 0:NS], 1, 2), ALU.mult).then_inc(dve_s.at("s_gram"), 1)
                update_state(0)
                dve.wait_ge(pe_s.sem, pe_s.value("s_d1", i))
                tt(sXT, sXT, ps[0:NS, 4, 0:2 * NS].rearrange("p (e f) -> p e f", f=NS), ALU.add)
                tt(sX, sX, ps[0:NS, 4, 2 * NS:4 * NS].rearrange("p (e f) -> p e f", f=NS), ALU.add)
                tt(sco, sL, unsq(lev(2, 0)[0:NS, 0:NS], 1, 2), ALU.mult).then_inc(dve_s.at("s_X1"), 1)
                update_state(1)
                dve.wait_ge(pe_s.sem, pe_s.value("s_d2", i))
                tt(sXT, sXT, ps[0:NS, 4, 0:2 * NS].rearrange("p (e f) -> p e f", f=NS), ALU.add).then_inc(dve_s.at("s_X2"), 1)
                update_state(2)
                dve.wait_ge(pe_s.sem, pe_s.value("s_RT", i))
                for h in range(2):
                    tt(s_pick[:, 4 * h:4 * h + 4, :], ps[:, 5 + h, :].rearrange("p (b f) -> p b f", f=P),
                       unsq(K.seq_of[:, 4 * h:4 * h + 4], 2, P), ALU.mult)
                dve.drain()
                dve.tensor_reduce(out=s_rows, in_=s_pick.rearrange("p b f -> p f b"), op=ALU.add, axis=AX.X)
                dve.drain()
                tt(sr_tok, s_rows[0:NS, :], ps[0:NS, 4, 0:P], ALU.add).then_inc(dve_s.at("s_RT"), 1)
                update_state(3)
                tt(v_exp, unsq(stok[:, 2, :], 1, SB), unsq(K.seq_of[0:NS], 2, P), ALU.mult)
                dve.wait_ge(pe_s.sem, pe_s.value("s_Y", i))
                dve.tensor_copy(y_s[:, T:N], ps[:, 4, 0:NS]).then_inc(dve_s.at("s_y"), 1)
                tt(u_exp, unsq(su_tok, 1, SB), unsq(K.seq_of[0:NS], 2, P), ALU.mult).then_inc(dve_s.at("s_exp"), 1)
                dve.wait_ge(pe_s.sem, pe_s.value("mean", i))
                stt(out=halves(yc), in0=of_banks(ps, 0), scalar=-1.0 / HD, in1=halves(y_s),
                               op0=ALU.mult, op1=ALU.add).then_inc(dve_s.at("yc"), 1)
                dve.wait_ge(pe_s.sem, pe_s.value("s_S", i))
                for h in range(2):
                    hb = slice(4 * h, 4 * h + 4)
                    tt(s_prod[:, hb, :], ps[:, 6 + h, :].rearrange("p (b f) -> p b f", f=P), unsq(K.headones, 1, 4), ALU.mult)
                dve.drain()
                tt(s_state, s_state, s_prod, ALU.add)
                dve.drain()
                tt(s_state, s_state, unsq(esc[:, 3 * NB:3 * NB + SB], 2, P), ALU.mult).then_inc(dve_s.at("s_state"), 1)
                dve.wait_ge(act_s.sem, act_s.value("sd", i))
                dve.reciprocal(sd, sd)
                dve.drain()
                tt(yc, yc, sd, ALU.mult)
                dve.drain()
                ts(yc, yc, ln[:, 0:1], ln[:, 1:2], ALU.mult, ALU.add)
                dve.drain()
                tt(yc, yc, bon, ALU.add)
                dve.drain()
                tt(y_out[:, bass.ds(i, 1), :].squeeze(1), yc, g_s, ALU.mult).then_inc(dve_s.at("y"), 1)

        @block.gpsimd
        def _(pool):
            with pool.Fori(0, C) as i:
                pool.wait_ge(dve_s.sem, dve_s.value("factors", i))
                pool.nop(nofuse=True)
                pool.tensor_copy(s_at_rt, factors[:, 0:2, T:N]).then_inc(pool_s.at("s_at_rt"), 1)
                for l in range(1, LEVELS):
                    for e in range(2):
                        if l == 1:
                            pool.wait_ge(act_s.sem, act_s.value(f"gram_L{e}", i))
                        if l > 2:
                            pool.wait_ge(pe_s.sem, pe_s.value(f"y{l - 2}_{e}", i))
                        pool.tensor_tensor(co[l % 2][e], L[:, e], unsq(lev(l, 0), 1, NB), ALU.mult).then_inc(pool_s.at(f"co{l}_{e}"), 1)


def add_token_major(nc, K, acc):
    n = K.name()
    pe_s = Steps(K.sem(f"{n}_pe"), [f"turned{b}" for b in range(NB + 1)])
    dve_s = Steps(K.sem(f"{n}_dve"), [f"added{b}" for b in range(NB + 1)])
    with nc.Block() as block:
        @block.tensor
        def _(pe):
            for b in range(NB + 1):
                m = P if b < NB else NS
                if b >= 2:
                    pe.wait_ge(dve_s.sem, dve_s.value(f"added{b - 2}"))
                for c in range(C):
                    last = pe.transpose(K.ps[:, 2 * (b % 2) + c // 4, (c % 4) * P:(c % 4) * P + m],
                                        acc[0:m, b, c * P:(c + 1) * P], K.ident[0:m, 0:m])
                last.then_inc(pe_s.at(f"turned{b}"), 1)

        @block.vector
        def _(dve):
            for b in range(NB + 1):
                m = P if b < NB else NS
                dve.wait_ge(pe_s.sem, pe_s.value(f"turned{b}"))
                for h in range(2):
                    dst = K.x[:, 4 * h:4 * h + 4, b * P:b * P + m]
                    last = dve.tensor_tensor(dst, dst, K.ps[:, 2 * (b % 2) + h, :].rearrange(
                        "p (c t) -> p c t", t=P)[:, :, 0:m], ALU.add)
                last.then_inc(dve_s.at(f"added{b}"), 1)


def peer(nc, K, I, layer, h, h_tok, acc, R, wl):
    n = f"peer{layer}"
    RING = 8
    NU = NB + 1
    rows = [P] * NB + [NS]
    uring, vring = R.cut(RING, D), R.cut(RING, D)
    diag = R.cut(TOPK, P)
    q_sb, s_sb = R.cut(2, N), R.cut(NU, 2 * NKEYS)
    swork = R.cut(NKEYS)
    top_v, top_i = R.cut(2, TOPK), R.cut(2, TOPK, dtype=U32)
    top_f = R.cut(2, TOPK)
    cand, cwork = R.cut(TOPK * TOPK), R.cut(TOPK * TOPK)
    best_v, best_p = R.cut(NU, TOPK), R.cut(TOPK, dtype=U32)
    pos_u, pos_f = R.cut(2, TOPK, dtype=U32), R.cut(2, TOPK)
    hit = R.cut(2, TOPK, TOPK)
    part = R.cut(2, TOPK)
    idx_f, idx = R.cut(TOPK), R.cut(NU, TOPK, dtype=U32)
    neg_max, gate, gate_sum, gate_inv = R.cut(NU), R.cut(NU, TOPK), R.cut(NU), R.cut(1)
    dots, gelu, coef = R.cut(TOPK), R.cut(TOPK), R.cut(TOPK)
    spare = R.cut(2)

    u_here = [K.sem(f"{n}_u_here{j}") for j in range(RING)]
    v_here = [K.sem(f"{n}_v_here{j}") for j in range(RING)]
    u_free, v_free = K.sem(f"{n}_u_free"), K.sem(f"{n}_v_free")
    index_ready, keys_used, diag_ready = K.sem(f"{n}_index"), K.sem(f"{n}_keys"), K.sem(f"{n}_diag")
    LEAD = 3
    nxt = lambda b: (b + 1) % NU
    pick = lambda b: (b + LEAD) % NU

    def passes(sem, before, body, after):
        return (Steps(sem, before), Steps(sem, body, start=len(before)),
                Steps(sem, after, start=len(before) + (HEADS - 1) * len(body)))

    turned, copied = [f"turned{b}" for b in range(NU)], [f"copied{b}" for b in range(NU)]
    pe_p = passes(K.sem(f"{n}_pe"), ["q_a", "s_a", "q_b", "s_b"] + turned, ["v0", "q0", "v1", "q1", "s", "v2", "v3", "v4"],
                  [f"v{b}" for b in range(NU)])
    act_p = passes(K.sem(f"{n}_act"), ["q_a", "s_a", "q_b", "s_b"] + copied + ["exp0", "exp1", "gelu0", "exp2"],
                   ["gelu1", "exp3", "q0", "gelu2", "exp4", "q1", "s"]
                   + [x for b in range(2, NU) for x in (f"gelu{nxt(b)}", f"exp{pick(b)}")],
                   ["gelu1", "exp3", "gelu2", "exp4", "gelu3", "gelu4"])
    dve_p = passes(K.sem(f"{n}_dve"), ["top0", "top1", "coef0", "top2"],
                   [x for b in range(NU) for x in (f"acc{b}", f"coef{nxt(b)}", f"top{pick(b)}")],
                   ["acc0", "coef1", "top3", "acc1", "coef2", "top4", "acc2", "coef3", "acc3", "coef4", "acc4"])
    s_bank = ((6, 0, 2), (7, 2, 2), (2, 4, 1))
    ps = K.ps

    with nc.Block() as block:
        @block.sync
        def _(sp):
            with sp.Fori(1, HEADS) as i:
                sp.wait_ge(keys_used, i)
                for j in range(2):
                    sp.dma_start(K.w9[j], I["w_q"][layer, bass.ds(i * 2 + j, 1)].squeeze(0)).then_inc(wl[j], 16)

        @block.gpsimd
        def _(pool):
            pool.memset(spare[:, 0:1], 0.0).then_inc(u_free, RING)
            pool.memset(spare[:, 1:2], 0.0).then_inc(v_free, RING)

            def gather(i, b, j, ring, here, free, table):
                m = rows[b % NU]
                pool.wait_ge(free, i * (NU * TOPK) + (b * TOPK + j + 1))
                pool.nop(nofuse=True)
                pool.indirect_dma_start(ring[0:m, j % RING, :], None, table,
                                        bass.IndirectOffsetOnAxis(ap=idx[0:m, b % NU, j:j + 1], axis=0)
                                        ).then_inc(here[j % RING], 16)

            of_u, of_v = (uring, u_here, u_free, I["u"][layer]), (vring, v_here, v_free, I["v"][layer])
            pool.wait_ge(index_ready, 1)
            for j in range(TOPK):
                gather(0, 0, j, *of_u)
            with pool.Fori(0, HEADS - 1) as i:
                for b in range(NU):
                    pool.wait_ge(index_ready, i * NU + (b + 2))
                    for j in range(TOPK):
                        gather(i, b, j, *of_v)
                        gather(i, b + 1, j, *of_u)
            for b in range(NU):
                if b < NU - 1:
                    pool.wait_ge(index_ready, (HEADS - 1) * NU + (b + 2))
                for j in range(TOPK):
                    gather(HEADS - 1, b, j, *of_v)
                    if b < NU - 1:
                        gather(HEADS - 1, b + 1, j, *of_u)

        @block.tensor
        def _(pe):
            def query(S, j, head):
                pe.wait_ge(wl[j], head * 16 + 16)
                for s in range(2):
                    for k in range(C):
                        last = pe.matmul(ps[:, 2 + 2 * j + s, 0:HALF], K.w9[j][:, k, :],
                                         h[:, k, s * HALF:(s + 1) * HALF], start=k == 0, stop=k == C - 1)
                last.then_inc(S.at(f"q{j}"), 1)

            def score(groups):
                for bank, b0, nb in groups:
                    for b in range(b0, b0 + nb):
                        m = rows[b]
                        for j in range(2):
                            col = ((b - b0) * 2 + j) * NKEYS
                            last = pe.matmul(ps[0:m, bank, col:col + NKEYS], q_sb[:, j, b * P:b * P + m],
                                             K.w9[j][:, C, :], start=True, stop=True)
                return last

            def first_query(s, name):
                for j in range(2):
                    pe.wait_ge(wl[j], 16)
                    for k in range(C):
                        last = pe.matmul(ps[:, 2 + 2 * j + s, 0:HALF], K.w9[j][:, k, :],
                                         h[:, k, s * HALF:(s + 1) * HALF], start=k == 0, stop=k == C - 1)
                last.then_inc(pe_p[0].at(name), 1)

            def combine(S, i, b):
                m = rows[b]
                for j in range(TOPK):
                    pe.wait_ge(diag_ready, i * (NU * TOPK) + (b * TOPK + j + 1))
                    pe.wait_ge(v_here[j % RING], i * (2 * NU * 16) + (2 * b + j // RING + 1) * 16)
                    if m < P:
                        pe.nop(nofuse=True)
                    for s in range(2):
                        last = pe.matmul(ps[0:m, s, :], diag[0:m, j, 0:m],
                                         vring[0:m, j % RING, s * 512:(s + 1) * 512],
                                         start=j == 0, stop=j == TOPK - 1)
                    last.then_inc(v_free, 1)
                pe.drain().then_inc(S.at(f"v{b}"), 1)

            first_query(0, "q_a")
            pe.wait_ge(act_p[0].sem, act_p[0].value("q_a"))
            score(s_bank[:1]).then_inc(pe_p[0].at("s_a"), 1)
            first_query(1, "q_b")
            pe.wait_ge(act_p[0].sem, act_p[0].value("q_b"))
            score(s_bank[1:]).then_inc(keys_used, 1)
            pe.drain().then_inc(pe_p[0].at("s_b"), 1)
            for b in range(NU):
                m, bank = rows[b], (0, 4)[b % 2]
                if b >= 2:
                    pe.wait_ge(act_p[0].sem, act_p[0].value(f"copied{b - 2}"))
                for c in range(C):
                    last = pe.transpose(ps[0:m, bank + c // 4, (c % 4) * P:(c % 4 + 1) * P],
                                        h[:, c, b * P:b * P + m], K.ident)
                last.then_inc(pe_p[0].at(f"turned{b}"), 1)
            with pe.Fori(0, HEADS - 1) as i:
                combine(pe_p[1], i, 0)
                query(pe_p[1], 0, i + 1)
                combine(pe_p[1], i, 1)
                query(pe_p[1], 1, i + 1)
                pe.wait_ge(act_p[1].sem, act_p[1].value("q1", i))
                score(s_bank).then_inc(keys_used, 1)
                pe.drain().then_inc(pe_p[1].at("s"), 1)
                for b in range(2, NU):
                    combine(pe_p[1], i, b)
            for b in range(NU):
                combine(pe_p[2], HEADS - 1, b)

        @block.scalar
        def _(act):
            def query(S, Q, i, j):
                act.wait_ge(Q.sem, Q.value(f"q{j}", i))
                act.activation(halves(q_sb[:, j, :]), of_banks(ps, 2 + 2 * j), ACT.Copy).then_inc(S.at(f"q{j}"), 1)

            def scores(groups):
                for bank, b0, nb in groups:
                    m = rows[b0]
                    last = act.activation(s_sb[0:m, b0:b0 + nb, :], ps[0:m, bank, 0:nb * 2 * NKEYS].rearrange(
                        "p (b f) -> p b f", b=nb), ACT.Copy)
                return last

            def softmax(S, V, i, b):
                m = rows[b]
                act.wait_ge(V.sem, V.value(f"top{b}", i))
                act.activation(gate[0:m, b, :], best_v[0:m, b, :], ACT.Exp, bias=neg_max[0:m, b:b + 1],
                                      accum_out=gate_sum[0:m, b:b + 1]).then_inc(S.at(f"exp{b}"), 1)

            def diagonals(V, a, b):
                m = rows[b]
                act.wait_ge(V.sem, V.value(f"coef{b}", a))
                for j in range(TOPK):
                    act.activation(diag[0:m, j, 0:m], K.ident[0:m, 0:m], ACT.Copy,
                                   scale=coef[0:m, j:j + 1]).then_inc(diag_ready, 1)

            def activate(S, i, b):
                m = rows[b % NU]
                act.wait_ge(u_free, i * (NU * TOPK) + ((b + 1) * TOPK + RING))
                act.activation(gelu[0:m, :], dots[0:m, :], ACT.Gelu).then_inc(S.at(f"gelu{b % NU}"), 1)

            for s, (part, groups) in enumerate((("a", s_bank[:1]), ("b", s_bank[1:]))):
                act.wait_ge(pe_p[0].sem, pe_p[0].value(f"q_{part}"))
                for j in range(2):
                    last = act.activation(q_sb[:, j, s * HALF:(s + 1) * HALF], ps[:, 2 + 2 * j + s, 0:HALF], ACT.Copy)
                last.then_inc(act_p[0].at(f"q_{part}"), 1)
                act.wait_ge(pe_p[0].sem, pe_p[0].value(f"s_{part}"))
                scores(groups).then_inc(act_p[0].at(f"s_{part}"), 1)
            for b in range(NU):
                m, bank = rows[b], (0, 4)[b % 2]
                act.wait_ge(pe_p[0].sem, pe_p[0].value(f"turned{b}"))
                act.activation(h_tok[0:m, b, :].rearrange("p (a b) -> p a b", a=2),
                               ps[0:m, bank:bank + 2, :], ACT.Copy).then_inc(act_p[0].at(f"copied{b}"), 1)
            softmax(act_p[0], dve_p[0], 0, 0)
            softmax(act_p[0], dve_p[0], 0, 1)
            activate(act_p[0], 0, 0)
            diagonals(dve_p[0], 0, 0)
            softmax(act_p[0], dve_p[0], 0, 2)
            with act.Fori(0, HEADS - 1) as i:
                for b in range(NU):
                    activate(act_p[1], i, b + 1)
                    diagonals(dve_p[1], i, nxt(b))
                    softmax(act_p[1], dve_p[1], i, pick(b))
                    if b < 2:
                        query(act_p[1], pe_p[1], i, b)
                    if b == 1:
                        act.wait_ge(pe_p[1].sem, pe_p[1].value("s", i))
                        scores(s_bank).then_inc(act_p[1].at("s"), 1)
            for b in range(1, NU):
                activate(act_p[2], HEADS - 1, b)
                diagonals(dve_p[2], 0, b)
                if b - 1 < NU - LEAD:
                    softmax(act_p[2], dve_p[2], 0, pick(b - 1))

        @block.vector
        def _(dve):
            tt, ts, stt = dve.tensor_tensor, dve.tensor_scalar, dve.scalar_tensor_tensor

            def top16(values, work, out_v, out_i):
                dve.max(out_v[:, 0:8], values)
                dve.drain()
                dve.max_index(out_i[:, 0:8], out_v[:, 0:8], values)
                dve.match_replace(out=work, in_to_replace=out_v[:, 0:8], in_values=values, imm_value=LOWEST)
                dve.drain()
                dve.max(out_v[:, 8:16], work)
                dve.drain()
                dve.max_index(out_i[:, 8:16], out_v[:, 8:16], work)

            def choose(S, b):
                m = rows[b]
                for j in range(2):
                    top16(s_sb[0:m, b, j * NKEYS:(j + 1) * NKEYS], swork[0:m], top_v[0:m, j, :], top_i[0:m, j, :])
                    dve.drain()
                dve.tensor_copy(top_f[0:m], top_i[0:m])
                tt(cand[0:m].rearrange("p (a b) -> p a b", b=TOPK), unsq(top_v[0:m, 0, :], 2, TOPK),
                   unsq(top_v[0:m, 1, :], 1, TOPK), ALU.add)
                dve.drain()
                top16(cand[0:m], cwork[0:m], best_v[0:m, b, :], best_p[0:m])
                dve.drain()
                ts(neg_max[0:m, b:b + 1], best_v[0:m, b, 0:1], -1.0, None, ALU.mult).then_inc(S.at(f"top{b}"), 1)
                ts(pos_u[0:m, 0, :], best_p[0:m], 4, None, ALU.logical_shift_right)
                ts(pos_u[0:m, 1, :], best_p[0:m], TOPK - 1, None, ALU.bitwise_and)
                dve.drain()
                dve.tensor_copy(pos_f[0:m], pos_u[0:m])
                dve.drain()
                for j in range(2):
                    tt(hit[0:m, j], unsq(pos_f[0:m, j, :], 2, TOPK), unsq(K.iota[0:m], 1, TOPK), ALU.is_equal)
                dve.drain()
                for j in range(2):
                    tt(hit[0:m, j], hit[0:m, j], unsq(top_f[0:m, j, :], 1, TOPK), ALU.mult)
                dve.drain()
                dve.tensor_reduce(out=part[0:m], in_=hit[0:m], op=ALU.add, axis=AX.X)
                dve.drain()
                stt(out=idx_f[0:m], in0=part[0:m, 0, :], scalar=float(NKEYS), in1=part[0:m, 1, :],
                    op0=ALU.mult, op1=ALU.add)
                dve.drain()
                dve.tensor_copy(idx[0:m, b, :], idx_f[0:m]).then_inc(index_ready, 1)

            def dot(i, b):
                m = rows[b % NU]
                for j in range(TOPK):
                    dve.wait_ge(u_here[j % RING], i * (2 * NU * 16) + (2 * b + j // RING + 1) * 16)
                    row = uring[0:m, j % RING, :]
                    stt(out=row, in0=row, scalar=1.0, in1=h_tok[0:m, b % NU, :], op0=ALU.mult, op1=ALU.mult,
                        accum_out=dots[0:m, j:j + 1]).then_inc(u_free, 1)

            def weigh(S, A, a, b):
                m = rows[b]
                dve.reciprocal(gate_inv[0:m], gate_sum[0:m, b:b + 1])
                dve.drain()
                dve.wait_ge(A.sem, A.value(f"gelu{b}", a))
                stt(out=coef[0:m], in0=gate[0:m, b, :], scalar=gate_inv[0:m], in1=gelu[0:m],
                    op0=ALU.mult, op1=ALU.mult).then_inc(S.at(f"coef{b}"), 1)

            def add(S, Q, a, b):
                m = rows[b]
                dve.wait_ge(Q.sem, Q.value(f"v{b}", a))
                dst = acc[0:m, b, :].rearrange("p (a b) -> p a b", a=2)
                tt(dst, dst, ps[0:m, 0:2, :], ALU.add).then_inc(S.at(f"acc{b}"), 1)

            dve.memset(acc, 0.0)
            dve.wait_ge(act_p[0].sem, act_p[0].value("s_a"))
            dve.drain()
            choose(dve_p[0], 0)
            choose(dve_p[0], 1)
            dve.wait_ge(act_p[0].sem, act_p[0].value("exp0"))
            dot(0, 0)
            weigh(dve_p[0], act_p[0], 0, 0)
            choose(dve_p[0], 2)
            with dve.Fori(0, HEADS - 1) as i:
                for b in range(NU):
                    dot(i, b + 1)
                    add(dve_p[1], pe_p[1], i, b)
                    weigh(dve_p[1], act_p[1], i, nxt(b))
                    if pick(b) == 0:
                        dve.wait_ge(act_p[1].sem, act_p[1].value("s", i))
                        dve.nop(nofuse=True)
                    choose(dve_p[1], pick(b))
            for b in range(NU):
                if b < NU - 1:
                    dot(HEADS - 1, b + 1)
                add(dve_p[2], pe_p[2], 0, b)
                if b < NU - 1:
                    weigh(dve_p[2], act_p[2], 0, b + 1)
                if b < NU - LEAD:
                    choose(dve_p[2], pick(b))


def conv(nc, K, I, h, cv, R, wl):
    PE_TAPS = 9
    ups, uss = [R.cut(PAST + T) for _ in range(2)], [R.cut(SB, PAST + ST) for _ in range(2)]
    prms = [R.cut(NPAR) for _ in range(2)]
    sg, diags = R.cut(N), R.cut(PE_TAPS, P)
    projected = [K.sem(f"conv_projected{j}") for j in range(2)]
    small = [K.sem(f"conv_small{j}") for j in range(2)]
    stored, zeroed, tapped = K.sem("conv_stored"), K.sem("conv_zeroed"), K.sem("conv_tapped")
    gated, diags_ready = K.sem("conv_gated"), K.sem("conv_diags_ready")
    u_ready, summed = K.sem("conv_u_ready"), K.sem("conv_summed")
    ps = K.ps
    one = lambda tensor, c: tensor[c] if isinstance(c, int) else tensor[bass.ds(c, 1)].squeeze(0)
    with nc.Block() as block:
        @block.sync
        def _(sp):
            def load_weights(c, weights):
                for j in range(2):
                    sp.wait_ge(projected[j], c)
                    sp.dma_start(K.w[j], one(I["w_pw1"], weights[j])).then_inc(wl[j], 16)

            def load_small(c, j):
                sp.dma_start(prms[j], one(I["cpar"], c)).then_inc(small[j], 16)
                sp.dma_start(uss[j][:, :, 0:PAST], one(I["state_conv"], c)).then_inc(small[j], 16)

            def store(c, j):
                sp.wait_ge(u_ready, c + 1)
                sp.dma_start(one(I["o_conv_p"], c), ups[j][:, T:T + PAST]).then_inc(stored, 16)
                sp.dma_start(one(I["o_conv_s"], c), uss[j][:, :, ST:ST + PAST]).then_inc(stored, 16)

            sp.wait_ge(zeroed, 1)
            load_small(0, 0)
            load_small(1, 1)
            load_weights(1, (2, 3))
            store(0, 0)
            with sp.Fori(1, C // 2) as i:
                for j in range(2):
                    load_weights(i * 2 + j, [i * 4 + (2 * j + g) for g in range(2)])
                    sp.wait_ge(summed, i * 2 + (j - 1))
                    sp.wait_ge(stored, i * 64 + (32 * j - 32))
                    load_small(i * 2 + j, j)
                    store(i * 2 + (j - 1), 1 - j)
            store(C - 1, 1)
            sp.wait_ge(stored, C * 32)

        @block.tensor
        def _(pe):
            def project(c):
                if not isinstance(c, int) or c:
                    pe.wait_ge(u_ready, c)
                for j in range(2):
                    pe.wait_ge(wl[j], c * 16 + 16)
                    for s in range(2):
                        for k in range(C):
                            last = pe.matmul(ps[:, 2 * j + s, 0:HALF], K.w[j][:, k, :], h[:, k, s * HALF:(s + 1) * HALF],
                                             start=k == 0, stop=k == C - 1)
                    last.then_inc(projected[j], 1)

            def taps(c, j):
                pe.wait_ge(diags_ready, c + 1)
                pe.wait_ge(u_ready, c + 1)
                up, us = ups[j], uss[j]
                for k in range(PE_TAPS):
                    pe.matmul(ps[:, 4 + 2 * j, :], diags[:, k, :], up[:, k:k + T], start=k == 0, stop=k == PE_TAPS - 1)
                    last = pe.matmul(ps[:, 5 + 2 * j, 0:NS], diags[:, k, :], us[:, :, k:k + ST], start=k == 0, stop=k == PE_TAPS - 1)
                last.then_inc(tapped, 1)

            project(0)
            with pe.Fori(0, C // 2 - 1) as i:
                for j in range(2):
                    project(i * 2 + (j + 1))
                    taps(i * 2 + j, j)
            project(C - 1)
            taps(C - 2, 0)
            taps(C - 1, 1)

        @block.scalar
        def _(act):
            def chunk(c, j, later):
                act.wait_ge(small[j], later * 32 + 32)
                act.wait_ge(projected[1], c + 1)
                if not isinstance(c, int) or c:
                    act.wait_ge(u_ready, c)
                act.activation(halves(sg), of_banks(ps, 2), ACT.Sigmoid, bias=prms[j][:, B_PG:B_PG + 1]).then_inc(gated, 1)
                if not isinstance(c, int) or c:
                    act.wait_ge(tapped, c)
                for k in range(PE_TAPS):
                    last = act.activation(diags[:, k, :], K.ident, ACT.Copy, scale=prms[j][:, TAP0 + k:TAP0 + k + 1])
                last.then_inc(diags_ready, 1)

            chunk(0, 0, 0)
            with act.Fori(0, C // 2 - 1) as i:
                for j in range(2):
                    chunk(i * 2 + (j + 1), 1 - j, i + j)
            chunk(C - 1, 1, C // 2 - 1)

        @block.vector
        def _(dve):
            stt = dve.scalar_tensor_tensor

            def glu(c, j, later):
                up, us = ups[j], uss[j]
                dve.wait_ge(small[j], later * 32 + 32)
                dve.wait_ge(gated, c + 1)
                how = dict(scalar=prms[j][:, B_PA:B_PA + 1], op0=ALU.add, op1=ALU.mult)
                stt(out=up[:, PAST:PAST + HALF], in0=ps[:, 0, 0:HALF], in1=sg[:, 0:HALF], **how)
                stt(out=up[:, PAST + HALF:], in0=ps[:, 1, 0:T - HALF], in1=sg[:, HALF:T], **how)
                stt(out=us[:, :, PAST:], in0=ps[:, 1, T - HALF:HALF].rearrange("p (b t) -> p b t", t=ST),
                    in1=sg[:, T:N].rearrange("p (b t) -> p b t", t=ST), **how).then_inc(u_ready, 1)
                dve.drain()

            def outputs(c):
                rows = cv[:, c, :] if isinstance(c, int) else cv[:, bass.ds(c, 1), :].squeeze(1)
                return rows[:, 0:T], rows[:, T:N].rearrange("p (b t) -> p b t", t=ST)

            def taps(c, j):
                outp, outs = outputs(c)
                for k in range(PE_TAPS, TAPS):
                    w = prms[j][:, TAP0 + k:TAP0 + k + 1]
                    for o, u in ((outp, ups[j][:, k:k + T]), (outs, uss[j][:, :, k:k + ST])):
                        if k == PE_TAPS:
                            dve.tensor_scalar(o, u, w, prms[j][:, B_DW:B_DW + 1], ALU.mult, ALU.add)
                        else:
                            stt(out=o, in0=u, scalar=w, in1=o, op0=ALU.mult, op1=ALU.add)
                    dve.drain()

            def add(c, j):
                outp, outs = outputs(c)
                dve.wait_ge(tapped, c + 1)
                dve.tensor_tensor(outp, outp, ps[:, 4 + 2 * j, :], ALU.add)
                dve.tensor_tensor(outs, outs, ps[:, 5 + 2 * j, 0:NS].rearrange("p (b t) -> p b t", t=ST),
                                  ALU.add).then_inc(summed, 1)

            dve.memset(ups[0][:, 0:PAST], 0.0)
            dve.memset(ups[1][:, 0:PAST], 0.0).then_inc(zeroed, 1)
            glu(0, 0, 0)
            with dve.Fori(0, C // 2 - 1) as i:
                for j in range(2):
                    taps(i * 2 + j, j)
                    glu(i * 2 + (j + 1), 1 - j, i + j)
                    add(i * 2 + j, j)
            taps(C - 2, 0)
            glu(C - 1, 1, C // 2 - 1)
            add(C - 2, 0)
            taps(C - 1, 1)
            add(C - 1, 1)


def layernorm_silu(nc, K, v, ahead):
    act_s = Steps(K.sem("ln_act"), [f"square{c}" for c in range(C)] + ["root"])
    pe_s = Steps(K.sem("ln_pe"), ["sum"] + [f"summed{c}" for c in range(C)])
    dve_s = Steps(K.sem("ln_dve"), [f"centred{c}" for c in range(C)] + [f"scaled{c}" for c in range(C)])
    sq = [K.small[:, 0:N], K.small[:, N:2 * N]]
    mean, root = K.small[:, 2 * N:3 * N], K.small[:, 3 * N:4 * N]
    with nc.Block() as block:
        @block.sync
        def _(sp):
            for buffer, source, loaded in ahead:
                sp.dma_start(buffer, source).then_inc(loaded, 16)

        @block.tensor
        def _(pe):
            for h in range(2):
                for c in range(C):
                    last = pe.matmul(K.ps[:, h, 0:HALF], K.ones, v[:, c, h * HALF:(h + 1) * HALF],
                                     start=c == 0, stop=c == C - 1)
            last.then_inc(pe_s.at("sum"), 1)
            for c in range(C):
                pe.wait_ge(act_s.sem, act_s.value(f"square{c}"))
                for h in range(2):
                    last = pe.matmul(K.ps[:, 2 + h, 0:HALF], K.ones, sq[c % 2][:, h * HALF:(h + 1) * HALF],
                                     start=c == 0, stop=c == C - 1)
                last.then_inc(pe_s.at(f"summed{c}"), 1)

        @block.vector
        def _(dve):
            dve.wait_ge(pe_s.sem, pe_s.value("sum"))
            dve.tensor_scalar(halves(mean), of_banks(K.ps, 0), 1.0 / D, None, ALU.mult)
            dve.drain()
            for c in range(C):
                dve.tensor_tensor(v[:, c, :], v[:, c, :], mean, ALU.subtract).then_inc(dve_s.at(f"centred{c}"), 1)
            dve.wait_ge(act_s.sem, act_s.value("root"))
            dve.reciprocal(root, root)
            dve.drain()
            for c in range(C):
                dve.tensor_tensor(v[:, c, :], v[:, c, :], root, ALU.mult).then_inc(dve_s.at(f"scaled{c}"), 1)

        @block.scalar
        def _(act):
            for c in range(C):
                act.wait_ge(dve_s.sem, dve_s.value(f"centred{c}"))
                if c >= 2:
                    act.wait_ge(pe_s.sem, pe_s.value(f"summed{c - 2}"))
                act.activation(sq[c % 2], v[:, c, :], ACT.Square).then_inc(act_s.at(f"square{c}"), 1)
            act.wait_ge(pe_s.sem, pe_s.value(f"summed{C - 1}"))
            act.activation(halves(root), of_banks(K.ps, 2), ACT.Sqrt, bias=K.eps[:, 2:3], scale=1.0 / D).then_inc(act_s.at("root"), 1)
            for c in range(C):
                act.wait_ge(dve_s.sem, dve_s.value(f"scaled{c}"))
                act.activation(v[:, c, :], v[:, c, :], ACT.Silu, bias=K.par[:, CLN_B, c:c + 1],
                               scale=K.par[:, CLN_G, c:c + 1])


class Kernel:

    def __init__(self, nc, ctx):
        self.nc, self.ctx, self.phases = nc, ctx, 0
        sb = lambda name, shape: ctx.enter_context(nc.sbuf_tensor(name, shape, F32))[tuple(slice(None) for _ in shape)]
        self.x = sb("x", [P, C, N])
        self.par = sb("par", [P, NPAR, C])
        self.cst = sb("cst", [P, CST_COLS])
        self.level = sb("level", [P, 2 * LEVELS, P])
        self.wbuf = sb("wbuf", [P, 3 * (C + 1), P])
        self.eps = sb("eps", [P, 3])
        self.bias_cols = sb("bias_cols", [P, 2])
        self.arena = sb("arena", [P, ARENA])
        self.ps = ctx.enter_context(nc.psum_tensor("psum", [P, 8, 512], F32))[:, :, :]
        cut = Region(self.cst)
        self.ident, self.ones, self.headones = cut.cut(P), cut.cut(P), cut.cut(P)
        self.m_before, self.m_upto = cut.cut(P), cut.cut(P)
        self.ms_before, self.ms_upto = cut.cut(NS, parts=NS), cut.cut(NS, parts=NS)
        self.seq_of, self.iota, self.reset = cut.cut(SB), cut.cut(TOPK), cut.cut(N)
        self.w9 = [self.wbuf[:, j * (C + 1):(j + 1) * (C + 1), :] for j in range(3)]
        self.w = [w[:, 0:C, :] for w in self.w9]

    def sem(self, name):
        return self.ctx.enter_context(self.nc.semaphore(name))

    def name(self):
        self.phases += 1
        return f"phase{self.phases}"


ARENA = 41450
CST_COLS = 5 * P + 2 * NS + SB + TOPK + N


def build(nc, I):
    with ExitStack() as ctx:
        K = Kernel(nc, ctx)
        base = C * N
        h = Region(K.arena, 0).cut(C, N)
        work = base
        K.small = K.arena[:, ARENA - 4 * N:ARENA]
        load_constants(nc, K, I)
        pair = lambda name: [K.sem(f"{name}_loaded{j}") for j in range(2)]
        wo_loaded, pw1_loaded, pw2_loaded, wq_loaded = pair("w_o"), pair("pw1"), pair("pw2"), (pair("wq0"), pair("wq1"))
        ahead = lambda buffers, weights, sems: list(zip(buffers, (weights[0], weights[1]), sems))

        R = Region(K.arena, work)
        xm = [R.cut(C, N) for _ in range(3)]
        hid_wa, hid_g = R.cut(N), R.cut(N)
        X = Region(K.arena, R.at)
        xx = X.cut(C, N)
        K.low, K.shift, K.new_shift = X.cut(C, 2 * P), X.cut(C, SB), X.cut(C, 1 + SB)
        low_loaded = K.sem("low1_loaded")
        rmsnorm(nc, K, NMIX0, h, ahead=[(K.low, I["low1"], low_loaded), (K.shift, I["shift"], low_loaded)])
        time_mix_inputs(nc, K, I, h, xx, xm, hid_wa, hid_g, low_loaded)
        wkv(nc, K, I, xm, h, hid_wa, hid_g, R, wo_loaded)
        linear_into_x(nc, K, I["w_o"], h, wo_loaded)

        for layer, gain in ((0, NFFN0), (1, NFFN1)):
            if layer == 1:
                rmsnorm(nc, K, NMIX1, h, ahead=ahead(K.w, I["w_pw1"], pw1_loaded))
                R = Region(K.arena, work)
                cv = R.cut(C, N)
                conv(nc, K, I, h, cv, R, pw1_loaded)
                layernorm_silu(nc, K, cv, ahead(K.w, I["w_pw2"], pw2_loaded))
                linear_into_x(nc, K, I["w_pw2"], cv, pw2_loaded, bias=B_P2)
            rmsnorm(nc, K, gain, h, ahead=ahead(K.w9, I["w_q"][layer], wq_loaded[layer]))
            R = Region(K.arena, work)
            h_tok, acc = R.cut(NB + 1, D), R.cut(NB + 1, D)
            peer(nc, K, I, layer, h, h_tok, acc, R, wq_loaded[layer])
            add_token_major(nc, K, acc)
        rmsnorm(nc, K, NFIN, h, store=I["o_y"])


def constants():
    t, s = np.arange(P)[:, None], np.arange(P)[None, :]
    levels = []
    for l in range(LEVELS):
        m = ((t >> (l + 1)) == (s >> (l + 1))) & ((t >> l) % 2 == 1) & ((s >> l) % 2 == 0)
        levels += [m, m.T]
    tn, sn = np.arange(NS)[:, None], np.arange(NS)[None, :]
    same = (tn // ST) == (sn // ST)
    reset = np.ones(N)
    reset[0:T:P] = 0
    reset[T::ST] = 0
    parts = [np.eye(P), np.ones((P, P)), (t // HD) == (s // HD), t < s, t <= s,
             np.pad(same & (tn < sn), ((0, P - NS), (0, 0))), np.pad(same & (tn <= sn), ((0, P - NS), (0, 0))),
             (t % NS) // ST == np.arange(SB)[None, :],
             np.broadcast_to(np.arange(TOPK), (P, TOPK)), np.broadcast_to(reset, (P, N))]
    cst = np.concatenate([np.asarray(p, np.float32) for p in parts], axis=1)
    return cst, np.stack([np.asarray(m, np.float32) for m in levels], axis=1)


def kernel(**inputs):
    import concourse.bacc as bacc
    from concourse.bass_utils import run_bass_kernel_spmd

    a = {k: np.asarray(v) for k, v in inputs.items()}
    con = np.ascontiguousarray

    def chunks(w):
        return con(w.reshape(C, P, -1, P).transpose(2, 1, 0, 3))

    def feature_major(rows):
        return con(rows.reshape(-1, C, P).transpose(2, 1, 0))

    rows = [*a["rwkv_mu"][0], a["rwkv_w0"][0], a["rwkv_a0"][0], a["rwkv_k_k"][0], a["rwkv_k_a"][0],
            a["rwkv_r_k"][0].reshape(-1), a["rwkv_ln_w"][0], a["rwkv_ln_b"][0],
            a["conv_b_pw1"][0, :D], a["conv_b_pw1"][0, D:], a["conv_b_dw"][0], a["conv_ln_g"][0], a["conv_ln_b"][0],
            a["conv_b_pw2"][0], a["norm_mix"][0], a["norm_mix"][1], a["norm_ffn"][0], a["norm_ffn"][1],
            a["norm_final"], *a["conv_w_dw"][0]]
    par = np.stack(rows).reshape(NPAR, C, P)
    cst, level = constants()
    r, k, v = (chunks(a["rwkv_w_rkv"][0, j]) for j in range(3))
    low1 = np.concatenate([a["rwkv_w1"][0], a["rwkv_a1"][0], a["rwkv_g1"][0]], axis=1)
    low2 = np.concatenate([a["rwkv_w2"][0], a["rwkv_a2"][0], a["rwkv_g2"][0]], axis=0)
    pa, pg = chunks(a["conv_w_pw1"][0][:, :D]), chunks(a["conv_w_pw1"][0][:, D:])
    wq = []
    for j in range(2):
        keys = a["peer_sub_keys"][j].reshape(2 * HEADS, NKEYS, P).transpose(0, 2, 1)
        wq.append(np.concatenate([chunks(a["peer_w_q"][j]), keys[:, :, None, :]], axis=2))
    arrays = {
        "x": feature_major(np.concatenate([a["x_prompt"][0], a["x_sample"].reshape(NS, D)])),
        "par": con(par.transpose(2, 0, 1)),
        "cpar": con(par.transpose(1, 2, 0)),
        "cst": cst, "level": level,
        "shift": con(a["state_shift"][0].reshape(SB, C, P).transpose(2, 1, 0)),
        "low1": con(low1.reshape(C, P, 2 * P).transpose(1, 0, 2)),
        "low2": con(low2.reshape(2, P, C, P).transpose(2, 1, 0, 3)),
        "w_rkv": con(np.stack([r, k, v], axis=1).reshape(3 * C, P, C, P)),
        "w_o": chunks(a["rwkv_w_o"][0]),
        "w_pw1": con(np.stack([pa, pg], axis=1).reshape(2 * C, P, C, P)),
        "w_pw2": chunks(a["conv_w_pw2"][0]),
        "w_q": con(np.stack(wq)),
        "state": con(a["state_wkv"][0].reshape(SB, C, 2, HD, HD).transpose(1, 2, 4, 0, 3).reshape(C, P, SB, HD)),
        "state_conv": con(a["state_conv"][0].reshape(SB, PAST, C, P).transpose(2, 3, 0, 1)),
        "u0": a["peer_u"][0], "u1": a["peer_u"][1], "v0": a["peer_v"][0], "v1": a["peer_v"][1],
    }
    outs = {"o_y": (P, C, N), "o_shift": (P, C, 1 + SB), "o_wkv_p": (C, P, HD), "o_wkv_s": (C, P, SB, HD),
            "o_conv_p": (C, P, PAST), "o_conv_s": (C, P, SB, PAST)}
    nc = bacc.Bacc("TRN2", target_bir_lowering=False, num_devices=1)
    I = {k: nc.dram_tensor(f"in_{k}", v.shape, F32, kind="ExternalInput").ap() for k, v in arrays.items()}
    I |= {k: nc.dram_tensor(f"out_{k}", s, F32, kind="ExternalOutput").ap() for k, s in outs.items()}
    I["u"], I["v"] = (I["u0"], I["u1"]), (I["v0"], I["v1"])
    build(nc, I)
    got = run_bass_kernel_spmd(nc, [{f"in_{k}": con(v) for k, v in arrays.items()}], core_ids=[0]).results[0]
    y, shift, wp, ws, cp, cs = (np.asarray(got[f"out_{k}"]) for k in outs)
    tokens = y.transpose(2, 1, 0).reshape(N, D)
    rows_of = lambda s: s.transpose(2, 1, 0).reshape(-1, D)

    def states(w, b):
        return con(w.reshape(C, 2, HD, b, HD).transpose(3, 0, 1, 4, 2).reshape(1, b, 2 * C, HD, HD))

    return (con(tokens[:T])[None], con(tokens[T:]).reshape(SB, ST, D),
            states(wp, 1), con(rows_of(shift[:, :, 0:1]))[None],
            con(cp.transpose(2, 0, 1).reshape(1, 1, PAST, D)),
            states(ws, SB), con(rows_of(shift[:, :, 1:]))[None],
            con(cs.transpose(2, 3, 0, 1).reshape(1, SB, PAST, D)))
```
